# Optimizing a Trainium2 kernel written in Bass

```python
import math
import jax, jax.numpy as jnp
from jax import lax
import numpy as np

D_MODEL = 1024
BATCH = 1
SEQ = 512
DEPTH = 2

D_BRANCH = 512
M_HEADS = 4
M_HEAD_DIM = D_BRANCH // M_HEADS
M_CHUNK = 64
M_CONV = 4
R_BLOCKS = 8
R_BLOCK_DIM = D_BRANCH // R_BLOCKS
R_CONV = 4
R_C = 8.0
A_HEADS = 8
A_HEAD_DIM = D_BRANCH // A_HEADS
IDX_HEADS = 8
IDX_DIM = 64
TOPK_MAX = 256
Q_BLOCK = 128
ROPE_THETA = 10000.0
D_FF = 3 * D_MODEL
FFN_CONV = 3
EPS = 1e-6

IN_SPLITS = (
    2 * D_BRANCH,
    D_BRANCH,
    D_BRANCH,
    M_HEADS,
    M_HEADS,
    D_BRANCH,
    D_BRANCH,
    D_BRANCH,
    D_BRANCH,
    D_BRANCH,
    IDX_HEADS * IDX_DIM,
    IDX_DIM,
    IDX_HEADS,
    3 * D_MODEL,
)
N_IN = sum(IN_SPLITS)


def rms_norm(x, g):
    xf = x.astype(jnp.float32)
    y = xf * lax.rsqrt(jnp.mean(xf * xf, axis=-1, keepdims=True) + EPS)
    return (y * g.astype(jnp.float32)).astype(x.dtype)

def causal_dwconv(x, w, b):
    K, C = w.shape
    y = lax.conv_general_dilated(x, w[:, None, :].astype(x.dtype), window_strides=(1,),
                                 padding=[(K - 1, 0)], dimension_numbers=('NWC', 'WIO', 'NWC'),
                                 feature_group_count=C)
    return y + b.astype(x.dtype)

def rope_tables(positions, dim):
    inv = ROPE_THETA ** (-jnp.arange(0, dim, 2, dtype=jnp.float32) / dim)
    ang = positions.astype(jnp.float32)[..., None] * inv
    return jnp.cos(ang), jnp.sin(ang)

def apply_rope(x, cos, sin):
    x1, x2 = jnp.split(x.astype(jnp.float32), 2, axis=-1)
    c = cos[:, :, None, :]
    s = sin[:, :, None, :]
    return jnp.concatenate([x1 * c - x2 * s, x2 * c + x1 * s], axis=-1).astype(x.dtype)

def head_layer_norm(h, g):
    B, S, H, Dh = h.shape
    mu = jnp.mean(h, axis=-1, keepdims=True)
    var = jnp.mean(jnp.square(h - mu), axis=-1, keepdims=True)
    y = (h - mu) * lax.rsqrt(var + EPS)
    return y.reshape(B, S, H * Dh) * g.astype(jnp.float32)

def mlstm_chunkwise(q, k, v, i_pre, f_pre):
    B, S, H, Dh = q.shape
    L = M_CHUNK
    nc = S // L
    f32 = jnp.float32

    def to_chunks(t):
        return t.astype(f32).reshape(B, nc, L, H, Dh).transpose(1, 0, 3, 2, 4)

    def gate_chunks(t):
        return t.astype(f32).reshape(B, nc, L, H).transpose(1, 0, 3, 2)

    qc = to_chunks(q)
    kc = to_chunks(k) * (Dh ** -0.5)
    vc = to_chunks(v)
    ic = gate_chunks(i_pre)
    gc = jnp.cumsum(jax.nn.log_sigmoid(gate_chunks(f_pre)), axis=-1)
    causal = jnp.tril(jnp.ones((L, L), dtype=bool))

    def step(carry, inp):
        C, n, m = carry
        qb, kb, vb, ib, gb = inp
        logd = jnp.where(causal, gb[..., :, None] - gb[..., None, :] + ib[..., None, :], -jnp.inf)
        log_inter = gb + m[..., None]
        m_t = jnp.maximum(log_inter, jnp.max(logd, axis=-1))
        s = jnp.einsum('bhtd,bhsd->bhts', qb, kb) * jnp.exp(logd - m_t[..., None])
        w_inter = jnp.exp(log_inter - m_t)
        num = jnp.einsum('bhts,bhsd->bhtd', s, vb) + w_inter[..., None] * jnp.einsum('bhvk,bhtk->bhtv', C, qb)
        den = jnp.sum(s, axis=-1) + w_inter * jnp.einsum('bhk,bhtk->bht', n, qb)
        h = num / jnp.maximum(jnp.abs(den), jnp.exp(-m_t))[..., None]
        g_last = gb[..., -1]
        m_new = m_t[..., -1]
        w_state = jnp.exp(g_last[..., None] - gb + ib - m_new[..., None])
        decay = jnp.exp(g_last + m - m_new)
        C = decay[..., None, None] * C + jnp.einsum('bhs,bhsv,bhsk->bhvk', w_state, vb, kb)
        n = decay[..., None] * n + jnp.einsum('bhs,bhsk->bhk', w_state, kb)
        return (C, n, m_new), h

    init = (jnp.zeros((B, H, Dh, Dh), f32), jnp.zeros((B, H, Dh), f32), jnp.zeros((B, H), f32))
    _, hs = lax.scan(step, init, (qc, kc, vc, ic, gc))
    return hs.transpose(1, 0, 3, 2, 4).reshape(B, S, H, Dh)

def rg_lru(x, w_a, b_a, w_x, b_x, lam):
    B, S, C = x.shape
    xf = x.astype(jnp.float32)
    xb = xf.reshape(B, S, R_BLOCKS, R_BLOCK_DIM)
    r = jax.nn.sigmoid(jnp.einsum('bsnd,nde->bsne', xb, w_a.astype(jnp.float32)).reshape(B, S, C) + b_a.astype(jnp.float32))
    i = jax.nn.sigmoid(jnp.einsum('bsnd,nde->bsne', xb, w_x.astype(jnp.float32)).reshape(B, S, C) + b_x.astype(jnp.float32))
    log_a = -R_C * r * jax.nn.softplus(-lam.astype(jnp.float32))
    a = jnp.exp(log_a)
    u = jnp.sqrt(-jnp.expm1(2.0 * log_a)) * (i * xf)

    def combine(left, right):
        a1, b1 = left
        a2, b2 = right
        return a1 * a2, a2 * b1 + b2

    _, h = lax.associative_scan(combine, (a, u), axis=1)
    return h.astype(x.dtype)

def dsa_attention(q, k, v, q_idx, k_idx, w_idx):
    B, S, H, Dh = q.shape
    f32 = jnp.float32
    top_k = min(TOPK_MAX, S // 4)
    nb = S // Q_BLOCK
    key_pos = jnp.arange(S, dtype=jnp.int32)
    k_idx_f = k_idx.astype(f32)

    def blocks(t):
        return jnp.moveaxis(t.reshape((B, nb, Q_BLOCK) + t.shape[2:]), 1, 0)

    def attend(args):
        qb, qib, wb, start = args
        qpos = start + jnp.arange(Q_BLOCK, dtype=jnp.int32)
        visible = key_pos[None, None, :] <= qpos[None, :, None]
        logits = jnp.einsum('bqhd,bsd->bqhs', qib.astype(f32), k_idx_f) * (IDX_DIM ** -0.5)
        score = jnp.einsum('bqh,bqhs->bqs', wb.astype(f32) * (IDX_HEADS ** -0.5), jax.nn.relu(logits))
        score = jnp.where(visible, score, -jnp.inf)
        _, idx = lax.top_k(score, top_k)
        k_sel = jax.vmap(lambda kk, ii: kk[ii])(k, idx)
        v_sel = jax.vmap(lambda vv, ii: vv[ii])(v, idx)
        att = jnp.einsum('bqhd,bqkhd->bqhk', qb.astype(f32), k_sel.astype(f32)) * (Dh ** -0.5)
        keep = (idx <= qpos[None, :, None])[:, :, None, :]
        p = jax.nn.softmax(jnp.where(keep, att, -jnp.inf), axis=-1)
        return jnp.einsum('bqhk,bqkhd->bqhd', p, v_sel.astype(f32)).astype(q.dtype)

    starts = jnp.arange(nb, dtype=jnp.int32) * Q_BLOCK
    out = lax.map(attend, (blocks(q), blocks(q_idx), blocks(w_idx), starts))
    return jnp.moveaxis(out, 0, 1).reshape(B, S, H, Dh)

def first_inputs(seed: int = 0) -> dict:
    key = jax.random.key(seed)
    ks = jax.random.split(key, 24)
    f32 = jnp.float32

    def normal(k, shape, scale):
        return jax.random.normal(k, shape, f32) * scale

    def gain(k, shape):
        return 1.0 + 0.02 * jax.random.normal(k, shape, f32)

    x = normal(ks[0], (BATCH, SEQ, D_MODEL), 1.0)
    positions = (jnp.arange(SEQ, dtype=jnp.int32)[None, :]
                 + jax.random.randint(ks[1], (BATCH, 1), 0, 4096, dtype=jnp.int32))
    norm_mix = gain(ks[2], (DEPTH, D_MODEL))
    w_in = normal(ks[3], (DEPTH, D_MODEL, N_IN), D_MODEL ** -0.5)
    mlstm_conv_w = normal(ks[4], (DEPTH, M_CONV, 2 * D_BRANCH), M_CONV ** -0.5)
    mlstm_conv_b = normal(ks[5], (DEPTH, 2 * D_BRANCH), 0.02)
    mlstm_i_bias = normal(ks[6], (DEPTH, M_HEADS), 0.1)
    mlstm_f_bias = jnp.linspace(3.0, 6.0, M_HEADS, dtype=f32)[None, :] + normal(ks[7], (DEPTH, M_HEADS), 0.1)
    mlstm_norm = gain(ks[8], (DEPTH, D_BRANCH))
    rglru_conv_w = normal(ks[9], (DEPTH, R_CONV, D_BRANCH), R_CONV ** -0.5)
    rglru_conv_b = normal(ks[10], (DEPTH, D_BRANCH), 0.02)
    rglru_w_a = normal(ks[11], (DEPTH, R_BLOCKS, R_BLOCK_DIM, R_BLOCK_DIM), R_BLOCK_DIM ** -0.5)
    rglru_b_a = normal(ks[12], (DEPTH, D_BRANCH), 0.02)
    rglru_w_x = normal(ks[13], (DEPTH, R_BLOCKS, R_BLOCK_DIM, R_BLOCK_DIM), R_BLOCK_DIM ** -0.5)
    rglru_b_x = normal(ks[14], (DEPTH, D_BRANCH), 0.02)
    a_c = jax.random.uniform(ks[15], (DEPTH, D_BRANCH), f32, 0.9, 0.999)
    sig = a_c ** (1.0 / R_C)
    rglru_lambda = jnp.log(sig) - jnp.log1p(-sig)
    w_branch = normal(ks[16], (DEPTH, 3, D_BRANCH, D_MODEL), D_BRANCH ** -0.5)
    w_out = normal(ks[17], (DEPTH, D_MODEL, D_MODEL), D_MODEL ** -0.5)
    norm_ffn = gain(ks[18], (DEPTH, D_MODEL))
    ffn_up = normal(ks[19], (DEPTH, D_MODEL, 2 * D_FF), D_MODEL ** -0.5)
    ffn_conv_w = normal(ks[20], (DEPTH, FFN_CONV, D_FF), FFN_CONV ** -0.5)
    ffn_conv_b = normal(ks[21], (DEPTH, D_FF), 0.02)
    ffn_down = normal(ks[22], (DEPTH, D_FF, D_MODEL), D_FF ** -0.5)
    norm_final = gain(ks[23], (D_MODEL,))
    return {'x': x, 'positions': positions, 'norm_mix': norm_mix, 'w_in': w_in,
            'mlstm_conv_w': mlstm_conv_w, 'mlstm_conv_b': mlstm_conv_b,
            'mlstm_i_bias': mlstm_i_bias, 'mlstm_f_bias': mlstm_f_bias, 'mlstm_norm': mlstm_norm,
            'rglru_conv_w': rglru_conv_w, 'rglru_conv_b': rglru_conv_b,
            'rglru_w_a': rglru_w_a, 'rglru_b_a': rglru_b_a, 'rglru_w_x': rglru_w_x, 'rglru_b_x': rglru_b_x,
            'rglru_lambda': rglru_lambda, 'w_branch': w_branch, 'w_out': w_out, 'norm_ffn': norm_ffn,
            'ffn_up': ffn_up, 'ffn_conv_w': ffn_conv_w, 'ffn_conv_b': ffn_conv_b, 'ffn_down': ffn_down,
            'norm_final': norm_final}

def first_block(x, positions, norm_mix, w_in, mlstm_conv_w, mlstm_conv_b, mlstm_i_bias, mlstm_f_bias,
              mlstm_norm, rglru_conv_w, rglru_conv_b, rglru_w_a, rglru_b_a, rglru_w_x, rglru_b_x,
              rglru_lambda, w_branch, w_out, norm_ffn, ffn_up, ffn_conv_w, ffn_conv_b, ffn_down,
              norm_final):
    B, S, _ = x.shape
    cos, sin = rope_tables(positions, A_HEAD_DIM)
    split_at = np.cumsum(IN_SPLITS)[:-1].tolist()
    m_shape = (B, S, M_HEADS, M_HEAD_DIM)
    a_shape = (B, S, A_HEADS, A_HEAD_DIM)
    for l in range(DEPTH):
        h = rms_norm(x, norm_mix[l])
        (m_qk, m_v, m_o, m_i, m_f, r_x, r_g, a_q, a_k, a_v, a_qi, a_ki, a_w, gates) = jnp.split(
            h @ w_in[l], split_at, axis=-1)
        m_qk = jax.nn.silu(causal_dwconv(m_qk, mlstm_conv_w[l], mlstm_conv_b[l]))
        m_q, m_k = jnp.split(m_qk, 2, axis=-1)
        h_m = mlstm_chunkwise(m_q.reshape(m_shape), m_k.reshape(m_shape), m_v.reshape(m_shape),
                              m_i + mlstm_i_bias[l], m_f + mlstm_f_bias[l])
        y_a = (head_layer_norm(h_m, mlstm_norm[l]) * jax.nn.sigmoid(m_o.astype(jnp.float32))).astype(x.dtype)
        r_x = causal_dwconv(r_x, rglru_conv_w[l], rglru_conv_b[l])
        y_b = jax.nn.gelu(r_g) * rg_lru(r_x, rglru_w_a[l], rglru_b_a[l], rglru_w_x[l], rglru_b_x[l], rglru_lambda[l])
        q_c = apply_rope(a_q.reshape(a_shape), cos, sin)
        k_c = apply_rope(a_k.reshape(a_shape), cos, sin)
        qi = apply_rope(a_qi.reshape(B, S, IDX_HEADS, IDX_DIM), cos, sin)
        ki = apply_rope(a_ki[:, :, None, :], cos, sin)[:, :, 0, :]
        y_c = dsa_attention(q_c, k_c, a_v.reshape(a_shape), qi, ki, a_w).reshape(B, S, D_BRANCH)
        g_a, g_b, g_c = jnp.split(jax.nn.sigmoid(gates), 3, axis=-1)
        merged = (g_a * (y_a @ w_branch[l, 0]) + g_b * (y_b @ w_branch[l, 1])
                  + g_c * (y_c @ w_branch[l, 2]))
        x = x + merged @ w_out[l]
        h = rms_norm(x, norm_ffn[l])
        ff_g, ff_u = jnp.split(h @ ffn_up[l], 2, axis=-1)
        ff_g = causal_dwconv(ff_g, ffn_conv_w[l], ffn_conv_b[l])
        x = x + (jax.nn.gelu(ff_g) * ff_u) @ ffn_down[l]
    return rms_norm(x, norm_final)


GRID_W = 64
N_MIXERS = 2

N_MEM = 256
MEM_HEADS = 4
MEM_HEAD_DIM = 128
MEM_W = MEM_HEADS * MEM_HEAD_DIM

MLA_HEADS = 8
MLA_Q_RANK = 384
MLA_KV_RANK = 256
MLA_NOPE = 128
MLA_ROPE = 64
MLA_V = 128
MLA_IN_W = MLA_Q_RANK + MLA_KV_RANK + MLA_ROPE

GQA_HEADS = 8
GQA_KV_HEADS = 2
GQA_HEAD_DIM = 128
GQA_Q_W = GQA_HEADS * GQA_HEAD_DIM
GQA_KV_W = GQA_KV_HEADS * GQA_HEAD_DIM
GQA_IN_W = GQA_Q_W + 2 * GQA_KV_W

MIX_W = MLA_HEADS * MLA_V + MEM_W

D_FF_2 = -(-8 * D_MODEL // (3 * 256)) * 256


def _rmsnorm(x, g):
    x32 = x.astype(jnp.float32)
    y = x32 * lax.rsqrt(jnp.mean(x32 * x32, axis=-1, keepdims=True) + EPS)
    return (y * g.astype(jnp.float32)).astype(x.dtype)

def _axial_rope_tables(seq, dim, dtype):
    rows = seq // GRID_W
    row = jnp.repeat(jnp.arange(rows, dtype=jnp.float32), GRID_W)
    col = jnp.tile(jnp.arange(GRID_W, dtype=jnp.float32), rows)
    axis_dim = dim // 2
    inv = ROPE_THETA ** (-jnp.arange(0, axis_dim, 2, dtype=jnp.float32) / axis_dim)
    ang_r = row[:, None] * inv
    ang_c = col[:, None] * inv
    tabs = (jnp.cos(ang_r), jnp.sin(ang_r), jnp.cos(ang_c), jnp.sin(ang_c))
    return tuple(t[:, None, :].astype(dtype) for t in tabs)

def _rope_1d(x, cos, sin):
    x1, x2 = jnp.split(x, 2, axis=-1)
    return jnp.concatenate([x1 * cos - x2 * sin, x2 * cos + x1 * sin], axis=-1)

def _apply_axial_rope(x, tabs):
    cos_r, sin_r, cos_c, sin_c = tabs
    xr, xc = jnp.split(x, 2, axis=-1)
    return jnp.concatenate([_rope_1d(xr, cos_r, sin_r), _rope_1d(xc, cos_c, sin_c)], axis=-1)

def _blocked_attention(q_parts, k_parts, v, scale):
    B, S, Hk, Dv = v.shape
    H = q_parts[0].shape[2]
    G = H // Hk
    nb = S // Q_BLOCK
    qb = tuple(q.reshape(B, nb, Q_BLOCK, Hk, G, q.shape[-1]).transpose(1, 0, 2, 3, 4, 5)
               for q in q_parts)

    def one_block(qs):
        s = None
        for qp, kp in zip(qs, k_parts):
            eq = 'bqkgd,bskd->bkgqs' if kp.ndim == 4 else 'bqkgd,bsd->bkgqs'
            t = jnp.einsum(eq, qp, kp, preferred_element_type=jnp.float32)
            s = t if s is None else s + t
        p = jax.nn.softmax(s * scale, axis=-1).astype(v.dtype)
        return jnp.einsum('bkgqs,bskd->bqkgd', p, v)

    out = lax.map(one_block, qb)
    return out.transpose(1, 0, 2, 3, 4, 5).reshape(B, S, H, Dv)

def _mla_mixer(p, q_a_norm, w_q_b, kv_a_norm, w_kv_b, q_norm, k_norm, rope):
    B, S, _ = p.shape
    c_q = p[..., :MLA_Q_RANK]
    c_kv = p[..., MLA_Q_RANK:MLA_Q_RANK + MLA_KV_RANK]
    k_pe = p[..., MLA_Q_RANK + MLA_KV_RANK:]
    q = (_rmsnorm(c_q, q_a_norm) @ w_q_b).reshape(B, S, MLA_HEADS, MLA_NOPE + MLA_ROPE)
    kv = (_rmsnorm(c_kv, kv_a_norm) @ w_kv_b).reshape(B, S, MLA_HEADS, MLA_NOPE + MLA_V)
    q_nope = _rmsnorm(q[..., :MLA_NOPE], q_norm[:MLA_NOPE])
    q_pe = _apply_axial_rope(_rmsnorm(q[..., MLA_NOPE:], q_norm[MLA_NOPE:]), rope)
    k_nope = _rmsnorm(kv[..., :MLA_NOPE], k_norm[:MLA_NOPE])
    v = kv[..., MLA_NOPE:]
    k_pe = _apply_axial_rope(_rmsnorm(k_pe, k_norm[MLA_NOPE:])[:, :, None, :], rope)[:, :, 0, :]
    out = _blocked_attention([q_nope, q_pe], [k_nope, k_pe], v,
                             (MLA_NOPE + MLA_ROPE) ** -0.5)
    return out.reshape(B, S, MLA_HEADS * MLA_V)

def _gqa_mixer(p, q_norm, k_norm, rope):
    B, S, _ = p.shape
    q = p[..., :GQA_Q_W].reshape(B, S, GQA_HEADS, GQA_HEAD_DIM)
    k = p[..., GQA_Q_W:GQA_Q_W + GQA_KV_W].reshape(B, S, GQA_KV_HEADS, GQA_HEAD_DIM)
    v = p[..., GQA_Q_W + GQA_KV_W:].reshape(B, S, GQA_KV_HEADS, GQA_HEAD_DIM)
    q = _apply_axial_rope(_rmsnorm(q, q_norm), rope)
    k = _apply_axial_rope(_rmsnorm(k, k_norm), rope)
    out = _blocked_attention([q], [k], v, GQA_HEAD_DIM ** -0.5)
    return out.reshape(B, S, GQA_Q_W)

def _memory_attention(q, mem_n, w_kv, q_norm, k_norm):
    B, S, _ = q.shape
    M = mem_n.shape[1]
    q = _rmsnorm(q.reshape(B, S, MEM_HEADS, MEM_HEAD_DIM), q_norm)
    kv = (mem_n @ w_kv).reshape(B, M, 2, MEM_HEADS, MEM_HEAD_DIM)
    k = _rmsnorm(kv[:, :, 0], k_norm)
    v = kv[:, :, 1]
    s = jnp.einsum('bqhd,bmhd->bhqm', q, k, preferred_element_type=jnp.float32)
    p = jax.nn.softmax(s * (MEM_HEAD_DIM ** -0.5), axis=-1).astype(v.dtype)
    return jnp.einsum('bhqm,bmhd->bqhd', p, v).reshape(B, S, MEM_W)

def _swiglu(h, w_gate_up, w_down):
    gu = h @ w_gate_up
    g, u = gu[..., :D_FF_2], gu[..., D_FF_2:]
    return (jax.nn.silu(g) * u) @ w_down

def second_inputs(seed: int = 0) -> dict:
    key = jax.random.key(seed)
    ks = iter(jax.random.split(key, 32))
    n_mla = (DEPTH + 1) // 2
    n_gqa = DEPTH // 2

    def w(shape, fan_in):
        return jax.random.normal(next(ks), shape, jnp.float32) * (fan_in ** -0.5)

    def gain(shape):
        return 1.0 + 0.05 * jax.random.normal(next(ks), shape, jnp.float32)

    return {
        "x": jax.random.normal(next(ks), (BATCH, SEQ, D_MODEL), jnp.float32),
        "mem": jax.random.normal(next(ks), (BATCH, N_MEM, D_MODEL), jnp.float32),
        "mem_norm": gain((D_MODEL,)),
        "norm_mix": gain((DEPTH, D_MODEL)),
        "norm_ffn": gain((DEPTH, D_MODEL)),
        "w_out": w((DEPTH, MIX_W, D_MODEL), MIX_W),
        "w_mem_kv": w((DEPTH, D_MODEL, 2 * MEM_W), D_MODEL),
        "memq_norm": gain((DEPTH, MEM_HEAD_DIM)),
        "memk_norm": gain((DEPTH, MEM_HEAD_DIM)),
        "w_gate_up": w((DEPTH, D_MODEL, 2 * D_FF_2), D_MODEL),
        "w_down": w((DEPTH, D_FF_2, D_MODEL), D_FF_2),
        "mla_w_in": w((n_mla, D_MODEL, MLA_IN_W + MEM_W), D_MODEL),
        "mla_q_a_norm": gain((n_mla, MLA_Q_RANK)),
        "mla_w_q_b": w((n_mla, MLA_Q_RANK, MLA_HEADS * (MLA_NOPE + MLA_ROPE)), MLA_Q_RANK),
        "mla_kv_a_norm": gain((n_mla, MLA_KV_RANK)),
        "mla_w_kv_b": w((n_mla, MLA_KV_RANK, MLA_HEADS * (MLA_NOPE + MLA_V)), MLA_KV_RANK),
        "mla_q_norm": gain((n_mla, MLA_NOPE + MLA_ROPE)),
        "mla_k_norm": gain((n_mla, MLA_NOPE + MLA_ROPE)),
        "gqa_w_in": w((n_gqa, D_MODEL, GQA_IN_W + MEM_W), D_MODEL),
        "gqa_q_norm": gain((n_gqa, GQA_HEAD_DIM)),
        "gqa_k_norm": gain((n_gqa, GQA_HEAD_DIM)),
    }

def second_block(x, mem, mem_norm, norm_mix, norm_ffn, w_out, w_mem_kv, memq_norm, memk_norm,
              w_gate_up, w_down, mla_w_in, mla_q_a_norm, mla_w_q_b, mla_kv_a_norm, mla_w_kv_b,
              mla_q_norm, mla_k_norm, gqa_w_in, gqa_q_norm, gqa_k_norm):
    S = x.shape[1]
    rope_mla = _axial_rope_tables(S, MLA_ROPE, x.dtype)
    rope_gqa = _axial_rope_tables(S, GQA_HEAD_DIM, x.dtype)
    mem_n = _rmsnorm(mem, mem_norm)
    for i in range(DEPTH):
        j = i // N_MIXERS
        h = _rmsnorm(x, norm_mix[i])
        if i % N_MIXERS == 0:
            proj = h @ mla_w_in[j]
            mix = _mla_mixer(proj[..., :MLA_IN_W], mla_q_a_norm[j], mla_w_q_b[j],
                             mla_kv_a_norm[j], mla_w_kv_b[j], mla_q_norm[j], mla_k_norm[j],
                             rope_mla)
            q_mem = proj[..., MLA_IN_W:]
        else:
            proj = h @ gqa_w_in[j]
            mix = _gqa_mixer(proj[..., :GQA_IN_W], gqa_q_norm[j], gqa_k_norm[j], rope_gqa)
            q_mem = proj[..., GQA_IN_W:]
        mem_out = _memory_attention(q_mem, mem_n, w_mem_kv[i], memq_norm[i], memk_norm[i])
        x = x + jnp.concatenate([mix, mem_out], axis=-1) @ w_out[i]
        x = x + _swiglu(_rmsnorm(x, norm_ffn[i]), w_gate_up[i], w_down[i])
    return x


def setup_inputs(seed=0):
    out = dict(first_inputs(seed))
    for name, value in second_inputs(seed + 1).items():
        if name != "x":
            out[name + "_2"] = value
    return out


def reference(
    x, positions, norm_mix, w_in, mlstm_conv_w, mlstm_conv_b, mlstm_i_bias, mlstm_f_bias,
    mlstm_norm, rglru_conv_w, rglru_conv_b, rglru_w_a, rglru_b_a, rglru_w_x, rglru_b_x,
    rglru_lambda, w_branch, w_out, norm_ffn, ffn_up, ffn_conv_w, ffn_conv_b, ffn_down,
    norm_final, mem_2, mem_norm_2, norm_mix_2, norm_ffn_2, w_out_2, w_mem_kv_2, memq_norm_2,
    memk_norm_2, w_gate_up_2, w_down_2, mla_w_in_2, mla_q_a_norm_2, mla_w_q_b_2,
    mla_kv_a_norm_2, mla_w_kv_b_2, mla_q_norm_2, mla_k_norm_2, gqa_w_in_2, gqa_q_norm_2,
    gqa_k_norm_2,
):
    x = first_block(
        x, positions, norm_mix, w_in, mlstm_conv_w, mlstm_conv_b, mlstm_i_bias, mlstm_f_bias,
        mlstm_norm, rglru_conv_w, rglru_conv_b, rglru_w_a, rglru_b_a, rglru_w_x, rglru_b_x,
        rglru_lambda, w_branch, w_out, norm_ffn, ffn_up, ffn_conv_w, ffn_conv_b, ffn_down,
        norm_final,
    )
    return second_block(
        x, mem_2, mem_norm_2, norm_mix_2, norm_ffn_2, w_out_2, w_mem_kv_2, memq_norm_2,
        memk_norm_2, w_gate_up_2, w_down_2, mla_w_in_2, mla_q_a_norm_2, mla_w_q_b_2,
        mla_kv_a_norm_2, mla_w_kv_b_2, mla_q_norm_2, mla_k_norm_2, gqa_w_in_2, gqa_q_norm_2,
        gqa_k_norm_2,
    )


_drawn_inputs = setup_inputs


def setup_inputs(seed=0):
    import zlib

    import numpy as np

    out = dict(_drawn_inputs(seed))
    spreads = {}
    factors = {'mlstm_conv_b': 4.665,
     'mlstm_i_bias': 64.0,
     'mlstm_norm': 4.411,
     'rglru_b_a': 8.0,
     'rglru_b_x': 8.0,
     'ffn_conv_b': 2.776,
     'mem_norm_2': 8.0,
     'norm_mix_2': 3.993,
     'memq_norm_2': 8.0,
     'memk_norm_2': 8.0,
     'mla_q_a_norm_2': 8.0,
     'mla_kv_a_norm_2': 5.811,
     'mla_q_norm_2': 8.0,
     'mla_k_norm_2': 8.0,
     'gqa_q_norm_2': 8.0,
     'gqa_k_norm_2': 8.0}
    for name, (base, spread) in spreads.items():
        noise = np.random.default_rng([zlib.crc32(name.encode()), seed]).standard_normal(out[name].shape)
        drawn = base * np.exp(spread * noise) if base else spread * noise
        out[name] = __import__('jax').numpy.asarray(drawn.astype(out[name].dtype))
    for name, factor in factors.items():
        out[name] = (out[name] * factor).astype(out[name].dtype)
    return out
```

```python
from contextlib import ExitStack

import numpy as np

import concourse.bass as bass
from concourse import mybir

F32 = mybir.dt.float32
F32R = mybir.dt.float32r
I32 = mybir.dt.int32
ALU = mybir.AluOpType
ACT = mybir.ActivationFunctionType
AX = mybir.AxisListType.X

P = 128
S = 512
D = 1024
ND = D // P
DEPTH = 2
EPS = 1e-6
BR = 512
NBR = BR // P
M_HEADS = 4
A_HEADS = 8
HD = 64
FF = 3 * D
NFF = FF // P
TOPK = 128
NQ = S // P
NEG = -1e30
UNSEEN = -3.0e38
TAKEN = -3.4e38
SLOT = 16
RAW, HALF = 3, 2
PAGE = 2048
M_SCALE = float(P) ** -0.5
A_SCALE = float(HD) ** -0.5
SPLITS = (2 * BR, BR, BR, M_HEADS, M_HEADS, BR, BR, BR, BR, BR, BR, HD, A_HEADS, 3 * D)
(O_QK, O_V, O_O, O_I, O_F, O_RX, O_RG, O_AQ, O_AK, O_AV, O_QI, O_KI, O_W, O_G) = (
    int(v) for v in np.cumsum((0,) + SPLITS)[:-1])

MEM = 256
NMEM = MEM // P
MEM_HEADS = 4
H2 = 8
QR, KVR, ROPE = 384, 256, 64
NQR, NKV = QR // P, KVR // P
MLA_IN = QR + KVR + ROPE
GKV = 2
FF2 = 2816
NFF2 = FF2 // P
MIX = 12
MLA_SCALE = float(P + ROPE) ** -0.5
HD_SCALE = float(P) ** -0.5


HEADS2 = MEM_HEADS + H2
N_FINAL = 2 * DEPTH
N_SECOND = N_FINAL + 1


def prep_tiles(l, u):
    if u < MEM_HEADS:
        return []
    if l == 1:
        return [("q", ND)]
    return [("q", NQR), ("k", NKV)] + ([("pe", NQR)] if u % 2 == 0 else [])


def n_jobs(l, u):
    return max(1, len(prep_tiles(l, u))) if u < HEADS2 else 0


def schedule():
    tiles, blocks, nt, nb = {}, {}, 0, 0

    def stage(name, t, b=0):
        nonlocal nt, nb
        tiles[name], blocks[name] = nt, nb
        nt += t
        nb += b

    for l in range(DEPTH):
        stage(("norm", 2 * l), 1)
        stage(("qi", l), 4, 32)
        stage(("ki", l), 1, 8)
        stage(("if", l), 1, 8)
        stage(("w", l), 1)
        stage(("idx", l), 3 * A_HEADS)
        stage(("mqk", l), 8, 64)
        stage(("mv", l), 4, 32)
        stage(("acol", l), 1)
        stage(("m1", l, 0), 6)
        for h in range(M_HEADS):
            stage(("rx", l, h), 1, 8)
            stage(("mo", l, h), 1, 8)
            stage(("m2", l, h), 2)
            stage(("ak", l, h), 1, 8)
            stage(("m3", l, h), 1)
            if h + 1 < M_HEADS:
                stage(("m1", l, h + 1), 6)
            stage(("m4", l, h), 1)
        for c in range(NBR):
            stage(("rg", l, c), 1, 8)
            stage(("rgl", l, c), 2)
            stage(("aq", l, c), 1, 8)
        stage(("av", l), 4, 32)
        for m in range(ND):
            stage(("br", l, 0, m), 2, 12)
        stage(("s", l, 0), 4)
        for h in range(A_HEADS):
            stage(("br", l, 1, h), 2, 12)
            stage(("o", l, h), 9)
        stage(("gc", l), 8, 64)
        stage(("bc", l), 8, 32)
        stage(("wo", l), 8, 64)
        stage(("norm", 2 * l + 1), 1)
        for half in range(2):
            for p in range(NFF // 2):
                stage(("up", l, half, p), 2, 16)
            stage(("down", l, half), 8, 8 * NFF // 2)
    stage(("norm", N_FINAL), 1)
    for l in range(DEPTH):
        stage(("memnorm", l), 1)
        stage(("memk", l), 4, 32)
        stage(("memv", l), 2, 32)
        stage(("memkst", l), 2)
        stage(("norm", N_SECOND + 2 * l), 1)
        if l == 0:
            stage(("cq", l), NQR, NQR * ND)
            stage(("ckv", l), NKV, NKV * ND)
            stage(("kpe", l), 1, ND)
            stage(("qmem", l), 4, 4 * ND)
            stage(("cqst", l), 1)
            stage(("ckvst", l), 1)
            stage(("kst", l), 1)
            stage(("v2", l), 8, 16)
        else:
            stage(("kg", l), GKV, GKV * ND)
            stage(("vg", l), NQ, 2 * ND)
            stage(("qmem", l), 4, 4 * ND)
            stage(("kst", l), GKV)
        for v in range(2):
            stage(("pb", l, v), 1)
        stage(("s2", l), 4)
        for u in range(HEADS2):
            if u + 2 < HEADS2:
                stage(("pa", l, u + 2), len(prep_tiles(l, u + 2)), sum(n for _, n in prep_tiles(l, u + 2)))
            stage(("o2", l, u), 9 + n_jobs(l, u + 2))
            tiles["pb", l, u + 2] = tiles["o2", l, u] + 5
        stage(("wo2", l), 8, 8 * MIX)
        stage(("norm", N_SECOND + 2 * l + 1), 1)
        for half in range(2):
            for p in range(NFF2 // 2):
                stage(("up2", l, half, p), 2, 16)
            stage(("down2", l, half), 8, 8 * NFF2 // 2)
    return tiles, blocks, nt, nb


TILE, BLOCK, N_TILES, N_BLOCKS = schedule()


def score_tile(l, h, j):
    return TILE["s", l, 0] + j if h == 0 else TILE["o", l, h - 1] + (2 * j + 2 if j else 1)


def turn_tile(l, h, j):
    return TILE["o", l, h] + (2 * j + 1 if j else 0)


def out_tile(l, h):
    return TILE["o", l, h] + 2


def turn_tile2(l, u, j):
    return TILE["o2", l, u] + 2 * j + (1 + n_jobs(l, u + 2) if j >= 2 else 0)


def score_tile2(l, u, j):
    return TILE["s2", l] + j if u == 0 else turn_tile2(l, u - 1, j) + 1


def out_tile2(l, u):
    return TILE["o2", l, u] + 4


UNUSED = ({score_tile(l, A_HEADS, j) for l in range(DEPTH) for j in range(NQ)}
          | {score_tile2(l, HEADS2, j) for l in range(DEPTH) for j in range(NQ)})


N_SLOTS = -(-N_BLOCKS // SLOT)


def param_columns():
    at, n = {}, 0
    for name, c in (("norm_mix", ND), ("mlstm_conv_w", 4 * 8), ("mlstm_conv_b", 8), ("mlstm_norm", 4),
                    ("rglru_conv_w", 16), ("rglru_conv_b", 4), ("rglru_b_a", 4), ("rglru_b_x", 4),
                    ("rglru_lambda", 4), ("norm_ffn", ND), ("ffn_conv_w", 3 * NFF), ("ffn_conv_b", NFF),
                    ("i_bias", 1), ("f_bias", 1)):
        at[name] = n
        n += c
    return at, n


PCOL, PLAYER = param_columns()
P_FINAL = DEPTH * PLAYER


def second_columns():
    at, n = {}, P_FINAL + ND
    for name, c in (("mem_norm", ND), ("norm_mix", DEPTH * ND), ("norm_ffn", DEPTH * ND), ("memq", DEPTH),
                    ("memk", DEPTH), ("q_a", NQR), ("kv_a", NKV), ("mla_q", 1), ("mla_qpe", 1),
                    ("mla_k", 1), ("mla_kpe", 1), ("gqa_q", 1), ("gqa_k", 1)):
        at[name] = n
        n += c
    return at, n


PCOL2, P_TOTAL = second_columns()
PE_ORDER = np.r_[0:16, 32:48, 16:32, 48:64]


def pack_weights(w):
    out = np.zeros((N_SLOTS * SLOT, P, P), np.float32)
    place = [0]

    def put(a):
        out[place[0], :, :a.shape[1]] = a
        place[0] += 1

    def by_tile(a, cols=None):
        k, n = a.shape
        for m in range(n // P):
            for c in range(k // P):
                put(a[c * P:(c + 1) * P, m * P:(m + 1) * P])

    def by_k(a):
        k, n = a.shape
        for c in range(k // P):
            for m in range(n // P):
                put(a[c * P:(c + 1) * P, m * P:(m + 1) * P])

    for l in range(DEPTH):
        wi, wb, wo = w["w_in"][l], w["w_branch"][l], w["w_out"][l]
        up, down = w["ffn_up"][l], w["ffn_down"][l]
        by_tile(wi[:, O_QI:O_QI + BR])
        ki = wi[:, O_KI:O_KI + HD]
        by_tile(np.concatenate([ki, ki], axis=1))
        small = np.zeros((D, P), np.float32)
        small[:, 0:4] = wi[:, O_I:O_I + 4]
        small[:, 32:36] = wi[:, O_F:O_F + 4]
        small[:, 64:72] = wi[:, O_W:O_W + 8]
        by_tile(small)
        by_tile(wi[:, O_QK:O_QK + 2 * BR])
        by_k(wi[:, O_V:O_V + BR])
        for h in range(M_HEADS):
            for o in (O_RX, O_O, O_AK):
                by_tile(wi[:, o + h * P:o + (h + 1) * P])
        for c in range(NBR):
            for o in (O_RG, O_AQ):
                by_tile(wi[:, o + c * P:o + (c + 1) * P])
        by_k(wi[:, O_AV:O_AV + BR])
        for b in range(2):
            for m in range(ND):
                by_tile(wi[:, O_G + b * D + m * P:O_G + b * D + (m + 1) * P])
                by_tile(wb[b][:, m * P:(m + 1) * P])
        by_tile(wi[:, O_G + 2 * D:O_G + 3 * D])
        by_tile(wb[2])
        by_tile(wo)
        for half in range(2):
            for p in range(half * NFF // 2, (half + 1) * NFF // 2):
                by_tile(up[:, p * P:(p + 1) * P])
                by_tile(up[:, FF + p * P:FF + (p + 1) * P])
            by_tile(down[half * FF // 2:(half + 1) * FF // 2])
    for l in range(DEPTH):
        mkv = w["w_mem_kv_2"][l]
        by_tile(mkv[:, :BR])
        by_k(mkv[:, BR:])
        if l == 0:
            wi, qb = w["mla_w_in_2"][0], w["mla_w_q_b_2"][0].reshape(QR, H2, P + ROPE)
            kvb = w["mla_w_kv_b_2"][0].reshape(KVR, H2, 2 * P)
            by_tile(wi[:, :QR + KVR])
            kpe = wi[:, QR + KVR:MLA_IN][:, PE_ORDER]
            by_tile(np.concatenate([kpe, kpe], axis=1))
            by_tile(wi[:, MLA_IN:])
            for g in range(2):
                by_k(kvb[:, 4 * g:4 * g + 4, P:].reshape(KVR, 4 * P))
        else:
            wi = w["gqa_w_in_2"][0]
            q, kv = H2 * P, GKV * P
            by_tile(wi[:, q:q + kv])
            by_k(wi[:, q + kv:q + 2 * kv])
            by_tile(wi[:, q + 2 * kv:])
        for u in range(MEM_HEADS, HEADS2):
            h = u - MEM_HEADS
            for kind, _ in prep_tiles(l, u):
                if l == 1:
                    by_tile(wi[:, h * P:(h + 1) * P])
                elif kind == "q":
                    by_tile(qb[:, h, :P])
                elif kind == "k":
                    by_tile(kvb[:, h, :P])
                else:
                    by_tile(qb[:, h:h + 2, P:][:, :, PE_ORDER].reshape(QR, 2 * ROPE))
        by_tile(w["w_out_2"][l])
        gu, down = w["w_gate_up_2"][l], w["w_down_2"][l]
        for half in range(2):
            for p in range(half * NFF2 // 2, (half + 1) * NFF2 // 2):
                by_tile(gu[:, p * P:(p + 1) * P])
                by_tile(gu[:, FF2 + p * P:FF2 + (p + 1) * P])
            by_tile(down[half * FF2 // 2:(half + 1) * FF2 // 2])
    assert place[0] == N_BLOCKS
    return out.reshape(N_SLOTS, SLOT, P, P).transpose(0, 2, 1, 3).reshape(N_SLOTS, P, SLOT * P).copy()


def pack_params(w):
    out = np.zeros((P, P_TOTAL), np.float32)

    def col(v):
        return np.asarray(v, np.float32).reshape(-1, P).T

    for l in range(DEPTH):
        o = l * PLAYER
        for name in ("norm_mix", "mlstm_conv_w", "mlstm_conv_b", "mlstm_norm", "rglru_conv_w",
                     "rglru_conv_b", "rglru_b_a", "rglru_b_x", "rglru_lambda", "norm_ffn",
                     "ffn_conv_w", "ffn_conv_b"):
            c = col(w[name][l])
            out[:, o + PCOL[name]:o + PCOL[name] + c.shape[1]] = c
        out[0:4, o + PCOL["i_bias"]] = w["mlstm_i_bias"][l]
        out[0:4, o + PCOL["f_bias"]] = w["mlstm_f_bias"][l]
    out[:, P_FINAL:P_FINAL + ND] = col(w["norm_final"])
    q, k = w["mla_q_norm_2"][0], w["mla_k_norm_2"][0]
    for name, v in (("mem_norm", w["mem_norm_2"]), ("norm_mix", w["norm_mix_2"]), ("norm_ffn", w["norm_ffn_2"]),
                    ("memq", w["memq_norm_2"]), ("memk", w["memk_norm_2"]), ("q_a", w["mla_q_a_norm_2"][0]),
                    ("kv_a", w["mla_kv_a_norm_2"][0]), ("mla_q", q[:P]), ("mla_k", k[:P]),
                    ("mla_qpe", np.concatenate([q[P:][PE_ORDER]] * 2)),
                    ("mla_kpe", np.concatenate([k[P:][PE_ORDER]] * 2)),
                    ("gqa_q", w["gqa_q_norm_2"][0]), ("gqa_k", w["gqa_k_norm_2"][0])):
        c = col(v)
        out[:, PCOL2[name]:PCOL2[name] + c.shape[1]] = c
    return out


def pack_rglru(w):
    out = np.zeros((P, DEPTH, 8, P), np.float32)
    for l in range(DEPTH):
        for g, name in enumerate(("rglru_w_a", "rglru_w_x")):
            for c in range(NBR):
                for e in range(2):
                    r = slice(64 * e, 64 * e + 64)
                    out[r, l, 4 * g + c, r] = w[name][l, 2 * c + e]
    return out


C_ID, C_ONE, C_ST, C_QK, C_ONE64 = (i * P for i in range(5))
C_INV, C_SGN = 5 * P, 5 * P + 1
C_TOTAL = 5 * P + 2


def constants():
    i = np.arange(P)
    out = np.zeros((P, C_TOTAL), np.float32)
    out[:, C_ID:C_ID + P] = np.eye(P)
    out[:, C_ONE:C_ONE + P] = 1.0
    out[:, C_ST:C_ST + P] = np.where(i[:, None] <= i[None, :], 0.0, NEG)
    out[:, C_QK:C_QK + P] = np.where(i[:, None] >= i[None, :], 0.0, NEG)
    inv = np.float32(10000.0) ** (-np.arange(0, HD, 2, dtype=np.float32) / np.float32(HD))
    out[:, C_INV] = inv[i % 32]
    out[:, C_SGN] = np.where(i % 64 < 32, -1.0, 1.0)
    out[:, C_ONE64:C_ONE64 + P] = i[:, None] // 64 == i[None, :] // 64
    return out


def axial_tables():
    t = np.arange(S)
    row, col = (t // 64).astype(np.float32), (t % 64).astype(np.float32)
    out = np.zeros((2, 2, P, S), np.float32)
    for g in range(2):
        for p in range(P):
            if g == 0:
                f, axis, first, width = p % 16, (p % 32) // 16, p % 64 < 32, 32
            else:
                f, axis, first, width = p % 32, p // 64, p % 64 < 32, 64
            inv = np.float32(10000.0) ** (-np.arange(0, width, 2, dtype=np.float32) / np.float32(width))
            a = (col if axis else row) * inv[f]
            out[g, 0, p] = np.cos(a)
            out[g, 1, p] = -np.sin(a) if first else np.sin(a)
    return out


class Engine:

    def __init__(self, name, sems, marks, known):
        self.name, self.sems, self.marks, self.known = name, sems, marks, known
        self.count, self.previous = {}, None

    def signals(self, *names):
        own = [n[0] for n in names if n[0] not in ("read", "full", "slot")] + [n[0] for n in names]
        kind = own[0] if own and own[0] != "read" else self.name + ("_read" if own else "_step")
        n = self.count[kind] = self.count.get(kind, 0) + 1
        for name in names:
            assert name not in self.marks, name
            self.marks[name] = (kind, n)
        self.previous = self.sems[kind], n
        return self.sems[kind], 1

    def after(self, *name):
        kind, n = self.known[name] if self.known else ("x_in0", 1)
        return self.sems[kind], n


def build(nc, args, known, probe=None):
    A = dict(args)
    marks = {}
    with ExitStack() as ctx:
        base = nc.sbuf_base + (-nc.sbuf_base) % 32

        def at(name, off, shape, dt=F32):
            return nc.alloc_sbuf_tensor_at(name, shape, dt, offset=off)

        off = base

        def fixed(name, shape, dt=F32):
            nonlocal off
            t = at(name, off, shape, dt)
            off += int(np.prod(shape[1:])) * 4
            off += (-off) % 32
            return t

        x = fixed("x", [P, ND, S])
        hh = fixed("hh", [P, ND, S], F32R)
        hl = fixed("hl", [P, ND, S], F32R)
        raw = fixed("raw", [P, RAW, SLOT * P])
        whi = fixed("whi", [P, HALF, SLOT * P], F32R)
        wlo = fixed("wlo", [P, HALF, SLOT * P], F32R)
        tabc = fixed("tabc", [P, S])
        tabs = fixed("tabs", [P, S])
        cin = fixed("cin", [P, 2, S + 3])
        cacc = fixed("cacc", [P, 2, S])
        con = fixed("con", [P, C_TOTAL])
        par = fixed("par", [P, P_TOTAL])
        sp8 = fixed("sp8", [P, DEPTH * 4])
        spt = fixed("spt", [P, 6, DEPTH * 4])
        rgw_off = off
        rgw = fixed("rgw", [P, DEPTH, 8, P])
        acol = fixed("acol", [P, NQ, M_HEADS])
        wcol = fixed("wcol", [P, NQ, A_HEADS])
        top = fixed("top", [P, 3, 8])
        nmx = fixed("nmx", [P, 8])
        rsum = fixed("rsum", [P, 8])
        rinv = fixed("rinv", [P, 8])
        bcol = fixed("bcol", [P, 4])
        region = off + (-off) % 32
        n_pages = (nc.sbuf_usable_end - region) // PAGE
        assert n_pages >= 46, n_pages

        def pages(name, p, shape, dt=F32):
            assert p * PAGE + int(np.prod(shape[1:])) * 4 <= n_pages * PAGE
            return at(name, region + p * PAGE, shape, dt)

        ah = pages("ah", 0, [P, 12, S], F32R)
        al = pages("al", 12, [P, 12, S], F32R)
        qi = pages("qi", 4, [P, 4, S])
        ki = pages("ki", 8, [P, S])
        work = pages("work", 9, [P, 3, S])
        relu = pages("relu", 16, [P, 2, S])
        rsw = pages("rsw", 18, [P, 2, S])
        rt1 = pages("rt1", 20, [P, 2, S])
        mq = pages("mq", 24, [P, 4, S])
        mk = pages("mk", 28, [P, 4, S])
        mv = pages("mv", 32, [P, NQ, BR])
        mo = pages("mo", 45, [P, S])
        aswap = pages("aswap", 43, [P, S])
        atmp = pages("atmp", 44, [P, S])
        rows = [pages(f"row{i}", p, [4, S]) for i, p in enumerate((0, 1, 2, 3, 12, 13))]
        wrow = pages("wrow", 14, [8, S])
        negm = pages("negm", 40, [4, S])
        negg = pages("negg", 41, [4, S])
        xc = pages("xc", 4, [P, 4, S])
        mp = pages("mp", 16, [P, 4, S])
        mnm = pages("mnm", 20, [P, S])
        mdm = pages("mdm", 21, [P, NQ, P])
        mwx = pages("mwx", 22, [P, 2, S])
        mex = pages("mex", 8, [P, S])
        mdn = pages("mdn", 42, [P, S])
        yf = pages("yf", 28, [P, 4, S])
        rg = pages("rg", 24, [P, 4, S])
        rt = pages("rt", 16, [P, 6, S])
        rsw2 = pages("rsw2", 22, [P, 2, S])
        aq = pages("aq", 32, [P, 4, S])
        ak = pages("ak", 36, [P, 4, S])
        av = [pages(f"av{i}", p, [P, BR]) for i, p in enumerate((40, 41, 42, 8))]
        mer = pages("mer", 16, [P, ND, S])
        sm = pages("sm", 4, [P, 4, S])
        pt = pages("pt", 24, [P, 3, S])
        sig = pages("sig", 27, [P, S])
        sigc = pages("sigc", 32, [P, ND, S])
        nsq = pages("nsq", 28, [P, 2, S])
        nrm = pages("nrm", 30, [P, S])
        nri = pages("nri", 31, [P, S])
        nhf = pages("nhf", 32, [P, 2, S])
        fga = pages("fga", 24, [P, 2, S])
        fhf = pages("fhf", 26, [P, 2, S])
        pos_i = pages("pos_i", 0, [P, S], I32)
        rtab = pages("rtab", 1, [P, 6, S])

        memf = pages("memf", 8, [P, ND, MEM])
        memh = pages("memh", 0, [P, ND, MEM], F32R)
        meml = pages("meml", 4, [P, ND, MEM], F32R)
        mri = pages("mri", 12, [P, MEM])
        msq = pages("msq", 13, [P, 2, MEM])
        kraw = pages("kraw", 14, [P, 2, S])
        ksq = pages("ksq", 16, [P, 2, S])
        kst = pages("kst", 18, [P, 2, S])
        kmem = pages("kmem", 36, [P, MEM_HEADS, MEM])
        vmem = pages("vmem", 38, [P, NMEM, BR])
        kpe = pages("kpe", 40, [P, S])
        pt2 = [pages(f"pt2_{i}", p, [P, S]) for i, p in enumerate((41, 42, 43))]
        v2 = pages("v2", 24, [P, NQ, 2 * BR])
        qmem = pages("qmem", 32, [P, MEM_HEADS, S])
        cqr = pages("cqr", 0, [P, NQR + NKV, S])
        cqs = pages("cqs", 5, [P, 2, S])
        cqi = pages("cqi", 7, [P, 2, S])
        cqf = pages("cqf", 9, [P, 2, S])
        jst = pages("jst", 44, [P, 2, S])
        off_h = base + ND * S * 4
        ring_q = [at(f"ringq{i}", off_h + (5 + i) * PAGE, [P, S]) for i in range(2)]
        ring_k = [at("ringk0", off_h + 7 * PAGE, [P, S]), at("ringk1", off_h + (ND + 5) * PAGE, [P, S])]
        ring_p = [at(f"ringp{i}", off_h + (ND + 6 + i) * PAGE, [P, S]) for i in range(2)]
        gq = [pages(f"gq{i}", 24 + i, [P, S]) for i in range(2)]
        kg = pages("kg", 26, [P, GKV, S])
        vg = pages("vg", 28, [P, NQ, GKV * P])
        sm2 = at("sm2", rgw_off, [P, NQ, S])
        fga2 = pages("fga2", 24, [P, 2, S])
        fhf2 = pages("fhf2", 26, [P, 2, S])

        ps = [ctx.enter_context(nc.psum_tensor(f"bank{i}", [P, S], F32)) for i in range(8)]
        sems = {n: ctx.enter_context(nc.semaphore(n)) for n in (
            "x_in0 x_in1 con_in par_in rgw_in pos_in mem_in tab_in out_stored "
            "full slot sqmm turned pv msqmm csqmm turned2 pv2 "
            "act_step act_read hi lam_exp sin tabc sq rms hh swap if wcol wrow fexp relu cin mqk mv mo acol mnm mex mwx "
            "rcin mhsq mstd yh rg rr ri rth ra rs av sig e pt yfo sigc merh fcin fga ffh msq mrms memh kraw ksq "
            "vmem kst craw kperaw jsq qmemraw csq cstd lath jstd jswap v2 e2 pt2 mixh fga2 ffh2 "
            "dve_step dve_read bcol lo lam_abs spn ang nri hf h qi ki fabs arow negm negg acc conv mdm mp mh mhc xc "
            "yf y rq aq ak merged sm p merf mer x fconv fhf ff xhalf memn mem kmem clat lat jn jend nmx2 p2 mix "
            "fhf2 ff2 out").split()}
        landed = [ctx.enter_context(nc.semaphore(f"landed{i}")) for i in range(RAW)]
        for i in range(RAW):
            sems[f"landed{i}"] = landed[i]
        for s in range(N_SLOTS):
            marks[("landed", s)] = (f"landed{s % RAW}", 16 * (s // RAW + 1))
        for n in ("con", "par", "rgw", "pos"):
            marks[(n + "_in",)] = (n + "_in", 16)
        for l in range(DEPTH):
            marks["mem_in", l] = ("mem_in", 16 * (l + 1))
            marks["tab_in", l] = ("tab_in", 32 * (l + 1))
        ones64 = con[:, C_ONE64:C_ONE64 + P]

        def jobs(l, u):
            h = u - MEM_HEADS
            g = lambda name, i=0: par[:, PCOL2[name] + i:PCOL2[name] + i + 1]
            if u < MEM_HEADS:
                return [(("q2", l, u), qmem[:, u, :], ones, P, g("memq", l), False)]
            if l == 1:
                return [(("q2", l, u), gq[h % 2][:, :], ones, P, g("gqa_q"), True)]
            out = [(("q2", l, u), ring_q[h % 2][:, :], ones, P, g("mla_q"), False),
                   (("k2", l, u), ring_k[h % 2][:, :], ones, P, g("mla_k"), False)]
            if h % 2 == 0:
                out.append((("pe2", l, u), ring_p[h // 2 % 2][:, :], ones64, ROPE, g("mla_qpe"), True))
            return out

        sqbuf = [cacc[:, 0, :], cacc[:, 1, :], cin[:, 0, 0:S]]
        swap2 = cin[:, 1, 0:S]

        ident = con[:, C_ID:C_ID + P]
        ones = con[:, C_ONE:C_ONE + P]
        mask_st = con[:, C_ST:C_ST + P]
        mask_qk = con[:, C_QK:C_QK + P]

        def bank(t):
            return ps[t % 8]

        def pcol(name, l, i=0, n=1):
            c = l * PLAYER + PCOL[name] + i
            return par[:, c:c + n]

        def norm_gain(n, c):
            if n == N_FINAL:
                return par[:, P_FINAL + c:P_FINAL + c + 1]
            if n > N_FINAL:
                i = n - N_SECOND
                o = PCOL2["norm_ffn" if i % 2 else "norm_mix"] + i // 2 * ND + c
                return par[:, o:o + 1]
            return pcol("norm_ffn" if n % 2 else "norm_mix", n // 2, c)

        block = ctx.enter_context(nc.Block())

        @block.sync
        def _(eng):
            sp = Engine("sp", sems, marks, known)
            eng.dma_start(par[:, :], A["par"]).then_inc(sems["par_in"], 16)
            eng.dma_start(pos_i[:, :], A["pos"][0:1, :].partition_broadcast(P)).then_inc(sems["pos_in"], 16)
            eng.dma_start(con[:, :], A["con"]).then_inc(sems["con_in"], 16)
            for i in range(2):
                c = slice(i * ND // 2, (i + 1) * ND // 2)
                eng.dma_start(x[:, c, :], A["x"][:, c, :]).then_inc(sems[f"x_in{i}"], 16)
            for s in range(2):
                eng.dma_start(raw[:, s % RAW, :], A["w"][s]).then_inc(landed[s % RAW], 16)
            eng.dma_start(rgw[:, :, :, :], A["rgw"]).then_inc(sems["rgw_in"], 16)
            for s in range(2, N_SLOTS):
                if s >= RAW:
                    eng.wait_ge(*sp.after("lo", s - RAW))
                eng.dma_start(raw[:, s % RAW, :], A["w"][s]).then_inc(landed[s % RAW], 16)
            for c in range(ND):
                eng.wait_ge(*sp.after("out", c))
            eng.dma_start(A["out"], x[:, :, :]).then_inc(sems["out_stored"], 16)
            eng.wait_ge(sems["out_stored"], 16)

        @block.tensor
        def _(eng):
            pe = Engine("pe", sems, marks, known)

            def opened(t):
                t -= 8
                while t in UNUSED:
                    t -= 8
                if t >= 0:
                    eng.wait_ge(*pe.after("read", t))

            def three(out, wh, wl, rh, rl, start, stop):
                eng.matmul(out, wh, rl, start=start, stop=False)
                eng.matmul(out, wh, rh, start=False, stop=False)
                return eng.matmul(out, wl, rh, start=False, stop=stop)

            def wblk(b, n=1):
                s, i = b // SLOT % HALF, b % SLOT
                return whi[:, s, i * P:(i + n) * P], wlo[:, s, i * P:(i + n) * P]

            def take(b):
                if b % SLOT == 0:
                    eng.wait_ge(*pe.after("lo", b // SLOT))

            def gemm(t, b, nk, rh, rl, key, start=True):
                opened(t)
                for k in range(nk):
                    take(b)
                    eng.wait_ge(*pe.after(*key(k)))
                    wh, wl = wblk(b)
                    ins = three(bank(t)[:, :], wh, wl, rh[:, k, :], rl[:, k, :], k == 0, k == nk - 1)
                    ends = [("full", t)] if k == nk - 1 else []
                    if b % SLOT == SLOT - 1:
                        ends.append(("slot", b // SLOT))
                    if ends:
                        ins.then_inc(*pe.signals(*ends))
                    b += 1

            def gemm_tokens(t, b, nk, lh, ll, key):
                for i in range(NQ):
                    opened(t + i)
                for k in range(nk):
                    take(b)
                    eng.wait_ge(*pe.after(*key(k)))
                    wh, wl = wblk(b, 4)
                    for i in range(NQ):
                        c = slice(i * P, i * P + P)
                        ins = three(bank(t + i)[:, :], lh[:, k, c], ll[:, k, c], wh, wl, k == 0, k == nk - 1)
                        ends = [("full", t + i)] if k == nk - 1 else []
                        if i == NQ - 1 and (b + 3) % SLOT == SLOT - 1:
                            ends.append(("slot", b // SLOT))
                        if ends:
                            ins.then_inc(*pe.signals(*ends))
                    b += 4

            def norm(n):
                t = TILE["norm", n]
                opened(t)
                eng.wait_ge(*pe.after("con_in"))
                for c in range(ND):
                    eng.wait_ge(*pe.after("sq", n, c))
                    ins = eng.matmul(bank(t)[:, :], ones, nsq[:, c % 2, :], start=c == 0, stop=c == ND - 1)
                    ins.then_inc(*pe.signals(("sqmm", n, c), *([("full", t)] if c == ND - 1 else [])))

            def tile_mm(t, pairs):
                opened(t)
                for i, (out, a, b) in enumerate(pairs):
                    ins = eng.matmul(out, a, b, start=i == 0, stop=i == len(pairs) - 1)
                ins.then_inc(*pe.signals(("full", t)))

            for l in range(DEPTH):
                n1 = 2 * l
                hkey = lambda k, n1=n1: ("h", n1, k)
                norm(n1)
                for m in range(4):
                    gemm(TILE["qi", l] + m, BLOCK["qi", l] + 8 * m, 8, hh, hl, hkey)
                gemm(TILE["ki", l], BLOCK["ki", l], 8, hh, hl, hkey)
                t, b = TILE["if", l], BLOCK["if", l]
                opened(t)
                for k in range(ND):
                    take(b + k)
                    wh, wl = wblk(b + k)
                    ins = three(bank(t)[:, :], wh, wl, hh[:, k, :], hl[:, k, :], k == 0, k == ND - 1)
                assert (b + ND) % SLOT == 0
                ins.then_inc(*pe.signals(("full", t), ("slot", b // SLOT)))
                eng.wait_ge(*pe.after("wrow", l))
                opened(t + 1)
                for i in range(NQ):
                    ins = eng.transpose(bank(t + 1)[:, 8 * i:8 * i + 8], wrow[:, P * i:P * i + P], con[0:8, 0:8])
                ins.then_inc(*pe.signals(("full", t + 1)))
                t = TILE["idx", l]
                for m in range(4):
                    eng.wait_ge(*pe.after("qi", l, m))
                eng.wait_ge(*pe.after("ki", l))
                for j in range(3, 0, -1):
                    for h in range(A_HEADS):
                        r = slice(64 * (h % 2), 64 * (h % 2) + 64)
                        tile_mm(t, [(bank(t)[:, 0:P * (j + 1)], qi[r, h // 2, P * j:P * j + P],
                                     ki[r, 0:P * (j + 1)])])
                        t += 1
                for m in range(8):
                    gemm(TILE["mqk", l] + m, BLOCK["mqk", l] + 8 * m, 8, hh, hl, hkey)
                gemm_tokens(TILE["mv", l], BLOCK["mv", l], 8, hh, hl, hkey)
                t = TILE["acol", l]
                opened(t)
                eng.wait_ge(*pe.after("arow", l))
                for j in range(NQ):
                    ins = eng.transpose(bank(t)[:, 4 * j:4 * j + 4], rows[0][:, P * j:P * j + P], con[0:4, 0:4])
                ins.then_inc(*pe.signals(("full", t)))
                def m1(h):
                    t = TILE["m1", l, h]
                    one_row = con[0:4, h:h + 1].to_broadcast([4, P])
                    eng.wait_ge(*pe.after("negm", l))
                    eng.wait_ge(*pe.after("negg", l))
                    tile_mm(t, [(bank(t)[:, :], one_row, negm[:, :])])
                    tile_mm(t + 1, [(bank(t + 1)[:, :], one_row, negg[:, :])])
                    eng.wait_ge(*pe.after("mqk", l, h))
                    eng.wait_ge(*pe.after("mqk", l, 4 + h))
                    for j in range(NQ):
                        tile_mm(t + 2 + j, [(bank(t + 2 + j)[:, P * j:], mk[:, h, P * j:P * j + P], mq[:, h, P * j:])])

                m1(0)
                for h in range(M_HEADS):
                    gemm(TILE["rx", l, h], BLOCK["rx", l, h], 8, hh, hl, hkey)
                    gemm(TILE["mo", l, h], BLOCK["mo", l, h], 8, hh, hl, hkey)
                    t = TILE["m2", l, h]
                    for i in range(NQ):
                        eng.wait_ge(*pe.after("mv", l, i))
                        eng.wait_ge(*pe.after("mp", l, h, i))
                    tile_mm(t, [(bank(t)[:, P * j:], mv[:, j, P * h:P * h + P], mp[:, j, P * j:]) for j in range(NQ)])
                    tile_mm(t + 1, [(bank(t + 1)[:, P * j:], ones, mp[:, j, P * j:]) for j in range(NQ)])
                    gemm(TILE["ak", l, h], BLOCK["ak", l, h], 8, hh, hl, hkey)
                    eng.wait_ge(*pe.after("mh", l, h))
                    t = TILE["m3", l, h]
                    tile_mm(t, [(bank(t)[:, :], ones, mq[:, h, :])])
                    if h + 1 < M_HEADS:
                        m1(h + 1)
                    eng.wait_ge(*pe.after("mhsq", l, h))
                    t = TILE["m4", l, h]
                    tile_mm(t, [(bank(t)[:, :], ones, mwx[:, 0, :])])
                eng.wait_ge(*pe.after("rgw_in"))
                for c in range(NBR):
                    gemm(TILE["rg", l, c], BLOCK["rg", l, c], 8, hh, hl, hkey)
                    eng.wait_ge(*pe.after("xc", l, c))
                    t = TILE["rgl", l, c]
                    tile_mm(t, [(bank(t)[:, :], rgw[:, l, c, :], xc[:, c, :])])
                    tile_mm(t + 1, [(bank(t + 1)[:, :], rgw[:, l, 4 + c, :], xc[:, c, :])])
                    gemm(TILE["aq", l, c], BLOCK["aq", l, c], 8, hh, hl, hkey)
                gemm_tokens(TILE["av", l], BLOCK["av", l], 8, hh, hl, hkey)

                def branch(b, m):
                    t, blk = TILE["br", l, b, m], BLOCK["br", l, b, m]
                    gemm(t, blk, 8, hh, hl, hkey)
                    gemm(t + 1, blk + 8, 4, ah, al, lambda k: ("y", l, b, k))

                def scores(h, j):
                    t = score_tile(l, h, j)
                    r = slice(64 * (h % 2), 64 * (h % 2) + 64)
                    eng.wait_ge(*pe.after("aq", l, h // 2))
                    eng.wait_ge(*pe.after("ak", l, h // 2))
                    tile_mm(t, [(bank(t)[:, 0:P * (j + 1)], aq[r, h // 2, P * j:P * j + P],
                                 ak[r, h // 2, 0:P * (j + 1)])])

                def turn(h, j):
                    t = turn_tile(l, h, j)
                    opened(t)
                    eng.wait_ge(*pe.after("p", l, h, j))
                    for i in range(j + 1):
                        ins = eng.transpose(bank(t)[:, P * i:P * i + P], sm[:, j, P * i:P * i + P], ident)
                    ins.then_inc(*pe.signals(("full", t), ("turned", l, h, j)))

                def outputs(h):
                    to = out_tile(l, h)
                    hp = slice(P * (h // 2), P * (h // 2) + P)
                    for j in range(NQ + 1):
                        if j < NQ:
                            turn(h, j)
                            if h + 1 < A_HEADS:
                                scores(h + 1, j)
                        if j == 0:
                            opened(to)
                            for i in range(NQ):
                                eng.wait_ge(*pe.after("av", l, i))
                            continue
                        jj = j - 1
                        eng.wait_ge(*pe.after("pt", l, h, jj))
                        for i in range(jj + 1):
                            ins = eng.matmul(bank(to)[:, P * jj:P * jj + P], av[i][:, hp],
                                             pt[:, (4 * h + jj) % 3, P * i:P * i + P], start=i == 0, stop=i == jj)
                        ins.then_inc(*pe.signals(("pv", l, h, jj), *([("full", to)] if jj == NQ - 1 else [])))

                for m in range(ND):
                    branch(0, m)
                for j in range(NQ):
                    scores(0, j)
                for h in range(A_HEADS):
                    branch(1, h)
                    outputs(h)
                for m in range(ND):
                    gemm(TILE["gc", l] + m, BLOCK["gc", l] + 8 * m, 8, hh, hl, hkey)
                for m in range(ND):
                    gemm(TILE["bc", l] + m, BLOCK["bc", l] + 4 * m, 4, ah, al, lambda k: ("y", l, 2, k))
                for m in range(ND):
                    gemm(TILE["wo", l] + m, BLOCK["wo", l] + 8 * m, 8, hh, hl, lambda k: ("mer", l, k))
                norm(2 * l + 1)
                for half in range(2):
                    for p in range(NFF // 2):
                        t, b = TILE["up", l, half, p], BLOCK["up", l, half, p]
                        gemm(t, b, 8, hh, hl, lambda k: ("h", 2 * l + 1, k))
                        gemm(t + 1, b + 8, 8, hh, hl, lambda k: ("h", 2 * l + 1, k))
                    for m in range(ND):
                        gemm(TILE["down", l, half] + m, BLOCK["down", l, half] + 12 * m, 12, ah, al,
                             lambda k: ("ff", l, half, k))
            norm(N_FINAL)
            for l in range(DEPTH):
                n1 = N_SECOND + 2 * l
                hkey = lambda k: ("h", n1, k)
                t = TILE["memnorm", l]
                opened(t)
                for c in range(ND):
                    eng.wait_ge(*pe.after("msq", l, c))
                    ins = eng.matmul(bank(t)[:, 0:MEM], ones, msq[:, c % 2, :], start=c == 0, stop=c == ND - 1)
                    ins.then_inc(*pe.signals(("msqmm", l, c), *([("full", t)] if c == ND - 1 else [])))
                b = BLOCK["memk", l]
                for m in range(MEM_HEADS):
                    t = TILE["memk", l] + m
                    opened(t)
                    for k in range(ND):
                        take(b)
                        eng.wait_ge(*pe.after("mem", l, k))
                        wh, wl = wblk(b)
                        ins = three(bank(t)[:, 0:MEM], wh, wl, memh[:, k, :], meml[:, k, :], k == 0, k == ND - 1)
                        ends = [("full", t)] if k == ND - 1 else []
                        if b % SLOT == SLOT - 1:
                            ends.append(("slot", b // SLOT))
                        if ends:
                            ins.then_inc(*pe.signals(*ends))
                        b += 1
                b = BLOCK["memv", l]
                t = TILE["memv", l]
                for i in range(NMEM):
                    opened(t + i)
                for k in range(ND):
                    take(b)
                    wh, wl = wblk(b, 4)
                    for i in range(NMEM):
                        c = slice(i * P, i * P + P)
                        ins = three(bank(t + i)[:, :], memh[:, k, c], meml[:, k, c], wh, wl, k == 0, k == ND - 1)
                        ends = [("full", t + i)] if k == ND - 1 else []
                        if i == NMEM - 1 and (b + 3) % SLOT == SLOT - 1:
                            ends.append(("slot", b // SLOT))
                        if ends:
                            ins.then_inc(*pe.signals(*ends))
                    b += 4
                for i in range(2):
                    t = TILE["memkst", l] + i
                    eng.wait_ge(*pe.after("ksq", l, i))
                    tile_mm(t, [(bank(t)[:, :], ones, ksq[:, i, :])])
                norm(n1)
                if l == 0:
                    for name, n in (("cq", NQR), ("ckv", NKV), ("kpe", 1), ("qmem", 4)):
                        for m in range(n):
                            gemm(TILE[name, l] + m, BLOCK[name, l] + ND * m, ND, hh, hl, hkey)
                    for name, c0, n in (("cqst", 0, NQR), ("ckvst", NQR, NKV)):
                        t = TILE[name, l]
                        opened(t)
                        for c in range(n):
                            eng.wait_ge(*pe.after("csq", l, c0 + c))
                            ins = eng.matmul(bank(t)[:, :], ones, cqs[:, (c0 + c) % 2, :], start=c == 0, stop=c == n - 1)
                            ins.then_inc(*pe.signals(("csqmm", l, c0 + c), *([("full", t)] if c == n - 1 else [])))
                    t = TILE["kst", l]
                    eng.wait_ge(*pe.after("jsq", l, "kpe"))
                    tile_mm(t, [(bank(t)[:, :], ones64, sqbuf[0])])
                    for g in range(2):
                        b, t = BLOCK["v2", l] + 8 * g, TILE["v2", l] + 4 * g
                        gemm_tokens(t, b, NKV, hh[:, NQR:, :], hl[:, NQR:, :], lambda k: ("lat", l, NQR + k))
                else:
                    for m in range(GKV):
                        gemm(TILE["kg", l] + m, BLOCK["kg", l] + ND * m, ND, hh, hl, hkey)
                    t, b = TILE["vg", l], BLOCK["vg", l]
                    for i in range(NQ):
                        opened(t + i)
                    for k in range(ND):
                        take(b)
                        wh, wl = wblk(b, 2)
                        for i in range(NQ):
                            c = slice(i * P, i * P + P)
                            ins = three(bank(t + i)[:, 0:GKV * P], hh[:, k, c], hl[:, k, c], wh, wl, k == 0, k == ND - 1)
                            ends = [("full", t + i)] if k == ND - 1 else []
                            if i == NQ - 1 and (b + 1) % SLOT == SLOT - 1:
                                ends.append(("slot", b // SLOT))
                            if ends:
                                ins.then_inc(*pe.signals(*ends))
                        b += 2
                    for m in range(4):
                        gemm(TILE["qmem", l] + m, BLOCK["qmem", l] + ND * m, ND, hh, hl, hkey)
                    for m in range(GKV):
                        t = TILE["kst", l] + m
                        eng.wait_ge(*pe.after("jsq", l, "kg", m))
                        tile_mm(t, [(bank(t)[:, :], ones, sqbuf[m])])

                def scores2(u, j):
                    t = score_tile2(l, u, j)
                    q = slice(P * j, P * j + P)
                    eng.wait_ge(*pe.after("q2", l, u))
                    if u < MEM_HEADS:
                        eng.wait_ge(*pe.after("kmem", l))
                        tile_mm(t, [(bank(t)[:, 0:MEM], qmem[:, u, q], kmem[:, u, :])])
                        return
                    h = u - MEM_HEADS
                    if l == 1:
                        eng.wait_ge(*pe.after("kg", l, h // (H2 // GKV)))
                        tile_mm(t, [(bank(t)[:, :], gq[h % 2][:, q], kg[:, h // (H2 // GKV), :])])
                        return
                    eng.wait_ge(*pe.after("k2", l, u))
                    eng.wait_ge(*pe.after("pe2", l, u - h % 2))
                    eng.wait_ge(*pe.after("kpe", l))
                    r = slice(64 * (h % 2), 64 * (h % 2) + 64)
                    tile_mm(t, [(bank(t)[:, :], ring_q[h % 2][:, q], ring_k[h % 2][:, :]),
                                (bank(t)[:, :], ring_p[h // 2 % 2][r, q], kpe[r, :])])

                def turn2(u, j):
                    t = turn_tile2(l, u, j)
                    opened(t)
                    eng.wait_ge(*pe.after("p2", l, u, j))
                    for i in range(NMEM if u < MEM_HEADS else NQ):
                        ins = eng.transpose(bank(t)[:, P * i:P * i + P], sm2[:, j, P * i:P * i + P], ident)
                    ins.then_inc(*pe.signals(("full", t), ("turned2", l, u, j)))

                def prep_a(u):
                    if not prep_tiles(l, u):
                        return
                    t, b = TILE["pa", l, u], BLOCK["pa", l, u]
                    for kind, n in prep_tiles(l, u):
                        if l == 1:
                            gemm(t, b, n, hh, hl, hkey)
                        elif kind == "k":
                            gemm(t, b, n, hh[:, NQR:, :], hl[:, NQR:, :], lambda k: ("lat", l, NQR + k))
                        else:
                            gemm(t, b, n, hh, hl, lambda k: ("lat", l, k))
                        t += 1
                        b += n

                def prep_b(u):
                    for i, (key, buf, one, n, gain, turns) in enumerate(jobs(l, u)):
                        t = TILE["pb", l, u] + i
                        eng.wait_ge(*pe.after("jsq", *key))
                        tile_mm(t, [(bank(t)[:, :], one, sqbuf[i])])

                for u in range(2):
                    prep_b(u)
                for j in range(NQ):
                    scores2(0, j)
                for u in range(HEADS2):
                    if u + 2 < HEADS2:
                        prep_a(u + 2)
                    to = out_tile2(l, u)
                    h = u - MEM_HEADS
                    nk = NMEM if u < MEM_HEADS else NQ
                    for j in range(NQ + 1):
                        if j < NQ:
                            turn2(u, j)
                            if u + 1 < HEADS2:
                                scores2(u + 1, j)
                        if j == 0:
                            continue
                        if j == 1:
                            opened(to)
                            for i in range(nk):
                                eng.wait_ge(*pe.after(*(("vmem", l, i) if u < MEM_HEADS else ("v2", l, i))))
                        jj = j - 1
                        eng.wait_ge(*pe.after("pt2", l, u, jj))
                        for i in range(nk):
                            if u < MEM_HEADS:
                                v = vmem[:, i, u * P:u * P + P]
                            elif l == 0:
                                v = v2[:, i, h * P:h * P + P]
                            else:
                                g = h // (H2 // GKV)
                                v = vg[:, i, g * P:g * P + P]
                            ins = eng.matmul(bank(to)[:, P * jj:P * jj + P], v, pt2[(4 * u + jj) % 3][:, P * i:P * i + P],
                                             start=i == 0, stop=i == nk - 1)
                        ins.then_inc(*pe.signals(("pv2", l, u, jj), *([("full", to)] if jj == NQ - 1 else [])))
                        if j == 1 and u + 2 < HEADS2:
                            prep_b(u + 2)
                for m in range(ND):
                    gemm(TILE["wo2", l] + m, BLOCK["wo2", l] + MIX * m, MIX, ah, al,
                         lambda k: ("mix", l, (k + MEM_HEADS) % HEADS2))
                norm(n1 + 1)
                for half in range(2):
                    for p in range(NFF2 // 2):
                        t, b = TILE["up2", l, half, p], BLOCK["up2", l, half, p]
                        gemm(t, b, 8, hh, hl, lambda k: ("h", n1 + 1, k))
                        gemm(t + 1, b + 8, 8, hh, hl, lambda k: ("h", n1 + 1, k))
                    for m in range(ND):
                        gemm(TILE["down2", l, half] + m, BLOCK["down2", l, half] + 11 * m, 11, ah, al,
                             lambda k: ("ff2", l, half, k))

        @block.scalar
        def _(eng):
            act = Engine("act", sems, marks, known)
            nxt = [0]

            def ahead(b):
                while nxt[0] <= min(b // SLOT + 1, N_SLOTS - 1):
                    s = nxt[0]
                    eng.wait_ge(*act.after("landed", s))
                    if s >= HALF:
                        eng.wait_ge(*act.after("slot", s - HALF))
                    eng.activation(whi[:, s % HALF, :], raw[:, s % RAW, :], ACT.Copy).then_inc(*act.signals(("hi", s)))
                    eng.wait_ge(*act.previous)
                    nxt[0] += 1

            def read(t, out, func, *names, **kw):
                eng.wait_ge(*act.after("full", t))
                eng.activation(out, bank(t)[:, :], func, **kw).then_inc(*act.signals(("read", t), *names))
                eng.wait_ge(*act.previous)

            def norm(n):
                for c in range(ND):
                    eng.wait_ge(*act.after("x", n, c))
                    if c >= 2:
                        eng.wait_ge(*act.after("sqmm", n, c - 2))
                    eng.activation(nsq[:, c % 2, :], x[:, c, :], ACT.Square).then_inc(*act.signals(("sq", n, c)))
                    eng.wait_ge(*act.previous)
                t = TILE["norm", n]
                eng.wait_ge(*act.after("full", t))
                eng.activation(nrm[:, :], bank(t)[:, :], ACT.Sqrt, bias=bcol[:, 0:1], scale=1.0 / D).then_inc(*act.signals(("read", t), ("rms", n)))
                eng.wait_ge(*act.previous)
                if n != N_FINAL:
                    for c in range(ND):
                        eng.wait_ge(*act.after("hf", n, c))
                        eng.activation(hh[:, c, :], nhf[:, c % 2, :], ACT.Copy).then_inc(*act.signals(("hh", n, c)))
                        eng.wait_ge(*act.previous)

            def rope(t, swap, key):
                eng.wait_ge(*act.after("full", t))
                for g in range(4):
                    o = g ^ 1
                    ins = eng.activation(swap[32 * g:32 * g + 32, :], bank(t)[32 * o:32 * o + 32, :], ACT.Copy)
                ins.then_inc(*act.signals(("swap",) + key))
                eng.wait_ge(*act.previous)

            eng.wait_ge(*act.after("bcol"))
            ahead(0)
            eng.wait_ge(*act.after("con_in"))
            eng.wait_ge(*act.after("par_in"))
            for l in range(DEPTH):
                if l == 0:
                    eng.wait_ge(*act.after("lam_abs"))
                    eng.activation(spt[:, 1, :], spt[:, 0, :], ACT.Exp, scale=-1.0).then_inc(*act.signals(("lam_exp",)))
                    eng.wait_ge(*act.previous)
                norm(2 * l)
                if l == 0:
                    eng.wait_ge(*act.after("ang", 0))
                    eng.activation(tabs[:, :], rtab[:, 2, :], ACT.Sin).then_inc(*act.signals(("sin",)))
                    eng.wait_ge(*act.previous)
                    eng.wait_ge(*act.after("ang", 1))
                    eng.activation(tabc[:, :], rtab[:, 4, :], ACT.Sin).then_inc(*act.signals(("tabc",)))
                    eng.wait_ge(*act.previous)
                for m in range(4):
                    ahead(BLOCK["qi", l] + 8 * m + 7)
                    if m >= 2:
                        eng.wait_ge(*act.after("qi", l, m - 2))
                    rope(TILE["qi", l] + m, rsw[:, m % 2, :], ("qi", l, m))
                ahead(BLOCK["ki", l] + 7)
                eng.wait_ge(*act.after("qi", l, 2))
                rope(TILE["ki", l], rsw[:, 0, :], ("ki", l))
                ahead(BLOCK["if", l] + 7)
                t = TILE["if", l]
                eng.wait_ge(*act.after("full", t))
                eng.activation(rows[0][:, :], bank(t)[0:4, :], ACT.Identity, bias=par[0:4, l * PLAYER + PCOL["i_bias"]:l * PLAYER + PCOL["i_bias"] + 1]).then_inc(*act.signals())
                eng.wait_ge(*act.previous)
                eng.activation(rows[1][:, :], bank(t)[32:36, :], ACT.Copy).then_inc(*act.signals(("if", l)))
                eng.wait_ge(*act.previous)
                eng.activation(wrow[:, :], bank(t)[64:72, :], ACT.Copy,
                               scale=float(A_HEADS) ** -0.5).then_inc(*act.signals(("read", t), ("wrow", l)))
                eng.wait_ge(*act.previous)
                t += 1
                eng.wait_ge(*act.after("full", t))
                eng.activation(wcol[:, :, :], bank(t)[:, 0:32].rearrange("p (a b) -> p a b", b=8), ACT.Copy).then_inc(*act.signals(("read", t), ("wcol", l)))
                eng.wait_ge(*act.previous)
                eng.wait_ge(*act.after("fabs", l))
                eng.activation(rows[3][:, :], rows[2][:, :], ACT.Exp, scale=-1.0).then_inc(*act.signals(("fexp", l)))
                eng.wait_ge(*act.previous)
                t = TILE["idx", l]
                for j in range(3, 0, -1):
                    for h in range(A_HEADS):
                        i = t - TILE["idx", l]
                        eng.wait_ge(*act.after("full", t))
                        if i >= 2:
                            eng.wait_ge(*act.after("acc", l, i - 2))
                        eng.activation(relu[:, i % 2, 0:P * (j + 1)], bank(t)[:, 0:P * (j + 1)],
                                                ACT.Relu, scale=float(HD) ** -0.5).then_inc(*act.signals(("read", t), ("relu", l, i)))
                        eng.wait_ge(*act.previous)
                        t += 1
                def mqk_silu(m):
                    eng.wait_ge(*act.after("conv", l, m))
                    dst = mq if m < 4 else mk
                    eng.activation(dst[:, m % 4, :], cacc[:, m % 2, :], ACT.Silu).then_inc(*act.signals(("mqk", l, m)))
                    eng.wait_ge(*act.previous)
                for m in range(8):
                    ahead(BLOCK["mqk", l] + 8 * m + 7)
                    t = TILE["mqk", l] + m
                    if m >= 2:
                        eng.wait_ge(*act.after("conv", l, m - 2))
                    read(t, cin[:, m % 2, 3:3 + S], ACT.Copy, ("cin", l, m))
                    if m:
                        mqk_silu(m - 1)
                mqk_silu(7)
                ahead(BLOCK["mv", l] + 31 - SLOT)
                for i in range(NQ):
                    if i == 0:
                        ahead(BLOCK["mv", l] + 31)
                    read(TILE["mv", l] + i, mv[:, i, :], ACT.Copy, ("mv", l, i))
                t = TILE["acol", l]
                eng.wait_ge(*act.after("full", t))
                eng.activation(acol[:, :, :], bank(t)[:, 0:16].rearrange("p (a b) -> p a b", b=4), ACT.Copy).then_inc(*act.signals(("read", t), ("acol", l)))
                eng.wait_ge(*act.previous)
                def m_open(h):
                    t = TILE["m1", l, h]
                    read(t, mnm[:, :], ACT.Copy, ("mnm", l, h))
                    read(t + 1, mex[:, :], ACT.Exp, ("mex", l, h))

                def m_weights(h, js):
                    eng.wait_ge(*act.after("mdm", l, h))
                    for j in js:
                        if j >= 2:
                            eng.wait_ge(*act.after("mp", l, h, j - 2))
                        bias = acol[:, j, h:h + 1]
                        ins = eng.activation(mwx[:, j % 2, P * j:P * j + P], mdm[:, j, :], ACT.Exp, bias=bias)
                        if j < NQ - 1:
                            ins = eng.activation(mwx[:, j % 2, P * j + P:], mnm[:, P * j + P:], ACT.Exp, bias=bias)
                        ins.then_inc(*act.signals(("mwx", l, h, j)))
                        eng.wait_ge(*act.previous)

                m_open(0)
                m_weights(0, range(NQ))
                for h in range(M_HEADS):
                    ahead(BLOCK["rx", l, h] + 7)
                    if h >= 2:
                        eng.wait_ge(*act.after("xc", l, h - 2))
                    read(TILE["rx", l, h], cin[:, h % 2, 3:3 + S], ACT.Copy, ("rcin", l, h))
                    ahead(BLOCK["mo", l, h] + 7)
                    read(TILE["mo", l, h], mo[:, :], ACT.Sigmoid, ("mo", l, h))
                    ahead(BLOCK["ak", l, h] + 7)
                    if h:
                        eng.wait_ge(*act.after("ak", l, h - 1))
                    rope(TILE["ak", l, h], aswap, ("ak", l, h))
                    eng.wait_ge(*act.after("mhc", l, h))
                    eng.activation(mwx[:, 0, :], mq[:, h, :], ACT.Square).then_inc(*act.signals(("mhsq", l, h)))
                    eng.wait_ge(*act.previous)
                    if h + 1 < M_HEADS:
                        m_open(h + 1)
                    t = TILE["m4", l, h]
                    read(t, mdn[:, :], ACT.Sqrt, ("mstd", l, h), bias=bcol[:, 0:1], scale=1.0 / P)
                    if h + 1 < M_HEADS:
                        m_weights(h + 1, (0, 1))
                    eng.wait_ge(*act.after("yf", l, 0, h))
                    eng.activation(ah[:, h, :], yf[:, h, :], ACT.Copy).then_inc(*act.signals(("yh", l, 0, h)))
                    eng.wait_ge(*act.previous)
                    if h + 1 < M_HEADS:
                        m_weights(h + 1, (2, 3))
                for c in range(NBR):
                    ahead(BLOCK["rg", l, c] + 7)
                    read(TILE["rg", l, c], rg[:, c, :], ACT.Gelu_apprx_tanh, ("rg", l, c))
                    t = TILE["rgl", l, c]
                    if c:
                        eng.wait_ge(*act.after("rgdone", l, c - 1))
                    read(t, rt[:, 0, :], ACT.Sigmoid, ("rr", l, c), bias=pcol("rglru_b_a", l, c))
                    read(t + 1, rt[:, 1, :], ACT.Sigmoid, ("ri", l, c), bias=pcol("rglru_b_x", l, c))
                    eng.wait_ge(*act.after("spn"))
                    eng.activation(rt[:, 2, :], rt[:, 0, :], ACT.Tanh,
                                   scale=sp8[:, 4 * l + c:4 * l + c + 1]).then_inc(*act.signals(("rth", l, c)))
                    eng.wait_ge(*act.previous)
                    eng.activation(rt[:, 3, :], rt[:, 0, :], ACT.Exp,
                                   scale=spt[:, 5, 4 * l + c:4 * l + c + 1]).then_inc(*act.signals(("ra", l, c)))
                    eng.wait_ge(*act.previous)
                    eng.wait_ge(*act.after("rq", l, c))
                    eng.activation(rt[:, 5, :], rt[:, 4, :], ACT.Sqrt, scale=2.0).then_inc(*act.signals(("rs", l, c)))
                    eng.wait_ge(*act.previous)
                    ahead(BLOCK["aq", l, c] + 7)
                    if c >= 2:
                        eng.wait_ge(*act.after("aq", l, c - 2))
                    rope(TILE["aq", l, c], rsw2[:, c % 2, :], ("aq", l, c))
                ahead(BLOCK["av", l] + 31 - SLOT)
                for i in range(NQ):
                    if i == 0:
                        ahead(BLOCK["av", l] + 31)
                    read(TILE["av", l] + i, av[i][:, :], ACT.Copy, ("av", l, i))

                n_sig = [0]

                def branch(b, m):
                    t, blk = TILE["br", l, b, m], BLOCK["br", l, b, m]
                    ahead(blk + 7)
                    if n_sig[0]:
                        eng.wait_ge(*act.after("merged", l, (8 * b + m - 1) // 8, (m - 1) % 8))
                    read(t, sig[:, :], ACT.Sigmoid, ("sig", l, b, m))
                    n_sig[0] += 1
                    ahead(blk + 11)

                def split_y(b):
                    for k in range(4):
                        if b == 2:
                            eng.wait_ge(*act.after("yfo", l, 2 * k))
                            eng.wait_ge(*act.after("yfo", l, 2 * k + 1))
                        else:
                            eng.wait_ge(*act.after("yf", l, b, k))
                        if k == 0:
                            eng.wait_ge(*act.after("full", TILE["br", l, b - 1, ND - 1] + 1))
                        eng.activation(ah[:, k, :], yf[:, k, :], ACT.Copy).then_inc(*act.signals(("yh", l, b, k)))
                        eng.wait_ge(*act.previous)

                def exp(h, j):
                    eng.wait_ge(*act.after("sm", l, h, j))
                    eng.activation(sm[:, j, 0:P * (j + 1)], sm[:, j, 0:P * (j + 1)], ACT.Exp,
                                   bias=nmx[:, j:j + 1], scale=-1.0,
                                   accum_out=rsum[:, j:j + 1]).then_inc(*act.signals(("e", l, h, j)))
                    eng.wait_ge(*act.previous)

                for m in range(ND):
                    branch(0, m)
                split_y(1)
                for j in range(NQ):
                    exp(0, j)
                for h in range(A_HEADS):
                    branch(1, h)
                    for j in range(NQ):
                        t = turn_tile(l, h, j)
                        u = 4 * h + j
                        if u >= 3:
                            eng.wait_ge(*act.after("pv", l, (u - 3) // 4, (u - 3) % 4))
                        eng.wait_ge(*act.after("full", t))
                        eng.activation(pt[:, u % 3, 0:P * (j + 1)], bank(t)[:, 0:P * (j + 1)], ACT.Copy).then_inc(*act.signals(("read", t), ("pt", l, h, j)))
                        eng.wait_ge(*act.previous)
                        if j and h + 1 < A_HEADS:
                            exp(h + 1, j - 1)
                    if h + 1 < A_HEADS:
                        exp(h + 1, NQ - 1)
                    t = out_tile(l, h)
                    r = slice(64 * (h % 2), 64 * (h % 2) + 64)
                    eng.wait_ge(*act.after("full", t))
                    eng.activation(yf[r, h // 2, :], bank(t)[r, :], ACT.Copy).then_inc(*act.signals(("read", t), ("yfo", l, h)))
                    eng.wait_ge(*act.previous)
                for m in range(ND):
                    ahead(BLOCK["gc", l] + 8 * m + 7)
                    read(TILE["gc", l] + m, sigc[:, m, :], ACT.Sigmoid, ("sigc", l, m))
                split_y(2)
                for m in range(ND):
                    ahead(BLOCK["bc", l] + 4 * m + 3)
                    eng.wait_ge(*act.after("merf", l, m))
                    if m == 0:
                        eng.wait_ge(*act.after("full", TILE["gc", l] + ND - 1))
                    eng.activation(hh[:, m, :], mer[:, m, :], ACT.Copy).then_inc(*act.signals(("merh", l, m)))
                    eng.wait_ge(*act.previous)
                for m in range(ND):
                    ahead(BLOCK["wo", l] + 8 * m + 7)
                norm(2 * l + 1)
                for half in range(2):
                    for p in range(NFF // 2):
                        t, b = TILE["up", l, half, p], BLOCK["up", l, half, p]
                        i = half * NFF // 2 + p
                        ahead(b + 7)
                        if i >= 2:
                            eng.wait_ge(*act.after("fconv", l, i - 2))
                        read(t, cin[:, i % 2, 3:3 + S], ACT.Copy, ("fcin", l, i))
                        ahead(b + 15)
                        eng.wait_ge(*act.after("fconv", l, i))
                        if i >= 2:
                            eng.wait_ge(*act.after("fhf", l, i - 2))
                        eng.activation(fga[:, i % 2, :], cacc[:, i % 2, :], ACT.Gelu_apprx_tanh).then_inc(*act.signals(("fga", l, i)))
                        eng.wait_ge(*act.previous)
                        if p:
                            eng.wait_ge(*act.after("fhf", l, i - 1))
                            eng.activation(ah[:, p - 1, :], fhf[:, (i - 1) % 2, :], ACT.Copy).then_inc(*act.signals(("ffh", l, half, p - 1)))
                            eng.wait_ge(*act.previous)
                        elif half:
                            eng.wait_ge(*act.after("full", TILE["down", l, 0] + ND - 1))
                    p = NFF // 2
                    i = half * NFF // 2 + p
                    eng.wait_ge(*act.after("fhf", l, i - 1))
                    eng.activation(ah[:, p - 1, :], fhf[:, (i - 1) % 2, :], ACT.Copy).then_inc(*act.signals(("ffh", l, half, p - 1)))
                    eng.wait_ge(*act.previous)
                    for m in range(ND):
                        ahead(BLOCK["down", l, half] + 12 * m + 11)
            norm(N_FINAL)

            def job_sq(i, key, raw_):
                eng.activation(sqbuf[i], raw_, ACT.Square).then_inc(*act.signals(("jsq",) + key))
                eng.wait_ge(*act.previous)

            def job_std(i, t, key, n):
                if job_prev[i % 2]:
                    eng.wait_ge(*act.after(*job_prev[i % 2]))
                eng.wait_ge(*act.after("full", t))
                eng.activation(jst[:, i % 2, :], bank(t)[:, :], ACT.Sqrt, bias=bcol[:, 0:1],
                               scale=1.0 / n).then_inc(*act.signals(("read", t), ("jstd",) + key))
                eng.wait_ge(*act.previous)
                job_prev[i % 2] = ("jend",) + key

            def job_swap(key, buf):
                eng.wait_ge(*act.after("jn", *key))
                for g in range(4):
                    o = g ^ 1
                    ins = eng.activation(swap2[32 * g:32 * g + 32, :], buf[32 * o:32 * o + 32, :], ACT.Copy)
                ins.then_inc(*act.signals(("jswap",) + key))
                eng.wait_ge(*act.previous)

            job_prev = [None, None]
            for l in range(DEPTH):
                n1 = N_SECOND + 2 * l
                if l == 0:
                    eng.wait_ge(*act.after("x", N_SECOND, 0))
                    eng.wait_ge(*act.after("full", TILE["down", 1, 1] + ND - 1))
                else:
                    eng.wait_ge(*act.after("full", TILE["down2", 0, 1] + ND - 1))
                eng.dma_start(memf[:, :, :], A["mem"]).then_inc(sems["mem_in"], 16)
                if l == 1:
                    eng.wait_ge(*act.after("jend", "pe2", 0, HEADS2 - 2))
                eng.dma_start(tabc[:, :], A["tab"][l, 0]).then_inc(sems["tab_in"], 16)
                eng.dma_start(tabs[:, :], A["tab"][l, 1]).then_inc(sems["tab_in"], 16)
                eng.wait_ge(*act.after("mem_in", l))
                for c in range(ND):
                    if c >= 2:
                        eng.wait_ge(*act.after("msqmm", l, c - 2))
                    eng.activation(msq[:, c % 2, :], memf[:, c, :], ACT.Square).then_inc(*act.signals(("msq", l, c)))
                    eng.wait_ge(*act.previous)
                t = TILE["memnorm", l]
                eng.wait_ge(*act.after("full", t))
                eng.activation(mri[:, :], bank(t)[:, 0:MEM], ACT.Sqrt, bias=bcol[:, 0:1], scale=1.0 / D).then_inc(*act.signals(("read", t), ("mrms", l)))
                eng.wait_ge(*act.previous)
                for c in range(ND):
                    eng.wait_ge(*act.after("memn", l, c))
                    eng.activation(memh[:, c, :], memf[:, c, :], ACT.Copy).then_inc(*act.signals(("memh", l, c)))
                    eng.wait_ge(*act.previous)
                for m in range(MEM_HEADS):
                    ahead(BLOCK["memk", l] + 8 * m + 7)
                    t = TILE["memk", l] + m
                    eng.wait_ge(*act.after("full", t))
                    eng.activation(kraw[:, m // 2, MEM * (m % 2):MEM * (m % 2) + MEM], bank(t)[:, 0:MEM], ACT.Copy).then_inc(*act.signals(("read", t), ("kraw", l, m)))
                    eng.wait_ge(*act.previous)
                    if m % 2:
                        eng.activation(ksq[:, m // 2, :], kraw[:, m // 2, :], ACT.Square).then_inc(*act.signals(("ksq", l, m // 2)))
                        eng.wait_ge(*act.previous)
                ahead(BLOCK["memv", l] + SLOT - 1)
                ahead(BLOCK["memv", l] + 31)
                for i in range(NMEM):
                    read(TILE["memv", l] + i, vmem[:, i, :], ACT.Copy, ("vmem", l, i))
                for i in range(2):
                    read(TILE["memkst", l] + i, kst[:, i, :], ACT.Sqrt, ("kst", l, i), bias=bcol[:, 0:1], scale=1.0 / P)
                norm(n1)
                if l == 0:
                    for c in range(NQR + NKV):
                        ahead(BLOCK["cq", l] + ND * c + ND - 1)
                        read(TILE["cq", l] + c, cqr[:, c, :], ACT.Copy, ("craw", l, c))
                    ahead(BLOCK["kpe", l] + ND - 1)
                    read(TILE["kpe", l], kpe[:, :], ACT.Copy, ("kperaw", l))
                    job_sq(0, (l, "kpe"), kpe[:, :])
                    for m in range(4):
                        ahead(BLOCK["qmem", l] + ND * m + ND - 1)
                        read(TILE["qmem", l] + m, qmem[:, m, :], ACT.Copy, ("qmemraw", l, m))
                    for c in range(NQR + NKV):
                        if c >= 2:
                            eng.wait_ge(*act.after("csqmm", l, c - 2))
                        eng.activation(cqs[:, c % 2, :], cqr[:, c, :], ACT.Square).then_inc(*act.signals(("csq", l, c)))
                        eng.wait_ge(*act.previous)
                    for i, (name, n) in enumerate((("cqst", QR), ("ckvst", KVR))):
                        read(TILE[name, l], cqi[:, i, :], ACT.Sqrt, ("cstd", l, i), bias=bcol[:, 0:1], scale=1.0 / n)
                    for c in range(NQR + NKV):
                        if c == 0:
                            eng.wait_ge(*act.after("full", TILE["qmem", l] + 3))
                        eng.wait_ge(*act.after("clat", l, c))
                        eng.activation(hh[:, c, :], cqf[:, c % 2, :], ACT.Copy).then_inc(*act.signals(("lath", l, c)))
                        eng.wait_ge(*act.previous)
                    job_std(0, TILE["kst", l], ("kpe", l), ROPE)
                    eng.wait_ge(*act.after("tab_in", l))
                    job_swap(("kpe", l), kpe[:, :])
                    ahead(BLOCK["v2", l] + 15)
                    for i in range(8):
                        g, j = i // 4, i % 4
                        read(TILE["v2", l] + i, v2[:, j, g * BR:g * BR + BR], ACT.Copy, *([("v2", l, j)] if g else []))
                else:
                    for m in range(GKV):
                        ahead(BLOCK["kg", l] + ND * m + ND - 1)
                        read(TILE["kg", l] + m, kg[:, m, :], ACT.Copy)
                        job_sq(m, (l, "kg", m), kg[:, m, :])
                    ahead(BLOCK["vg", l] + 15)
                    for i in range(NQ):
                        t = TILE["vg", l] + i
                        eng.wait_ge(*act.after("full", t))
                        eng.activation(vg[:, i, :], bank(t)[:, 0:GKV * P], ACT.Copy).then_inc(*act.signals(("read", t), ("v2", l, i)))
                        eng.wait_ge(*act.previous)
                    for m in range(4):
                        ahead(BLOCK["qmem", l] + ND * m + ND - 1)
                        read(TILE["qmem", l] + m, qmem[:, m, :], ACT.Copy, ("qmemraw", l, m))
                    eng.wait_ge(*act.after("tab_in", l))
                    for m in range(GKV):
                        job_std(m, TILE["kst", l] + m, ("kg", l, m), P)
                        job_swap(("kg", l, m), kg[:, m, :])

                def prep_a(u):
                    js = jobs(l, u)
                    if u < MEM_HEADS:
                        job_sq(0, js[0][0], js[0][1])
                        return
                    b = BLOCK["pa", l, u]
                    h = u - MEM_HEADS
                    for i, (kind, n) in enumerate(prep_tiles(l, u)):
                        b += n
                        ahead(b - 1)
                        if h >= 2:
                            eng.wait_ge(*act.after("full", score_tile2(l, u - 2, NQ - 1)))
                        read(TILE["pa", l, u] + i, js[i][1], ACT.Copy)
                        job_sq(i, js[i][0], js[i][1])

                def prep_std(u, part):
                    for i, (key, buf, one, n, gain, turns) in enumerate(jobs(l, u)):
                        if i // 2 == part:
                            job_std(i, TILE["pb", l, u] + i, key, n)

                def prep_swap(u):
                    for key, buf, one, n, gain, turns in jobs(l, u):
                        if turns:
                            job_swap(key, buf)

                for u in range(2):
                    prep_a(u)
                    prep_std(u, 0)
                def exp2(u, j):
                    n = MEM if u < MEM_HEADS else S
                    t = score_tile2(l, u, j)
                    eng.wait_ge(*act.after("nmx2", l, u, j))
                    eng.activation(sm2[:, j, 0:n], bank(t)[:, 0:n], ACT.Exp, bias=nmx[:, j:j + 1],
                                   accum_out=rsum[:, j:j + 1]).then_inc(*act.signals(("read", t), ("e2", l, u, j)))
                    eng.wait_ge(*act.previous)

                for j in range(NQ):
                    exp2(0, j)
                for u in range(HEADS2):
                    n = MEM if u < MEM_HEADS else S
                    if u + 2 < HEADS2:
                        prep_a(u + 2)
                    for j in range(NQ):
                        t = turn_tile2(l, u, j)
                        i = 4 * u + j
                        if i >= 3:
                            eng.wait_ge(*act.after("pv2", l, (i - 3) // 4, (i - 3) % 4))
                        eng.wait_ge(*act.after("full", t))
                        eng.activation(pt2[i % 3][:, 0:n], bank(t)[:, 0:n], ACT.Copy).then_inc(*act.signals(("read", t), ("pt2", l, u, j)))
                        eng.wait_ge(*act.previous)
                        if j and u + 1 < HEADS2:
                            exp2(u + 1, j - 1)
                        if 0 < j < 3 and u + 2 < HEADS2:
                            prep_std(u + 2, j - 1)
                    t = out_tile2(l, u)
                    c = (u - MEM_HEADS) % HEADS2
                    eng.wait_ge(*act.after("full", t))
                    eng.activation(ah[:, c, :], bank(t)[:, :], ACT.Copy).then_inc(*act.signals(("mixh", l, u)))
                    eng.wait_ge(*act.previous)
                    if u + 1 < HEADS2:
                        exp2(u + 1, NQ - 1)
                    if u + 2 < HEADS2:
                        prep_swap(u + 2)
                for m in range(ND):
                    ahead(BLOCK["wo2", l] + MIX * m + MIX - 1)
                norm(n1 + 1)
                for half in range(2):
                    for p in range(NFF2 // 2):
                        t, b = TILE["up2", l, half, p], BLOCK["up2", l, half, p]
                        i = half * NFF2 // 2 + p
                        ahead(b + 7)
                        if i >= 2:
                            eng.wait_ge(*act.after("fhf2", l, i - 2))
                        read(t, fga2[:, i % 2, :], ACT.Silu, ("fga2", l, i))
                        ahead(b + 15)
                        if p:
                            eng.wait_ge(*act.after("fhf2", l, i - 1))
                            eng.activation(ah[:, p - 1, :], fhf2[:, (i - 1) % 2, :], ACT.Copy).then_inc(*act.signals(("ffh2", l, half, p - 1)))
                            eng.wait_ge(*act.previous)
                        elif half:
                            eng.wait_ge(*act.after("full", TILE["down2", l, 0] + ND - 1))
                    p = NFF2 // 2
                    i = half * NFF2 // 2 + p
                    eng.wait_ge(*act.after("fhf2", l, i - 1))
                    eng.activation(ah[:, p - 1, :], fhf2[:, (i - 1) % 2, :], ACT.Copy).then_inc(*act.signals(("ffh2", l, half, p - 1)))
                    eng.wait_ge(*act.previous)
                    for m in range(ND):
                        ahead(BLOCK["down2", l, half] + 11 * m + 10)

        @block.vector
        def _(eng):
            dve = Engine("dve", sems, marks, known)
            nxt = [0]
            uid = [0]

            def ahead(b):
                while nxt[0] <= min(b // SLOT + 1, N_SLOTS - 1):
                    s = nxt[0]
                    eng.wait_ge(*dve.after("hi", s))
                    eng.tensor_tensor(wlo[:, s % HALF, :], raw[:, s % RAW, :],
                                               whi[:, s % HALF, :].bitcast(F32), ALU.subtract).then_inc(*dve.signals(("lo", s)))
                    eng.wait_ge(*dve.previous)
                    nxt[0] += 1

            def lo(out, full, hi, *names):
                eng.tensor_tensor(out, full, hi.bitcast(F32), ALU.subtract).then_inc(*dve.signals(*names))
                eng.wait_ge(*dve.previous)

            def norm(n):
                eng.wait_ge(*dve.after("rms", n))
                eng.reciprocal(nri[:, :], nrm[:, :]).then_inc(*dve.signals(("nri", n)))
                eng.wait_ge(*dve.previous)
                last = n == N_FINAL
                for c in range(ND + 1):
                    if c < ND:
                        if last:
                            eng.scalar_tensor_tensor(out=x[:, c, :], in0=x[:, c, :], scalar=norm_gain(n, c),
                                                              in1=nri[:, :], op0=ALU.mult, op1=ALU.mult).then_inc(*dve.signals(("x", N_SECOND, c)))
                            eng.wait_ge(*dve.previous)
                            continue
                        eng.scalar_tensor_tensor(out=nhf[:, c % 2, :], in0=x[:, c, :], scalar=norm_gain(n, c),
                                                          in1=nri[:, :], op0=ALU.mult, op1=ALU.mult).then_inc(*dve.signals(("hf", n, c)))
                        eng.wait_ge(*dve.previous)
                    if c and not last:
                        eng.wait_ge(*dve.after("hh", n, c - 1))
                        lo(hl[:, c - 1, :], nhf[:, (c - 1) % 2, :], hh[:, c - 1, :], ("h", n, c - 1))

            def rope(t, swap, tmp, out, key, *names):
                eng.wait_ge(*dve.after("swap", *key))
                eng.wait_ge(*dve.after("tabc"))
                eng.tensor_tensor(tmp, bank(t)[:, :], tabc[:, :], ALU.mult).then_inc(*dve.signals(("read", t)))
                eng.wait_ge(*dve.previous)
                eng.tensor_tensor(swap, swap, tabs[:, :], ALU.mult).then_inc(*dve.signals())
                eng.wait_ge(*dve.previous)
                eng.tensor_tensor(out, tmp, swap, ALU.add).then_inc(*dve.signals(key, *names))
                eng.wait_ge(*dve.previous)

            def log1p(out, y, t0, t1):
                eng.tensor_scalar(t0, y, 2.0, None, ALU.add).then_inc(*dve.signals())
                eng.wait_ge(*dve.previous)
                eng.reciprocal(t1, t0).then_inc(*dve.signals())
                eng.wait_ge(*dve.previous)
                eng.tensor_tensor(t0, y, t1, ALU.mult).then_inc(*dve.signals())
                eng.wait_ge(*dve.previous)
                eng.tensor_tensor(t1, t0, t0, ALU.mult).then_inc(*dve.signals())
                eng.wait_ge(*dve.previous)
                eng.tensor_scalar(out, t1, 1.0 / 15, None, ALU.mult).then_inc(*dve.signals())
                eng.wait_ge(*dve.previous)
                for n in (13, 11, 9, 7, 5, 3):
                    eng.scalar_tensor_tensor(out=out, in0=out, scalar=1.0 / n, in1=t1, op0=ALU.add, op1=ALU.mult).then_inc(*dve.signals())
                    eng.wait_ge(*dve.previous)
                eng.tensor_scalar(out, out, 1.0, 2.0, ALU.add, ALU.mult).then_inc(*dve.signals())
                eng.wait_ge(*dve.previous)
                eng.tensor_tensor(out, out, t0, ALU.mult).then_inc(*dve.signals())
                eng.wait_ge(*dve.previous)

            def conv(taps, wcol, bcol_, src, dst, n, *names):
                first = 4 - taps
                eng.tensor_scalar(dst, src[:, first:first + S], wcol(0), bcol_, ALU.mult, ALU.add).then_inc(*dve.signals())
                eng.wait_ge(*dve.previous)
                for j in range(1, taps):
                    ins = eng.scalar_tensor_tensor(out=dst, in0=src[:, first + j:first + j + S], scalar=wcol(j),
                                                   in1=dst, op0=ALU.mult, op1=ALU.add)
                    if j < taps - 1:
                        ins.then_inc(*dve.signals())
                        eng.wait_ge(*dve.previous)
                    else:
                        ins.then_inc(*dve.signals(*names))
                        eng.wait_ge(*dve.previous)

            eng.memset(bcol[:, 0:1], EPS).then_inc(*dve.signals(("bcol",)))
            eng.wait_ge(*dve.previous)
            eng.memset(cin[:, :, 0:3], 0.0).then_inc(*dve.signals())
            eng.wait_ge(*dve.previous)
            ahead(0)
            for c in range(ND):
                marks[("x", 0, c)] = (f"x_in{2 * c // ND}", 16)
            eng.wait_ge(*dve.after("par_in"))
            for l in range(DEPTH):
                if l == 0:
                    for name, i, v in (("memq", 0, HD_SCALE), ("memq", 1, HD_SCALE), ("mla_q", 0, MLA_SCALE),
                                       ("mla_qpe", 0, MLA_SCALE), ("gqa_q", 0, HD_SCALE)):
                        c = par[:, PCOL2[name] + i:PCOL2[name] + i + 1]
                        eng.tensor_scalar(c, c, v, None, ALU.mult).then_inc(*dve.signals())
                        eng.wait_ge(*dve.previous)
                    eng.wait_ge(*dve.after("con_in"))
                    for d in range(DEPTH):
                        lam = pcol("rglru_lambda", d, 0, 4)
                        eng.scalar_tensor_tensor(out=spt[:, 0, 4 * d:4 * d + 4], in0=lam, scalar=-1.0, in1=lam,
                                                      op0=ALU.mult, op1=ALU.max).then_inc(*dve.signals(*([("lam_abs",)] if d == DEPTH - 1 else [])))
                        eng.wait_ge(*dve.previous)
                        eng.tensor_scalar(spt[:, 4, 4 * d:4 * d + 4], pcol("rglru_lambda", d, 0, 4), 0.0, -1.0, ALU.min, ALU.mult).then_inc(*dve.signals())
                        eng.wait_ge(*dve.previous)
                    eng.wait_ge(*dve.after("lam_exp"))
                    log1p(spt[:, 5, :], spt[:, 1, :], spt[:, 2, :], spt[:, 3, :])
                    eng.tensor_tensor(spt[:, 5, :], spt[:, 5, :], spt[:, 4, :], ALU.add).then_inc(*dve.signals())
                    eng.wait_ge(*dve.previous)
                    eng.tensor_scalar(sp8[:, :], spt[:, 5, :], 8.0, None, ALU.mult).then_inc(*dve.signals())
                    eng.wait_ge(*dve.previous)
                    eng.tensor_scalar(spt[:, 5, :], spt[:, 5, :], -8.0, None, ALU.mult).then_inc(*dve.signals(("spn",)))
                    eng.wait_ge(*dve.previous)
                    eng.wait_ge(*dve.after("pos_in"))
                    ang = rtab[:, 0, :]
                    eng.tensor_copy(rtab[:, 1, :], pos_i[:, :]).then_inc(*dve.signals())
                    eng.wait_ge(*dve.previous)
                    eng.tensor_scalar(ang, rtab[:, 1, :], con[:, C_INV:C_INV + 1], None, ALU.mult).then_inc(*dve.signals())
                    eng.wait_ge(*dve.previous)
                    two_pi = 2.0 * np.pi
                    c1 = 6.28125
                    c2 = float(np.float32(np.round((two_pi - c1) * 2 ** 21) / 2 ** 21))
                    c3 = float(two_pi - c1 - c2)
                    magic = float(3 << 22)
                    for i, shift in enumerate((0.0, 0.25)):
                        kk, r = rtab[:, 3, :], rtab[:, 2 + 2 * i, :]
                        eng.tensor_scalar(kk, ang, 1.0 / two_pi, shift, ALU.mult, ALU.add).then_inc(*dve.signals())
                        eng.wait_ge(*dve.previous)
                        eng.tensor_scalar(kk, kk, magic, None, ALU.add).then_inc(*dve.signals())
                        eng.wait_ge(*dve.previous)
                        eng.tensor_scalar(kk, kk, -magic, None, ALU.add).then_inc(*dve.signals())
                        eng.wait_ge(*dve.previous)
                        eng.scalar_tensor_tensor(out=r, in0=kk, scalar=-c1, in1=ang, op0=ALU.mult, op1=ALU.add).then_inc(*dve.signals())
                        eng.wait_ge(*dve.previous)
                        eng.scalar_tensor_tensor(out=r, in0=kk, scalar=-c2, in1=r, op0=ALU.mult, op1=ALU.add).then_inc(*dve.signals())
                        eng.wait_ge(*dve.previous)
                        eng.scalar_tensor_tensor(out=r, in0=kk, scalar=-c3, in1=r, op0=ALU.mult, op1=ALU.add).then_inc(*dve.signals())
                        eng.wait_ge(*dve.previous)
                        if i:
                            eng.tensor_scalar(r, r, float(np.pi / 2), None, ALU.add).then_inc(*dve.signals())
                            eng.wait_ge(*dve.previous)
                        pi = float(np.nextafter(np.float32(np.pi), np.float32(0)))
                        eng.tensor_scalar(r, r, pi, -pi, ALU.min, ALU.max).then_inc(*dve.signals(("ang", i)))
                        eng.wait_ge(*dve.previous)
                norm(2 * l)
                if l == 0:
                    eng.wait_ge(*dve.after("sin"))
                    eng.tensor_scalar(tabs[:, :], tabs[:, :], con[:, C_SGN:C_SGN + 1], None, ALU.mult).then_inc(*dve.signals())
                    eng.wait_ge(*dve.previous)
                for m in range(4):
                    ahead(BLOCK["qi", l] + 8 * m + 7)
                    rope(TILE["qi", l] + m, rsw[:, m % 2, :], rt1[:, m % 2, :], qi[:, m, :], ("qi", l, m))
                ahead(BLOCK["ki", l] + 7)
                rope(TILE["ki", l], rsw[:, 0, :], rt1[:, 0, :], ki[:, :], ("ki", l))
                ahead(BLOCK["if", l] + 7)
                eng.wait_ge(*dve.after("if", l))
                R = lambda i: rows[i][:, :]
                eng.tensor_scalar(R(1), R(1), par[0:4, l * PLAYER + PCOL["f_bias"]:l * PLAYER + PCOL["f_bias"] + 1], None, ALU.add).then_inc(*dve.signals())
                eng.wait_ge(*dve.previous)
                eng.scalar_tensor_tensor(out=R(2), in0=R(1), scalar=-1.0, in1=R(1), op0=ALU.mult, op1=ALU.max).then_inc(*dve.signals(("fabs", l)))
                eng.wait_ge(*dve.previous)
                eng.tensor_scalar(R(1), R(1), 0.0, None, ALU.min).then_inc(*dve.signals())
                eng.wait_ge(*dve.previous)
                eng.wait_ge(*dve.after("fexp", l))
                log1p(R(2), R(3), R(4), R(5))
                eng.tensor_tensor(R(1), R(1), R(2), ALU.subtract).then_inc(*dve.signals())
                eng.wait_ge(*dve.previous)
                eng.memset(R(4), 1.0).then_inc(*dve.signals())
                eng.wait_ge(*dve.previous)
                eng.tensor_tensor_scan(R(2), R(4), R(1), 0.0, ALU.mult, ALU.add).then_inc(*dve.signals())
                eng.wait_ge(*dve.previous)
                eng.tensor_tensor(R(0), R(0), R(2), ALU.subtract).then_inc(*dve.signals(("arow", l)))
                eng.wait_ge(*dve.previous)
                eng.memset(R(4), 0.0).then_inc(*dve.signals())
                eng.wait_ge(*dve.previous)
                eng.tensor_tensor_scan(R(3), R(4), R(0), 0.0, ALU.add, ALU.max).then_inc(*dve.signals())
                eng.wait_ge(*dve.previous)
                eng.tensor_scalar(negm[:, :], R(3), -1.0, None, ALU.mult).then_inc(*dve.signals(("negm", l)))
                eng.wait_ge(*dve.previous)
                eng.scalar_tensor_tensor(out=negg[:, :], in0=R(2), scalar=-1.0, in1=R(3),
                                              op0=ALU.mult, op1=ALU.subtract).then_inc(*dve.signals(("negg", l)))
                eng.wait_ge(*dve.previous)
                eng.wait_ge(*dve.after("wcol", l))
                i = 0
                for j in range(3, 0, -1):
                    w = work[:, j - 1, 0:P * (j + 1)]
                    for h in range(A_HEADS):
                        eng.wait_ge(*dve.after("relu", l, i))
                        src = relu[:, i % 2, 0:P * (j + 1)]
                        ws = wcol[:, j, h:h + 1]
                        if h == 0:
                            eng.tensor_scalar(w, src, ws, None, ALU.mult).then_inc(*dve.signals(("acc", l, i)))
                            eng.wait_ge(*dve.previous)
                        else:
                            eng.scalar_tensor_tensor(out=w, in0=src, scalar=ws, in1=w, op0=ALU.mult, op1=ALU.add).then_inc(*dve.signals(("acc", l, i)))
                            eng.wait_ge(*dve.previous)
                        i += 1
                    d = work[:, j - 1, P * j:P * j + P]
                    eng.scalar_tensor_tensor(out=d, in0=mask_qk, scalar=float(UNSEEN / NEG), in1=d,
                                                  op0=ALU.mult, op1=ALU.add).then_inc(*dve.signals())
                    eng.wait_ge(*dve.previous)

                rounds = [(j, r) for j in (3, 2, 1) for r in range(TOPK // 8)]

                def select(n):
                    for _ in range(n):
                        if not rounds:
                            return
                        j, r = rounds.pop(0)
                        w, t8 = work[:, j - 1, 0:P * (j + 1)], top[:, j - 1, :]
                        eng.max(t8, w).then_inc(*dve.signals())
                        eng.wait_ge(*dve.previous)
                        eng.match_replace(w, t8, w, TAKEN).then_inc(*dve.signals())
                        eng.wait_ge(*dve.previous)
                        if r == TOPK // 8 - 1:
                            eng.tensor_scalar(w, w, 0.5 * (UNSEEN + TAKEN), NEG, ALU.is_gt, ALU.mult).then_inc(*dve.signals())
                            eng.wait_ge(*dve.previous)

                for m in range(8):
                    ahead(BLOCK["mqk", l] + 8 * m + 7)
                    eng.wait_ge(*dve.after("cin", l, m))
                    if m >= 2:
                        eng.wait_ge(*dve.after("mqk", l, m - 2))
                    conv(4, lambda j: pcol("mlstm_conv_w", l, 8 * j + m), pcol("mlstm_conv_b", l, m),
                         cin[:, m % 2, :], cacc[:, m % 2, :], m, ("conv", l, m))
                    select(2)
                ahead(BLOCK["mv", l] + 31 - SLOT)
                select(8)
                ahead(BLOCK["mv", l] + 31)
                select(4)
                def m_masked(h):
                    eng.wait_ge(*dve.after("mnm", l, h))
                    eng.tensor_tensor(mdm[:, :, :], mnm[:, :].rearrange("p (a b) -> p a b", b=P),
                                           mask_st.unsqueeze(1).to_broadcast([P, NQ, P]), ALU.add).then_inc(*dve.signals(("mdm", l, h)))
                    eng.wait_ge(*dve.previous)

                m_masked(0)
                for h in range(M_HEADS):
                    t = TILE["m1", l, h] + 2
                    for j in range(NQ):
                        eng.wait_ge(*dve.after("mwx", l, h, j))
                        eng.wait_ge(*dve.after("full", t + j))
                        eng.scalar_tensor_tensor(out=mp[:, j, P * j:], in0=bank(t + j)[:, P * j:], scalar=M_SCALE,
                                                          in1=mwx[:, j % 2, P * j:], op0=ALU.mult, op1=ALU.mult).then_inc(*dve.signals(("read", t + j), ("mp", l, h, j)))
                        eng.wait_ge(*dve.previous)
                    ahead(BLOCK["rx", l, h] + 7)
                    ahead(BLOCK["mo", l, h] + 7)
                    t = TILE["m2", l, h]
                    eng.wait_ge(*dve.after("full", t + 1))
                    ahead(BLOCK["ak", l, h] + 7)
                    eng.wait_ge(*dve.after("mex", l, h))
                    eng.scalar_tensor_tensor(out=mdn[:, :], in0=bank(t + 1)[:, :], scalar=-1.0, in1=mex[:, :],
                                                  op0=ALU.mult, op1=ALU.max).then_inc(*dve.signals())
                    eng.wait_ge(*dve.previous)
                    eng.tensor_tensor(mdn[:, :], bank(t + 1)[:, :], mdn[:, :], ALU.max).then_inc(*dve.signals(("read", t + 1)))
                    eng.wait_ge(*dve.previous)
                    eng.reciprocal(mdn[:, :], mdn[:, :]).then_inc(*dve.signals())
                    eng.wait_ge(*dve.previous)
                    eng.wait_ge(*dve.after("full", t))
                    eng.tensor_tensor(mq[:, h, :], bank(t)[:, :], mdn[:, :], ALU.mult).then_inc(*dve.signals(("read", t), ("mh", l, h)))
                    eng.wait_ge(*dve.previous)
                    eng.wait_ge(*dve.after("rcin", l, h))
                    conv(4, lambda j: pcol("rglru_conv_w", l, 4 * j + h), pcol("rglru_conv_b", l, h),
                         cin[:, h % 2, :], xc[:, h, :], h, ("xc", l, h))
                    t = TILE["m3", l, h]
                    eng.wait_ge(*dve.after("full", t))
                    eng.scalar_tensor_tensor(out=mq[:, h, :], in0=bank(t)[:, :], scalar=-1.0 / P, in1=mq[:, h, :],
                                                  op0=ALU.mult, op1=ALU.add).then_inc(*dve.signals(("read", t), ("mhc", l, h)))
                    eng.wait_ge(*dve.previous)
                    rope(TILE["ak", l, h], aswap[:, :], atmp[:, :], ak[:, h, :], ("ak", l, h))
                    if h + 1 < M_HEADS:
                        m_masked(h + 1)
                    eng.wait_ge(*dve.after("mstd", l, h))
                    eng.reciprocal(mdn[:, :], mdn[:, :]).then_inc(*dve.signals())
                    eng.wait_ge(*dve.previous)
                    eng.scalar_tensor_tensor(out=mq[:, h, :], in0=mq[:, h, :], scalar=pcol("mlstm_norm", l, h),
                                                  in1=mdn[:, :], op0=ALU.mult, op1=ALU.mult).then_inc(*dve.signals())
                    eng.wait_ge(*dve.previous)
                    eng.wait_ge(*dve.after("mo", l, h))
                    eng.tensor_tensor(yf[:, h, :], mq[:, h, :], mo[:, :], ALU.mult).then_inc(*dve.signals(("yf", l, 0, h)))
                    eng.wait_ge(*dve.previous)
                    eng.wait_ge(*dve.after("yh", l, 0, h))
                    lo(al[:, h, :], yf[:, h, :], ah[:, h, :], ("y", l, 0, h), ("msplit", l, h))
                for c in range(NBR):
                    ahead(BLOCK["rg", l, c] + 7)
                    eng.wait_ge(*dve.after("rth", l, c))
                    eng.tensor_scalar(rt[:, 4, :], rt[:, 2, :], 1.0, None, ALU.add).then_inc(*dve.signals())
                    eng.wait_ge(*dve.previous)
                    eng.reciprocal(rt[:, 5, :], rt[:, 4, :]).then_inc(*dve.signals())
                    eng.wait_ge(*dve.previous)
                    eng.tensor_tensor(rt[:, 4, :], rt[:, 2, :], rt[:, 5, :], ALU.mult).then_inc(*dve.signals(("rq", l, c)))
                    eng.wait_ge(*dve.previous)
                    eng.wait_ge(*dve.after("ri", l, c))
                    eng.tensor_tensor(rt[:, 1, :], rt[:, 1, :], xc[:, c, :], ALU.mult).then_inc(*dve.signals())
                    eng.wait_ge(*dve.previous)
                    eng.wait_ge(*dve.after("rs", l, c))
                    eng.tensor_tensor(rt[:, 1, :], rt[:, 1, :], rt[:, 5, :], ALU.mult).then_inc(*dve.signals())
                    eng.wait_ge(*dve.previous)
                    eng.wait_ge(*dve.after("ra", l, c))
                    eng.tensor_tensor_scan(rt[:, 0, :], rt[:, 3, :], rt[:, 1, :], 0.0, ALU.mult, ALU.add).then_inc(*dve.signals())
                    eng.wait_ge(*dve.previous)
                    eng.wait_ge(*dve.after("rg", l, c))
                    eng.tensor_tensor(yf[:, c, :], rt[:, 0, :], rg[:, c, :], ALU.mult).then_inc(*dve.signals(("yf", l, 1, c), ("rgdone", l, c)))
                    eng.wait_ge(*dve.previous)
                    ahead(BLOCK["aq", l, c] + 7)
                    rope(TILE["aq", l, c], rsw2[:, c % 2, :], cacc[:, c % 2, :], aq[:, c, :], ("aq", l, c))
                ahead(BLOCK["av", l] + 31 - SLOT)
                ahead(BLOCK["av", l] + 31)

                def branch(b, m):
                    t, blk = TILE["br", l, b, m], BLOCK["br", l, b, m]
                    ahead(blk + 7)
                    ahead(blk + 11)
                    eng.wait_ge(*dve.after("sig", l, b, m))
                    eng.wait_ge(*dve.after("full", t + 1))
                    if b == 0:
                        eng.tensor_tensor(mer[:, m, :], bank(t + 1)[:, :], sig[:, :], ALU.mult).then_inc(*dve.signals(("read", t + 1), ("merged", l, b, m)))
                        eng.wait_ge(*dve.previous)
                    else:
                        eng.tensor_tensor(cacc[:, 0, :], bank(t + 1)[:, :], sig[:, :], ALU.mult).then_inc(*dve.signals(("read", t + 1), ("merged", l, b, m)))
                        eng.wait_ge(*dve.previous)
                        eng.tensor_tensor(mer[:, m, :], mer[:, m, :], cacc[:, 0, :], ALU.add).then_inc(*dve.signals())
                        eng.wait_ge(*dve.previous)

                def split_y(b):
                    for k in range(4):
                        eng.wait_ge(*dve.after("yh", l, b, k))
                        lo(al[:, k, :], yf[:, k, :], ah[:, k, :], ("y", l, b, k))

                def masked(h, j):
                    t = score_tile(l, h, j)
                    eng.wait_ge(*dve.after("full", t))
                    if h:
                        eng.wait_ge(*dve.after("turned", l, h - 1, j))
                    m = mask_qk if j == 0 else work[:, j - 1, 0:P * (j + 1)]
                    eng.tensor_tensor_reduce(sm[:, j, 0:P * (j + 1)], bank(t)[:, 0:P * (j + 1)], m, -A_SCALE,
                                                      3.0e38, ALU.add, ALU.min, nmx[:, j:j + 1]).then_inc(*dve.signals(("read", t), ("sm", l, h, j)))
                    eng.wait_ge(*dve.previous)

                def normed(h, j):
                    eng.wait_ge(*dve.after("e", l, h, j))
                    eng.reciprocal(rinv[:, j:j + 1], rsum[:, j:j + 1]).then_inc(*dve.signals())
                    eng.wait_ge(*dve.previous)
                    eng.tensor_scalar(sm[:, j, 0:P * (j + 1)], sm[:, j, 0:P * (j + 1)], rinv[:, j:j + 1],
                                               None, ALU.mult).then_inc(*dve.signals(("p", l, h, j)))
                    eng.wait_ge(*dve.previous)

                for m in range(ND):
                    branch(0, m)
                    select(3)
                select(48)
                split_y(1)
                for j in range(NQ):
                    masked(0, j)
                for j in range(NQ):
                    normed(0, j)
                for h in range(A_HEADS):
                    branch(1, h)
                    if h + 1 < A_HEADS:
                        for j in range(NQ):
                            masked(h + 1, j)
                            if j:
                                normed(h + 1, j - 1)
                        normed(h + 1, NQ - 1)
                for m in range(ND):
                    ahead(BLOCK["gc", l] + 8 * m + 7)
                split_y(2)
                for m in range(ND):
                    ahead(BLOCK["bc", l] + 4 * m + 3)
                    t = TILE["bc", l] + m
                    eng.wait_ge(*dve.after("sigc", l, m))
                    eng.wait_ge(*dve.after("full", t))
                    eng.tensor_tensor(sigc[:, m, :], bank(t)[:, :], sigc[:, m, :], ALU.mult).then_inc(*dve.signals(("read", t)))
                    eng.wait_ge(*dve.previous)
                    eng.tensor_tensor(mer[:, m, :], mer[:, m, :], sigc[:, m, :], ALU.add).then_inc(*dve.signals(("merf", l, m)))
                    eng.wait_ge(*dve.previous)
                    if m:
                        eng.wait_ge(*dve.after("merh", l, m - 1))
                        lo(hl[:, m - 1, :], mer[:, m - 1, :], hh[:, m - 1, :], ("mer", l, m - 1))
                eng.wait_ge(*dve.after("merh", l, ND - 1))
                lo(hl[:, ND - 1, :], mer[:, ND - 1, :], hh[:, ND - 1, :], ("mer", l, ND - 1))
                for m in range(ND):
                    ahead(BLOCK["wo", l] + 8 * m + 7)
                    t = TILE["wo", l] + m
                    eng.wait_ge(*dve.after("full", t))
                    eng.tensor_tensor(x[:, m, :], x[:, m, :], bank(t)[:, :], ALU.add).then_inc(*dve.signals(("read", t), ("x", 2 * l + 1, m)))
                    eng.wait_ge(*dve.previous)
                norm(2 * l + 1)
                for half in range(2):
                    for p in range(NFF // 2):
                        t, b = TILE["up", l, half, p], BLOCK["up", l, half, p]
                        i = half * NFF // 2 + p
                        ahead(b + 7)
                        eng.wait_ge(*dve.after("fcin", l, i))
                        if i >= 2:
                            eng.wait_ge(*dve.after("fga", l, i - 2))
                        conv(3, lambda j: pcol("ffn_conv_w", l, NFF * j + i), pcol("ffn_conv_b", l, i),
                             cin[:, i % 2, :], cacc[:, i % 2, :], i, ("fconv", l, i))
                        ahead(b + 15)
                        if p:
                            eng.wait_ge(*dve.after("ffh", l, half, p - 1))
                            lo(al[:, p - 1, :], fhf[:, (i - 1) % 2, :], ah[:, p - 1, :], ("ff", l, half, p - 1))
                        eng.wait_ge(*dve.after("fga", l, i))
                        eng.wait_ge(*dve.after("full", t + 1))
                        eng.tensor_tensor(fhf[:, i % 2, :], fga[:, i % 2, :], bank(t + 1)[:, :], ALU.mult).then_inc(*dve.signals(("read", t + 1), ("fhf", l, i)))
                        eng.wait_ge(*dve.previous)
                    p = NFF // 2
                    i = half * NFF // 2 + p
                    eng.wait_ge(*dve.after("ffh", l, half, p - 1))
                    lo(al[:, p - 1, :], fhf[:, (i - 1) % 2, :], ah[:, p - 1, :], ("ff", l, half, p - 1))
                    for m in range(ND):
                        ahead(BLOCK["down", l, half] + 12 * m + 11)
                        t = TILE["down", l, half] + m
                        eng.wait_ge(*dve.after("full", t))
                        eng.tensor_tensor(x[:, m, :], x[:, m, :], bank(t)[:, :], ALU.add).then_inc(*dve.signals(("read", t), ("x" if half else "xhalf", 2 * l + 2, m)))
                        eng.wait_ge(*dve.previous)
            norm(N_FINAL)

            def job(i, key, buf, gain, turns):
                r = jst[:, i % 2, :]
                eng.wait_ge(*dve.after("jstd", *key))
                eng.reciprocal(r, r).then_inc(*dve.signals())
                eng.wait_ge(*dve.previous)
                eng.scalar_tensor_tensor(out=buf, in0=buf, scalar=gain, in1=r, op0=ALU.mult,
                                         op1=ALU.mult).then_inc(*dve.signals(("jn",) + key, *([] if turns else [("jend",) + key, key])))
                eng.wait_ge(*dve.previous)

            def job_turn(i, key, buf):
                r = jst[:, i % 2, :]
                eng.wait_ge(*dve.after("jswap", *key))
                eng.tensor_tensor(r, swap2, tabs[:, :], ALU.mult).then_inc(*dve.signals())
                eng.wait_ge(*dve.previous)
                eng.tensor_tensor(buf, buf, tabc[:, :], ALU.mult).then_inc(*dve.signals())
                eng.wait_ge(*dve.previous)
                eng.tensor_tensor(buf, buf, r, ALU.add).then_inc(*dve.signals(("jend",) + key, key))
                eng.wait_ge(*dve.previous)

            for l in range(DEPTH):
                n1 = N_SECOND + 2 * l
                g = lambda name, i=0: par[:, PCOL2[name] + i:PCOL2[name] + i + 1]
                eng.wait_ge(*dve.after("mrms", l))
                eng.reciprocal(mri[:, :], mri[:, :]).then_inc(*dve.signals())
                eng.wait_ge(*dve.previous)
                for c in range(ND):
                    eng.scalar_tensor_tensor(out=memf[:, c, :], in0=memf[:, c, :], scalar=g("mem_norm", c),
                                                  in1=mri[:, :], op0=ALU.mult, op1=ALU.mult).then_inc(*dve.signals(("memn", l, c)))
                    eng.wait_ge(*dve.previous)
                    if c:
                        eng.wait_ge(*dve.after("memh", l, c - 1))
                        lo(meml[:, c - 1, :], memf[:, c - 1, :], memh[:, c - 1, :], ("mem", l, c - 1))
                eng.wait_ge(*dve.after("memh", l, ND - 1))
                lo(meml[:, ND - 1, :], memf[:, ND - 1, :], memh[:, ND - 1, :], ("mem", l, ND - 1))
                for m in range(MEM_HEADS):
                    ahead(BLOCK["memk", l] + 8 * m + 7)
                ahead(BLOCK["memv", l] + SLOT - 1)
                ahead(BLOCK["memv", l] + 31)
                for i in range(2):
                    eng.wait_ge(*dve.after("kst", l, i))
                    eng.reciprocal(kst[:, i, :], kst[:, i, :]).then_inc(*dve.signals())
                    eng.wait_ge(*dve.previous)
                    eng.scalar_tensor_tensor(out=kmem[:, 2 * i:2 * i + 2, :].rearrange("p a b -> p (a b)"),
                                                  in0=kraw[:, i, :], scalar=g("memk", l), in1=kst[:, i, :],
                                                  op0=ALU.mult, op1=ALU.mult).then_inc(*dve.signals(*([("kmem", l)] if i else [])))
                    eng.wait_ge(*dve.previous)
                norm(n1)
                if l == 0:
                    for c in range(NQR + NKV):
                        ahead(BLOCK["cq", l] + ND * c + ND - 1)
                    ahead(BLOCK["kpe", l] + ND - 1)
                    for m in range(4):
                        ahead(BLOCK["qmem", l] + ND * m + ND - 1)
                    for i in range(2):
                        eng.wait_ge(*dve.after("cstd", l, i))
                        eng.reciprocal(cqi[:, i, :], cqi[:, i, :]).then_inc(*dve.signals())
                        eng.wait_ge(*dve.previous)
                    for c in range(NQR + NKV):
                        eng.scalar_tensor_tensor(out=cqf[:, c % 2, :], in0=cqr[:, c, :],
                                                      scalar=g("q_a", c) if c < NQR else g("kv_a", c - NQR),
                                                      in1=cqi[:, int(c >= NQR), :], op0=ALU.mult, op1=ALU.mult).then_inc(*dve.signals(("clat", l, c)))
                        eng.wait_ge(*dve.previous)
                        eng.wait_ge(*dve.after("lath", l, c))
                        lo(hl[:, c, :], cqf[:, c % 2, :], hh[:, c, :], ("lat", l, c))
                    job(0, ("kpe", l), kpe[:, :], g("mla_kpe"), True)
                    job_turn(0, ("kpe", l), kpe[:, :])
                    ahead(BLOCK["v2", l] + 15)
                else:
                    for m in range(GKV):
                        ahead(BLOCK["kg", l] + ND * m + ND - 1)
                    ahead(BLOCK["vg", l] + 15)
                    for m in range(4):
                        ahead(BLOCK["qmem", l] + ND * m + ND - 1)
                    for m in range(GKV):
                        job(m, ("kg", l, m), kg[:, m, :], g("gqa_k"), True)
                        job_turn(m, ("kg", l, m), kg[:, m, :])

                def prep_a(u):
                    if u >= MEM_HEADS:
                        b = BLOCK["pa", l, u]
                        for kind, n in prep_tiles(l, u):
                            b += n
                            ahead(b - 1)

                def prep_norm(u, part):
                    for i, (key, buf, one, n, gain, turns) in enumerate(jobs(l, u)):
                        if i // 2 == part:
                            job(i, key, buf, gain, turns)

                def prep_turn(u):
                    for i, (key, buf, one, n, gain, turns) in enumerate(jobs(l, u)):
                        if turns:
                            job_turn(i, key, buf)

                for u in range(2):
                    prep_norm(u, 0)

                def peak(u, j):
                    n = MEM if u < MEM_HEADS else S
                    t = score_tile2(l, u, j)
                    eng.wait_ge(*dve.after("full", t))
                    if u:
                        eng.wait_ge(*dve.after("turned2", l, u - 1, j))
                    eng.tensor_reduce(nmx[:, j:j + 1], bank(t)[:, 0:n], AX, ALU.max, negate=True).then_inc(*dve.signals(("nmx2", l, u, j)))
                    eng.wait_ge(*dve.previous)

                def normed2(u, j):
                    n = MEM if u < MEM_HEADS else S
                    eng.wait_ge(*dve.after("e2", l, u, j))
                    eng.reciprocal(rinv[:, j:j + 1], rsum[:, j:j + 1]).then_inc(*dve.signals())
                    eng.wait_ge(*dve.previous)
                    eng.tensor_scalar(sm2[:, j, 0:n], sm2[:, j, 0:n], rinv[:, j:j + 1], None,
                                      ALU.mult).then_inc(*dve.signals(("p2", l, u, j)))
                    eng.wait_ge(*dve.previous)

                for j in range(NQ):
                    peak(0, j)
                for j in range(NQ):
                    normed2(0, j)
                for u in range(HEADS2):
                    if u + 2 < HEADS2:
                        prep_a(u + 2)
                    for j in range(NQ):
                        if u + 1 < HEADS2:
                            peak(u + 1, j)
                            if j:
                                normed2(u + 1, j - 1)
                        if 0 < j < 3 and u + 2 < HEADS2:
                            prep_norm(u + 2, j - 1)
                    t = out_tile2(l, u)
                    c = (u - MEM_HEADS) % HEADS2
                    eng.wait_ge(*dve.after("mixh", l, u))
                    eng.tensor_tensor(al[:, c, :], bank(t)[:, :], ah[:, c, :].bitcast(F32), ALU.subtract).then_inc(*dve.signals(("read", t), ("mix", l, u)))
                    eng.wait_ge(*dve.previous)
                    if u + 1 < HEADS2:
                        normed2(u + 1, NQ - 1)
                    if u + 2 < HEADS2:
                        prep_turn(u + 2)
                for m in range(ND):
                    ahead(BLOCK["wo2", l] + MIX * m + MIX - 1)
                    t = TILE["wo2", l] + m
                    eng.wait_ge(*dve.after("full", t))
                    eng.tensor_tensor(x[:, m, :], x[:, m, :], bank(t)[:, :], ALU.add).then_inc(*dve.signals(("read", t), ("x", n1 + 1, m)))
                    eng.wait_ge(*dve.previous)
                norm(n1 + 1)
                for half in range(2):
                    for p in range(NFF2 // 2):
                        t, b = TILE["up2", l, half, p], BLOCK["up2", l, half, p]
                        i = half * NFF2 // 2 + p
                        ahead(b + 7)
                        ahead(b + 15)
                        if p:
                            eng.wait_ge(*dve.after("ffh2", l, half, p - 1))
                            lo(al[:, p - 1, :], fhf2[:, (i - 1) % 2, :], ah[:, p - 1, :], ("ff2", l, half, p - 1))
                        eng.wait_ge(*dve.after("fga2", l, i))
                        eng.wait_ge(*dve.after("full", t + 1))
                        eng.tensor_tensor(fhf2[:, i % 2, :], fga2[:, i % 2, :], bank(t + 1)[:, :], ALU.mult).then_inc(*dve.signals(("read", t + 1), ("fhf2", l, i)))
                        eng.wait_ge(*dve.previous)
                    p = NFF2 // 2
                    i = half * NFF2 // 2 + p
                    eng.wait_ge(*dve.after("ffh2", l, half, p - 1))
                    lo(al[:, p - 1, :], fhf2[:, (i - 1) % 2, :], ah[:, p - 1, :], ("ff2", l, half, p - 1))
                    for m in range(ND):
                        ahead(BLOCK["down2", l, half] + 11 * m + 10)
                        t = TILE["down2", l, half] + m
                        eng.wait_ge(*dve.after("full", t))
                        names = [("read", t)]
                        if half:
                            names.append(("out", m) if l else ("x", N_SECOND + 2, m))
                        eng.tensor_tensor(x[:, m, :], x[:, m, :], bank(t)[:, :], ALU.add).then_inc(*dve.signals(*names))
                        eng.wait_ge(*dve.previous)

    return marks


def kernel(**inputs):
    import concourse.bacc as bacc
    from concourse.bass_utils import run_bass_kernel_spmd

    w = {name: np.asarray(a) for name, a in inputs.items()}
    arrays = {
        "x": np.ascontiguousarray(w["x"][0].T.reshape(ND, P, S).transpose(1, 0, 2)),
        "mem": np.ascontiguousarray(w["mem_2"][0].T.reshape(ND, P, MEM).transpose(1, 0, 2)),
        "pos": np.ascontiguousarray(w["positions"].astype(np.int32)),
        "w": pack_weights(w), "par": pack_params(w), "rgw": pack_rglru(w), "con": constants(), "tab": axial_tables(),
    }
    known = None
    for _ in range(2):
        nc = bacc.Bacc("TRN2", target_bir_lowering=False, num_devices=1, dynamic_dma_scratch_size=1024)
        args = {n: nc.dram_tensor(f"in_{n}", a.shape, mybir.dt.from_np(a.dtype), kind="ExternalInput").ap()
                for n, a in arrays.items()}
        args["out"] = nc.dram_tensor("out", (P, ND, S), F32, kind="ExternalOutput").ap()
        known = build(nc, args, known)
    r = run_bass_kernel_spmd(nc, [{f"in_{n}": a for n, a in arrays.items()}], core_ids=[0])
    out = r.results[0]["out"]
    return np.ascontiguousarray(out.transpose(1, 0, 2).reshape(D, S).T)[None]
```

```python
from contextlib import ExitStack

import numpy as np

import concourse.bass as bass
from concourse import mybir

F32 = mybir.dt.float32
F32R = mybir.dt.float32r
I32 = mybir.dt.int32
ALU = mybir.AluOpType
ACT = mybir.ActivationFunctionType
AX = mybir.AxisListType.X

P = 128
S = 512
D = 1024
ND = D // P
DEPTH = 2
EPS = 1e-6
BR = 512
NBR = BR // P
M_HEADS = 4
A_HEADS = 8
HD = 64
FF = 3 * D
NFF = FF // P
TOPK = 128
NQ = S // P
NEG = -1e30
UNSEEN = -3.0e38
TAKEN = -3.4e38
SLOT = 16
RAW, HALF = 3, 2
PAGE = 2048
M_SCALE = float(P) ** -0.5
A_SCALE = float(HD) ** -0.5
SPLITS = (2 * BR, BR, BR, M_HEADS, M_HEADS, BR, BR, BR, BR, BR, BR, HD, A_HEADS, 3 * D)
(O_QK, O_V, O_O, O_I, O_F, O_RX, O_RG, O_AQ, O_AK, O_AV, O_QI, O_KI, O_W, O_G) = (
    int(v) for v in np.cumsum((0,) + SPLITS)[:-1])

MEM = 256
NMEM = MEM // P
MEM_HEADS = 4
H2 = 8
QR, KVR, ROPE = 384, 256, 64
NQR, NKV = QR // P, KVR // P
MLA_IN = QR + KVR + ROPE
GKV = 2
FF2 = 2816
NFF2 = FF2 // P
MIX = 12
MLA_SCALE = float(P + ROPE) ** -0.5
HD_SCALE = float(P) ** -0.5


HEADS2 = MEM_HEADS + H2
N_FINAL = 2 * DEPTH
N_SECOND = N_FINAL + 1


def prep_tiles(l, u):
    if u < MEM_HEADS:
        return []
    if l == 1:
        return [("q", ND)]
    return [("q", NQR), ("k", NKV)] + ([("pe", NQR)] if u % 2 == 0 else [])


def n_jobs(l, u):
    return max(1, len(prep_tiles(l, u))) if u < HEADS2 else 0


def schedule():
    tiles, blocks, nt, nb = {}, {}, 0, 0

    def stage(name, t, b=0):
        nonlocal nt, nb
        tiles[name], blocks[name] = nt, nb
        nt += t
        nb += b

    for l in range(DEPTH):
        stage(("norm", 2 * l), 1)
        stage(("qi", l), 4, 32)
        stage(("ki", l), 1, 8)
        stage(("if", l), 1, 8)
        stage(("w", l), 1)
        stage(("idx", l), 3 * A_HEADS)
        stage(("mqk", l), 8, 64)
        stage(("mv", l), 4, 32)
        stage(("acol", l), 1)
        stage(("m1", l, 0), 6)
        for h in range(M_HEADS):
            stage(("rx", l, h), 1, 8)
            stage(("mo", l, h), 1, 8)
            stage(("m2", l, h), 2)
            stage(("ak", l, h), 1, 8)
            stage(("m3", l, h), 1)
            if h + 1 < M_HEADS:
                stage(("m1", l, h + 1), 6)
            else:
                stage(("rg", l, 0), 1, 8)
            stage(("m4", l, h), 1)
        for c in range(NBR):
            if c:
                stage(("rg", l, c), 1, 8)
            stage(("rgl", l, c), 2)
            stage(("aq", l, c), 1, 8)
        stage(("av", l), 4, 32)
        for m in range(ND):
            stage(("br", l, 0, m), 2, 12)
        stage(("s", l, 0), 4)
        for h in range(A_HEADS):
            stage(("br", l, 1, h), 2, 12)
            stage(("o", l, h), 9)
        stage(("gc", l), 8, 64)
        stage(("bc", l), 8, 32)
        stage(("wo", l), 8, 64)
        stage(("norm", 2 * l + 1), 1)
        for half in range(2):
            for p in range(NFF // 2):
                stage(("up", l, half, p), 2, 16)
            if l == DEPTH - 1 and half:
                stage(("memnorm", 0), 1)
            stage(("down", l, half), 8, 8 * NFF // 2)
    for l in range(DEPTH):
        stage(("memk", l), 4, 32)
        stage(("norm", N_FINAL if l == 0 else N_SECOND + 2 * l), 1)
        stage(("memv", l), 2, 32)
        stage(("memkst", l), 2)
        if l == 0:
            stage(("norm", N_SECOND), 1)
        if l == 0:
            stage(("cq", l), NQR, NQR * ND)
            stage(("ckv", l), NKV, NKV * ND)
            stage(("kpe", l), 1, ND)
            stage(("cqst", l), 1)
            stage(("ckvst", l), 1)
            stage(("kst", l), 1)
            stage(("qmem", l), 4, 4 * ND)
        else:
            stage(("kg", l), GKV, GKV * ND)
            stage(("qmem", l), 4 + GKV, 4 * ND)
            tiles["kst", l] = tiles["qmem", l] + 1
        for v in range(2):
            stage(("pb", l, v), 1)
        stage(("v2", l, 0), 4, 8 if l == 0 else 2 * ND)
        stage(("s2", l), 4)
        if l == 0:
            stage(("v2", l, 1), 4, 8)
        for u in range(HEADS2):
            if u + 2 < HEADS2:
                stage(("pa", l, u + 2), len(prep_tiles(l, u + 2)), sum(n for _, n in prep_tiles(l, u + 2)))
            stage(("o2", l, u), 9 + n_jobs(l, u + 2))
            tiles["pb", l, u + 2] = tiles["o2", l, u] + 5
        stage(("wo2", l), 8, 8 * MIX)
        stage(("norm", N_SECOND + 2 * l + 1), 1)
        for half in range(2):
            for p in range(NFF2 // 2):
                stage(("up2", l, half, p), 2, 16)
            if l == 0 and half:
                stage(("memnorm", 1), 1)
            stage(("down2", l, half), 8, 8 * NFF2 // 2)
    return tiles, blocks, nt, nb


TILE, BLOCK, N_TILES, N_BLOCKS = schedule()


def qmem_tile(l, m):
    return TILE["qmem", l] + m + (GKV if l and m else 0)


def score_tile(l, h, j):
    return TILE["s", l, 0] + j if h == 0 else TILE["o", l, h - 1] + (2 * j + 2 if j else 1)


def turn_tile(l, h, j):
    return TILE["o", l, h] + (2 * j + 1 if j else 0)


def out_tile(l, h):
    return TILE["o", l, h] + 2


def turn_tile2(l, u, j):
    return TILE["o2", l, u] + 2 * j + (1 + n_jobs(l, u + 2) if j >= 2 else 0)


def score_tile2(l, u, j):
    return TILE["s2", l] + j if u == 0 else turn_tile2(l, u - 1, j) + 1


def out_tile2(l, u):
    return TILE["o2", l, u] + 4


UNUSED = ({score_tile(l, A_HEADS, j) for l in range(DEPTH) for j in range(NQ)}
          | {score_tile2(l, HEADS2, j) for l in range(DEPTH) for j in range(NQ)})


N_SLOTS = -(-N_BLOCKS // SLOT)


def param_columns():
    at, n = {}, 0
    for name, c in (("norm_mix", ND), ("mlstm_conv_w", 4 * 8), ("mlstm_conv_b", 8), ("mlstm_norm", 4),
                    ("rglru_conv_w", 16), ("rglru_conv_b", 4), ("rglru_b_a", 4), ("rglru_b_x", 4),
                    ("rglru_lambda", 4), ("norm_ffn", ND), ("ffn_conv_w", 3 * NFF), ("ffn_conv_b", NFF),
                    ("i_bias", 1), ("f_bias", 1)):
        at[name] = n
        n += c
    return at, n


PCOL, PLAYER = param_columns()
P_FINAL = DEPTH * PLAYER


def second_columns():
    at, n = {}, P_FINAL + ND
    for name, c in (("mem_norm", ND), ("norm_mix", DEPTH * ND), ("norm_ffn", DEPTH * ND), ("memq", DEPTH),
                    ("memk", DEPTH), ("q_a", NQR), ("kv_a", NKV), ("mla_q", 1), ("mla_qpe", 1),
                    ("mla_k", 1), ("mla_kpe", 1), ("gqa_q", 1), ("gqa_k", 1)):
        at[name] = n
        n += c
    return at, n


PCOL2, P_TOTAL = second_columns()
PE_ORDER = np.r_[0:16, 32:48, 16:32, 48:64]


def pack_weights(w):
    out = np.zeros((N_SLOTS * SLOT, P, P), np.float32)
    place = [0]

    def put(a):
        out[place[0], :, :a.shape[1]] = a
        place[0] += 1

    def by_tile(a, cols=None):
        k, n = a.shape
        for m in range(n // P):
            for c in range(k // P):
                put(a[c * P:(c + 1) * P, m * P:(m + 1) * P])

    def by_k(a):
        k, n = a.shape
        for c in range(k // P):
            for m in range(n // P):
                put(a[c * P:(c + 1) * P, m * P:(m + 1) * P])

    def pair(gate, up, first):
        if first:
            by_k(np.concatenate([gate, up], axis=1))
        else:
            by_tile(gate)
            by_tile(up)

    for l in range(DEPTH):
        wi, wb, wo = w["w_in"][l], w["w_branch"][l], w["w_out"][l]
        up, down = w["ffn_up"][l], w["ffn_down"][l]
        by_k(wi[:, O_QI:O_QI + BR])
        ki = wi[:, O_KI:O_KI + HD]
        by_tile(np.concatenate([ki, ki], axis=1))
        small = np.zeros((D, P), np.float32)
        small[:, 0:4] = wi[:, O_I:O_I + 4]
        small[:, 32:36] = wi[:, O_F:O_F + 4]
        small[:, 64:72] = wi[:, O_W:O_W + 8]
        by_tile(small)
        by_tile(wi[:, O_QK:O_QK + 2 * BR])
        by_k(wi[:, O_V:O_V + BR])
        for h in range(M_HEADS):
            for o in (O_RX, O_O, O_AK):
                by_tile(wi[:, o + h * P:o + (h + 1) * P])
        for c in range(NBR):
            for o in (O_RG, O_AQ):
                by_tile(wi[:, o + c * P:o + (c + 1) * P])
        by_k(wi[:, O_AV:O_AV + BR])
        for b in range(2):
            for m in range(ND):
                by_tile(wi[:, O_G + b * D + m * P:O_G + b * D + (m + 1) * P])
                by_tile(wb[b][:, m * P:(m + 1) * P])
        by_tile(wi[:, O_G + 2 * D:O_G + 3 * D])
        by_tile(wb[2])
        by_tile(wo)
        for half in range(2):
            for p in range(half * NFF // 2, (half + 1) * NFF // 2):
                pair(up[:, p * P:(p + 1) * P], up[:, FF + p * P:FF + (p + 1) * P], p == 0)
            by_tile(down[half * FF // 2:(half + 1) * FF // 2])
    for l in range(DEPTH):
        mkv = w["w_mem_kv_2"][l]
        by_tile(mkv[:, :BR])
        by_k(mkv[:, BR:])
        if l == 0:
            wi, qb = w["mla_w_in_2"][0], w["mla_w_q_b_2"][0].reshape(QR, H2, P + ROPE)
            kvb = w["mla_w_kv_b_2"][0].reshape(KVR, H2, 2 * P)
            by_k(wi[:, :QR])
            by_tile(wi[:, QR:QR + KVR])
            kpe = wi[:, QR + KVR:MLA_IN][:, PE_ORDER]
            by_tile(np.concatenate([kpe, kpe], axis=1))
            by_tile(wi[:, MLA_IN:])
            for g in range(2):
                by_k(kvb[:, 4 * g:4 * g + 4, P:].reshape(KVR, 4 * P))
        else:
            wi = w["gqa_w_in_2"][0]
            q, kv = H2 * P, GKV * P
            by_k(wi[:, q:q + kv])
            by_tile(wi[:, q + 2 * kv:])
            by_k(wi[:, q + kv:q + 2 * kv])
        for u in range(MEM_HEADS, HEADS2):
            h = u - MEM_HEADS
            for kind, _ in prep_tiles(l, u):
                if l == 1:
                    by_tile(wi[:, h * P:(h + 1) * P])
                elif kind == "q":
                    by_tile(qb[:, h, :P])
                elif kind == "k":
                    by_tile(kvb[:, h, :P])
                else:
                    by_tile(qb[:, h:h + 2, P:][:, :, PE_ORDER].reshape(QR, 2 * ROPE))
        by_tile(w["w_out_2"][l])
        gu, down = w["w_gate_up_2"][l], w["w_down_2"][l]
        for half in range(2):
            for p in range(half * NFF2 // 2, (half + 1) * NFF2 // 2):
                pair(gu[:, p * P:(p + 1) * P], gu[:, FF2 + p * P:FF2 + (p + 1) * P], p == 0)
            by_tile(down[half * FF2 // 2:(half + 1) * FF2 // 2])
    assert place[0] == N_BLOCKS
    return out.reshape(N_SLOTS, SLOT, P, P).transpose(0, 2, 1, 3).reshape(N_SLOTS, P, SLOT * P).copy()


def pack_params(w):
    out = np.zeros((P, P_TOTAL), np.float32)

    def col(v):
        return np.asarray(v, np.float32).reshape(-1, P).T

    for l in range(DEPTH):
        o = l * PLAYER
        for name in ("norm_mix", "mlstm_conv_w", "mlstm_conv_b", "mlstm_norm", "rglru_conv_w",
                     "rglru_conv_b", "rglru_b_a", "rglru_b_x", "rglru_lambda", "norm_ffn",
                     "ffn_conv_w", "ffn_conv_b"):
            c = col(w[name][l])
            out[:, o + PCOL[name]:o + PCOL[name] + c.shape[1]] = c
        out[0:4, o + PCOL["i_bias"]] = w["mlstm_i_bias"][l]
        out[0:4, o + PCOL["f_bias"]] = w["mlstm_f_bias"][l]
    out[:, P_FINAL:P_FINAL + ND] = col(w["norm_final"])
    q, k = w["mla_q_norm_2"][0], w["mla_k_norm_2"][0]
    for name, v in (("mem_norm", w["mem_norm_2"]), ("norm_mix", w["norm_mix_2"]), ("norm_ffn", w["norm_ffn_2"]),
                    ("memq", w["memq_norm_2"]), ("memk", w["memk_norm_2"]), ("q_a", w["mla_q_a_norm_2"][0]),
                    ("kv_a", w["mla_kv_a_norm_2"][0]), ("mla_q", q[:P]), ("mla_k", k[:P]),
                    ("mla_qpe", np.concatenate([q[P:][PE_ORDER]] * 2)),
                    ("mla_kpe", np.concatenate([k[P:][PE_ORDER]] * 2)),
                    ("gqa_q", w["gqa_q_norm_2"][0]), ("gqa_k", w["gqa_k_norm_2"][0])):
        c = col(v)
        out[:, PCOL2[name]:PCOL2[name] + c.shape[1]] = c
    return out


def pack_rglru(w):
    out = np.zeros((P, DEPTH, 8, P), np.float32)
    for l in range(DEPTH):
        for g, name in enumerate(("rglru_w_a", "rglru_w_x")):
            for c in range(NBR):
                for e in range(2):
                    r = slice(64 * e, 64 * e + 64)
                    out[r, l, 4 * g + c, r] = w[name][l, 2 * c + e]
    return out


C_ID, C_ONE, C_ST, C_QK, C_ONE64 = (i * P for i in range(5))
C_INV, C_SGN = 5 * P, 5 * P + 1
C_TOTAL = 5 * P + 2


def constants():
    i = np.arange(P)
    out = np.zeros((P, C_TOTAL), np.float32)
    out[:, C_ID:C_ID + P] = np.eye(P)
    out[:, C_ONE:C_ONE + P] = 1.0
    out[:, C_ST:C_ST + P] = np.where(i[:, None] <= i[None, :], 0.0, NEG)
    out[:, C_QK:C_QK + P] = np.where(i[:, None] >= i[None, :], 0.0, NEG)
    inv = np.float32(10000.0) ** (-np.arange(0, HD, 2, dtype=np.float32) / np.float32(HD))
    out[:, C_INV] = inv[i % 32]
    out[:, C_SGN] = np.where(i % 64 < 32, -1.0, 1.0)
    out[:, C_ONE64:C_ONE64 + P] = i[:, None] // 64 == i[None, :] // 64
    return out


def axial_tables():
    t = np.arange(S)
    row, col = (t // 64).astype(np.float32), (t % 64).astype(np.float32)
    out = np.zeros((2, 2, P, S), np.float32)
    for g in range(2):
        for p in range(P):
            if g == 0:
                f, axis, first, width = p % 16, (p % 32) // 16, p % 64 < 32, 32
            else:
                f, axis, first, width = p % 32, p // 64, p % 64 < 32, 64
            inv = np.float32(10000.0) ** (-np.arange(0, width, 2, dtype=np.float32) / np.float32(width))
            a = (col if axis else row) * inv[f]
            out[g, 0, p] = np.cos(a)
            out[g, 1, p] = -np.sin(a) if first else np.sin(a)
    return out


class Engine:

    def __init__(self, name, sems, marks, known):
        self.name, self.sems, self.marks, self.known = name, sems, marks, known
        self.count, self.previous = {}, None

    def signals(self, *names):
        own = [n[0] for n in names if n[0] not in ("read", "full", "slot")] + [n[0] for n in names]
        kind = own[0] if own and own[0] != "read" else self.name + ("_read" if own else "_step")
        n = self.count[kind] = self.count.get(kind, 0) + 1
        for name in names:
            assert name not in self.marks, name
            self.marks[name] = (kind, n)
        self.previous = self.sems[kind], n
        return self.sems[kind], 1

    def after(self, *name):
        kind, n = self.known[name] if self.known else ("x_in0", 1)
        return self.sems[kind], n


def build(nc, args, known):
    A = dict(args)
    marks = {}
    with ExitStack() as ctx:
        base = nc.sbuf_base + (-nc.sbuf_base) % 32

        def at(name, off, shape, dt=F32):
            return nc.alloc_sbuf_tensor_at(name, shape, dt, offset=off)

        off = base

        def fixed(name, shape, dt=F32):
            nonlocal off
            t = at(name, off, shape, dt)
            off += int(np.prod(shape[1:])) * 4
            off += (-off) % 32
            return t

        x = fixed("x", [P, ND, S])
        hh = fixed("hh", [P, ND, S], F32R)
        hl = fixed("hl", [P, ND, S], F32R)
        raw = fixed("raw", [P, RAW, SLOT * P])
        whi = fixed("whi", [P, HALF, SLOT * P], F32R)
        wlo = fixed("wlo", [P, HALF, SLOT * P], F32R)
        tabc = fixed("tabc", [P, S])
        tabs = fixed("tabs", [P, S])
        cin = fixed("cin", [P, 2, S + 3])
        cacc = fixed("cacc", [P, 2, S])
        con = fixed("con", [P, C_TOTAL])
        par = fixed("par", [P, P_TOTAL])
        sp8 = fixed("sp8", [P, DEPTH * 4])
        spt = fixed("spt", [P, 6, DEPTH * 4])
        rgw_off = off
        rgw = fixed("rgw", [P, DEPTH, 8, P])
        acol = fixed("acol", [P, NQ, M_HEADS])
        wcol = fixed("wcol", [P, NQ, A_HEADS])
        top = fixed("top", [P, 3, 8])
        nmx = fixed("nmx", [P, 8])
        rsum = fixed("rsum", [P, 8])
        rinv = fixed("rinv", [P, 8])
        bcol = fixed("bcol", [P, 4])
        region = off + (-off) % 32
        n_pages = (nc.sbuf_usable_end - region) // PAGE
        assert n_pages >= 46, n_pages

        def pages(name, p, shape, dt=F32):
            assert p * PAGE + int(np.prod(shape[1:])) * 4 <= n_pages * PAGE
            return at(name, region + p * PAGE, shape, dt)

        ah = pages("ah", 0, [P, 12, S], F32R)
        al = pages("al", 12, [P, 12, S], F32R)
        qi = pages("qi", 4, [P, 4, S])
        ki = pages("ki", 8, [P, S])
        work = pages("work", 9, [P, 3, S])
        relu = pages("relu", 16, [P, 2, S])
        rsw = pages("rsw", 18, [P, 2, S])
        rt1 = pages("rt1", 20, [P, 2, S])
        mq = pages("mq", 24, [P, 4, S])
        mk = pages("mk", 28, [P, 4, S])
        mv = pages("mv", 32, [P, NQ, BR])
        mo = pages("mo", 45, [P, S])
        aswap = pages("aswap", 43, [P, S])
        atmp = pages("atmp", 44, [P, S])
        rows = [pages(f"row{i}", p, [4, S]) for i, p in enumerate((0, 1, 2, 3, 12, 13))]
        wrow = pages("wrow", 14, [8, S])
        negm = pages("negm", 40, [4, S])
        negg = pages("negg", 41, [4, S])
        xc = pages("xc", 4, [P, 4, S])
        mp = pages("mp", 16, [P, 4, S])
        mnm = pages("mnm", 20, [P, S])
        mdm = pages("mdm", 21, [P, NQ, P])
        mwx = pages("mwx", 22, [P, 2, S])
        mex = pages("mex", 8, [P, S])
        mdn = pages("mdn", 42, [P, S])
        yf = pages("yf", 28, [P, 4, S])
        rg = pages("rg", 24, [P, 4, S])
        rt = pages("rt", 16, [P, 6, S])
        rsw2 = pages("rsw2", 22, [P, 2, S])
        aq = pages("aq", 32, [P, 4, S])
        ak = pages("ak", 36, [P, 4, S])
        av = [pages(f"av{i}", p, [P, BR]) for i, p in enumerate((40, 41, 42, 8))]
        mer = pages("mer", 16, [P, ND, S])
        sm = pages("sm", 4, [P, 4, S])
        pt = pages("pt", 24, [P, 3, S])
        sig = pages("sig", 27, [P, S])
        sigc = pages("sigc", 32, [P, ND, S])
        nsq0 = pages("nsq0", 34, [P, ND, S])
        nsum = pages("nsum", 27, [P, S])
        nsq = pages("nsq", 25, [P, 2, S])
        nri = pages("nri", 24, [P, S])
        nhf = pages("nhf", 32, [P, 2, S])
        fga = pages("fga", 24, [P, 2, S])
        fhf = pages("fhf", 26, [P, 2, S])
        pos_i = pages("pos_i", 0, [P, S], I32)
        rtab = pages("rtab", 1, [P, 6, S])

        memf = pages("memf", 34, [P, ND, MEM])
        memh = pages("memh", 38, [P, ND, MEM], F32R)
        meml = pages("meml", 42, [P, ND, MEM], F32R)
        mri = pages("mri", 32, [P, MEM])
        msq = pages("msq", 28, [P, ND, MEM])
        kraw = pages("kraw", 14, [P, 2, S])
        ksq = pages("ksq", 16, [P, 2, S])
        kst = pages("kst", 18, [P, 2, S])
        kmem = pages("kmem", 36, [P, MEM_HEADS, MEM])
        vmem = pages("vmem", 38, [P, NMEM, BR])
        kpe = pages("kpe", 40, [P, S])
        pt2 = [pages(f"pt2_{i}", p, [P, S]) for i, p in enumerate((41, 42, 43))]
        v2 = pages("v2", 24, [P, NQ, 2 * BR])
        qmem = pages("qmem", 32, [P, MEM_HEADS, S])
        cqr = pages("cqr", 0, [P, NQR + NKV, S])
        cqs = pages("cqs", 5, [P, NQR + NKV, S])
        cqi = pages("cqi", 10, [P, 2, S])
        jst = pages("jst", 44, [P, 2, S])
        off_h = base + ND * S * 4
        ring_q = [at(f"ringq{i}", off_h + (5 + i) * PAGE, [P, S]) for i in range(2)]
        ring_k = [at("ringk0", off_h + 7 * PAGE, [P, S]), at("ringk1", off_h + (ND + 5) * PAGE, [P, S])]
        ring_p = [at(f"ringp{i}", off_h + (ND + 6 + i) * PAGE, [P, S]) for i in range(2)]
        gq = [pages(f"gq{i}", 24 + i, [P, S]) for i in range(2)]
        kg = pages("kg", 26, [P, GKV, S])
        vg = pages("vg", 28, [P, NQ, GKV * P])
        sm2 = at("sm2", rgw_off, [P, NQ, S])
        fga2 = pages("fga2", 24, [P, 2, S])
        fhf2 = pages("fhf2", 26, [P, 2, S])

        ps = [ctx.enter_context(nc.psum_tensor(f"bank{i}", [P, S], F32)) for i in range(8)]
        sems = {n: ctx.enter_context(nc.semaphore(n)) for n in (
            "x_in0 x_in1 con_in par_in rgw_in pos_in mem_in tab_in out_stored "
            "full slot turned pv turned2 pv2 "
            "act_step act_read hi lam_exp sin tabc sq rms hh swap if wcol wrow fexp relu cin mqk mv mo acol mnm mex mwx "
            "rcin mhsq mstd yh rg rr ri rth ra rs av sig e pt yfo sigc merh fcin fga ffh msq mrms memh kraw ksq "
            "vmem kst craw kperaw jsq qmemraw csq cstd lath jstd jswap v2 e2 pt2 mixh fga2 ffh2 "
            "dve_step dve_read bcol lo ssum lam_abs spn ang hf h qi ki fabs arow negm negg acc conv mdm mp mh mhc xc "
            "yf y rq aq ak merged sm p merf mer x fconv fhf ff xhalf memn mem kmem clat lat jn jend nmx2 p2 mix "
            "fhf2 ff2 out").split()}
        landed = [ctx.enter_context(nc.semaphore(f"landed{i}")) for i in range(RAW)]
        for i in range(RAW):
            sems[f"landed{i}"] = landed[i]
        for s in range(N_SLOTS):
            marks[("landed", s)] = (f"landed{s % RAW}", 16 * (s // RAW + 1))
        for n in ("con", "par", "rgw", "pos"):
            marks[(n + "_in",)] = (n + "_in", 16)
        for l in range(DEPTH):
            marks["mem_in", l] = ("mem_in", 16 * (l + 1))
            marks["tab_in", l] = ("tab_in", 32 * (l + 1))
        ones64 = con[:, C_ONE64:C_ONE64 + P]

        def jobs(l, u):
            h = u - MEM_HEADS
            g = lambda name, i=0: par[:, PCOL2[name] + i:PCOL2[name] + i + 1]
            if u < MEM_HEADS:
                return [(("q2", l, u), qmem[:, u, :], ones, P, g("memq", l), False)]
            if l == 1:
                return [(("q2", l, u), gq[h % 2][:, :], ones, P, g("gqa_q"), True)]
            out = [(("q2", l, u), ring_q[h % 2][:, :], ones, P, g("mla_q"), False),
                   (("k2", l, u), ring_k[h % 2][:, :], ones, P, g("mla_k"), False)]
            if h % 2 == 0:
                out.append((("pe2", l, u), ring_p[h // 2 % 2][:, :], ones64, ROPE, g("mla_qpe"), True))
            return out

        def place(u, i):
            return i + (u % 2 if u < MEM_HEADS else 0)

        sqbuf = [cacc[:, 0, :], cacc[:, 1, :], cin[:, 0, 0:S]]
        swap2 = cin[:, 1, 0:S]

        ident = con[:, C_ID:C_ID + P]
        ones = con[:, C_ONE:C_ONE + P]
        mask_st = con[:, C_ST:C_ST + P]
        mask_qk = con[:, C_QK:C_QK + P]

        def bank(t):
            return ps[t % 8]

        def pcol(name, l, i=0, n=1):
            c = l * PLAYER + PCOL[name] + i
            return par[:, c:c + n]

        def norm_gain(n, c):
            if n == N_FINAL:
                return par[:, P_FINAL + c:P_FINAL + c + 1]
            if n > N_FINAL:
                i = n - N_SECOND
                o = PCOL2["norm_ffn" if i % 2 else "norm_mix"] + i // 2 * ND + c
                return par[:, o:o + 1]
            return pcol("norm_ffn" if n % 2 else "norm_mix", n // 2, c)

        block = ctx.enter_context(nc.Block())

        @block.sync
        def _(eng):
            sp = Engine("sp", sems, marks, known)
            eng.dma_start(par[:, :], A["par"]).then_inc(sems["par_in"], 16)
            eng.dma_start(pos_i[:, :], A["pos"][0:1, :].partition_broadcast(P)).then_inc(sems["pos_in"], 16)
            eng.dma_start(con[:, :], A["con"]).then_inc(sems["con_in"], 16)
            for i in range(2):
                c = slice(i * ND // 2, (i + 1) * ND // 2)
                eng.dma_start(x[:, c, :], A["x"][:, c, :]).then_inc(sems[f"x_in{i}"], 16)
            for s in range(2):
                eng.dma_start(raw[:, s % RAW, :], A["w"][s]).then_inc(landed[s % RAW], 16)
            eng.dma_start(rgw[:, :, :, :], A["rgw"]).then_inc(sems["rgw_in"], 16)
            for s in range(2, N_SLOTS):
                if s >= RAW:
                    eng.wait_ge(*sp.after("lo", s - RAW))
                eng.dma_start(raw[:, s % RAW, :], A["w"][s]).then_inc(landed[s % RAW], 16)
            for c in range(ND):
                eng.wait_ge(*sp.after("out", c))
            eng.dma_start(A["out"], x[:, :, :]).then_inc(sems["out_stored"], 16)
            eng.wait_ge(sems["out_stored"], 16)

        @block.tensor
        def _(eng):
            pe = Engine("pe", sems, marks, known)

            def opened(t):
                t -= 8
                while t in UNUSED:
                    t -= 8
                if t >= 0:
                    eng.wait_ge(*pe.after("read", t))

            def three(out, wh, wl, rh, rl, start, stop):
                eng.matmul(out, wh, rl, start=start, stop=False)
                eng.matmul(out, wh, rh, start=False, stop=False)
                return eng.matmul(out, wl, rh, start=False, stop=stop)

            def wblk(b, n=1):
                s, i = b // SLOT % HALF, b % SLOT
                return whi[:, s, i * P:(i + n) * P], wlo[:, s, i * P:(i + n) * P]

            def take(b):
                if b % SLOT == 0:
                    eng.wait_ge(*pe.after("lo", b // SLOT))

            def gemm(t, b, nk, rh, rl, key, start=True):
                opened(t)
                for k in range(nk):
                    take(b)
                    eng.wait_ge(*pe.after(*key(k)))
                    wh, wl = wblk(b)
                    ins = three(bank(t)[:, :], wh, wl, rh[:, k, :], rl[:, k, :], k == 0, k == nk - 1)
                    ends = [("full", t)] if k == nk - 1 else []
                    if b % SLOT == SLOT - 1:
                        ends.append(("slot", b // SLOT))
                    if ends:
                        ins.then_inc(*pe.signals(*ends))
                    b += 1

            def gemm_abreast(t, b, n, nk, rh, rl, key):
                for i in range(n):
                    opened(t + i)
                for k in range(nk):
                    eng.wait_ge(*pe.after(*key(k)))
                    for i in range(n):
                        take(b)
                        wh, wl = wblk(b)
                        ins = three(bank(t + i)[:, :], wh, wl, rh[:, k, :], rl[:, k, :], k == 0, k == nk - 1)
                        ends = [("full", t + i)] if k == nk - 1 else []
                        if b % SLOT == SLOT - 1:
                            ends.append(("slot", b // SLOT))
                        if ends:
                            ins.then_inc(*pe.signals(*ends))
                        b += 1

            def gemm_tokens(t, b, nk, lh, ll, key):
                for i in range(NQ):
                    opened(t + i)
                for k in range(nk):
                    take(b)
                    eng.wait_ge(*pe.after(*key(k)))
                    wh, wl = wblk(b, 4)
                    for i in range(NQ):
                        c = slice(i * P, i * P + P)
                        ins = three(bank(t + i)[:, :], lh[:, k, c], ll[:, k, c], wh, wl, k == 0, k == nk - 1)
                        ends = [("full", t + i)] if k == nk - 1 else []
                        if i == NQ - 1 and (b + 3) % SLOT == SLOT - 1:
                            ends.append(("slot", b // SLOT))
                        if ends:
                            ins.then_inc(*pe.signals(*ends))
                    b += 4

            def norm(n):
                t = TILE["norm", n]
                opened(t)
                eng.wait_ge(*pe.after("con_in"))
                if n == 0:
                    for c in range(ND):
                        eng.wait_ge(*pe.after("sq", n, c))
                        ins = eng.matmul(bank(t)[:, :], ones, nsq0[:, c, :], start=c == 0, stop=c == ND - 1)
                else:
                    eng.wait_ge(*pe.after("ssum", n, ND - 1))
                    ins = eng.matmul(bank(t)[:, :], ones, nsum[:, :], start=True, stop=True)
                ins.then_inc(*pe.signals(("full", t)))

            def tile_mm(t, pairs):
                opened(t)
                for i, (out, a, b) in enumerate(pairs):
                    ins = eng.matmul(out, a, b, start=i == 0, stop=i == len(pairs) - 1)
                ins.then_inc(*pe.signals(("full", t)))

            def mem_norm(l):
                t = TILE["memnorm", l]
                opened(t)
                eng.wait_ge(*pe.after("msq", l, ND - 1))
                for c in range(ND):
                    ins = eng.matmul(bank(t)[:, 0:MEM], ones, msq[:, c, :], start=c == 0, stop=c == ND - 1)
                ins.then_inc(*pe.signals(("full", t)))

            for l in range(DEPTH):
                n1 = 2 * l
                hkey = lambda k, n1=n1: ("h", n1, k)
                norm(n1)
                gemm_abreast(TILE["qi", l], BLOCK["qi", l], 4, ND, hh, hl, hkey)
                gemm(TILE["ki", l], BLOCK["ki", l], 8, hh, hl, hkey)
                t, b = TILE["if", l], BLOCK["if", l]
                opened(t)
                for k in range(ND):
                    take(b + k)
                    wh, wl = wblk(b + k)
                    ins = three(bank(t)[:, :], wh, wl, hh[:, k, :], hl[:, k, :], k == 0, k == ND - 1)
                assert (b + ND) % SLOT == 0
                ins.then_inc(*pe.signals(("full", t), ("slot", b // SLOT)))
                eng.wait_ge(*pe.after("wrow", l))
                opened(t + 1)
                for i in range(NQ):
                    ins = eng.transpose(bank(t + 1)[:, 8 * i:8 * i + 8], wrow[:, P * i:P * i + P], con[0:8, 0:8])
                ins.then_inc(*pe.signals(("full", t + 1)))
                t = TILE["idx", l]
                for m in range(4):
                    eng.wait_ge(*pe.after("qi", l, m))
                eng.wait_ge(*pe.after("ki", l))
                for j in range(3, 0, -1):
                    for h in range(A_HEADS):
                        r = slice(64 * (h % 2), 64 * (h % 2) + 64)
                        tile_mm(t, [(bank(t)[:, 0:P * (j + 1)], qi[r, h // 2, P * j:P * j + P],
                                     ki[r, 0:P * (j + 1)])])
                        t += 1
                for m in range(8):
                    gemm(TILE["mqk", l] + m, BLOCK["mqk", l] + 8 * m, 8, hh, hl, hkey)
                gemm_tokens(TILE["mv", l], BLOCK["mv", l], 8, hh, hl, hkey)
                t = TILE["acol", l]
                opened(t)
                eng.wait_ge(*pe.after("arow", l))
                for j in range(NQ):
                    ins = eng.transpose(bank(t)[:, 4 * j:4 * j + 4], rows[0][:, P * j:P * j + P], con[0:4, 0:4])
                ins.then_inc(*pe.signals(("full", t)))
                def m1(h):
                    t = TILE["m1", l, h]
                    one_row = con[0:4, h:h + 1].to_broadcast([4, P])
                    eng.wait_ge(*pe.after("negm", l))
                    eng.wait_ge(*pe.after("negg", l))
                    tile_mm(t, [(bank(t)[:, :], one_row, negm[:, :])])
                    tile_mm(t + 1, [(bank(t + 1)[:, :], one_row, negg[:, :])])
                    eng.wait_ge(*pe.after("mqk", l, h))
                    eng.wait_ge(*pe.after("mqk", l, 4 + h))
                    for j in range(NQ):
                        tile_mm(t + 2 + j, [(bank(t + 2 + j)[:, P * j:], mk[:, h, P * j:P * j + P], mq[:, h, P * j:])])

                m1(0)
                for h in range(M_HEADS):
                    gemm(TILE["rx", l, h], BLOCK["rx", l, h], 8, hh, hl, hkey)
                    gemm(TILE["mo", l, h], BLOCK["mo", l, h], 8, hh, hl, hkey)
                    t = TILE["m2", l, h]
                    for i in range(NQ):
                        eng.wait_ge(*pe.after("mv", l, i))
                        eng.wait_ge(*pe.after("mp", l, h, i))
                    tile_mm(t, [(bank(t)[:, P * j:], mv[:, j, P * h:P * h + P], mp[:, j, P * j:]) for j in range(NQ)])
                    tile_mm(t + 1, [(bank(t + 1)[:, P * j:], ones, mp[:, j, P * j:]) for j in range(NQ)])
                    gemm(TILE["ak", l, h], BLOCK["ak", l, h], 8, hh, hl, hkey)
                    eng.wait_ge(*pe.after("mh", l, h))
                    t = TILE["m3", l, h]
                    tile_mm(t, [(bank(t)[:, :], ones, mq[:, h, :])])
                    if h + 1 < M_HEADS:
                        m1(h + 1)
                    else:
                        gemm(TILE["rg", l, 0], BLOCK["rg", l, 0], 8, hh, hl, hkey)
                    eng.wait_ge(*pe.after("mhsq", l, h))
                    t = TILE["m4", l, h]
                    tile_mm(t, [(bank(t)[:, :], ones, mwx[:, 0, :])])
                eng.wait_ge(*pe.after("rgw_in"))
                for c in range(NBR):
                    if c:
                        gemm(TILE["rg", l, c], BLOCK["rg", l, c], 8, hh, hl, hkey)
                    eng.wait_ge(*pe.after("xc", l, c))
                    t = TILE["rgl", l, c]
                    tile_mm(t, [(bank(t)[:, :], rgw[:, l, c, :], xc[:, c, :])])
                    tile_mm(t + 1, [(bank(t + 1)[:, :], rgw[:, l, 4 + c, :], xc[:, c, :])])
                    gemm(TILE["aq", l, c], BLOCK["aq", l, c], 8, hh, hl, hkey)
                gemm_tokens(TILE["av", l], BLOCK["av", l], 8, hh, hl, hkey)

                def branch(b, m):
                    t, blk = TILE["br", l, b, m], BLOCK["br", l, b, m]
                    gemm(t, blk, 8, hh, hl, hkey)
                    gemm(t + 1, blk + 8, 4, ah, al, lambda k: ("y", l, b, k))

                def scores(h, j):
                    t = score_tile(l, h, j)
                    r = slice(64 * (h % 2), 64 * (h % 2) + 64)
                    eng.wait_ge(*pe.after("aq", l, h // 2))
                    eng.wait_ge(*pe.after("ak", l, h // 2))
                    tile_mm(t, [(bank(t)[:, 0:P * (j + 1)], aq[r, h // 2, P * j:P * j + P],
                                 ak[r, h // 2, 0:P * (j + 1)])])

                def turn(h, j):
                    t = turn_tile(l, h, j)
                    opened(t)
                    eng.wait_ge(*pe.after("p", l, h, j))
                    for i in range(j + 1):
                        ins = eng.transpose(bank(t)[:, P * i:P * i + P], sm[:, j, P * i:P * i + P], ident)
                    ins.then_inc(*pe.signals(("full", t), ("turned", l, h, j)))

                def outputs(h):
                    to = out_tile(l, h)
                    hp = slice(P * (h // 2), P * (h // 2) + P)
                    for j in range(NQ + 1):
                        if j < NQ:
                            turn(h, j)
                            if h + 1 < A_HEADS:
                                scores(h + 1, j)
                        if j == 0:
                            opened(to)
                            for i in range(NQ):
                                eng.wait_ge(*pe.after("av", l, i))
                            continue
                        jj = j - 1
                        eng.wait_ge(*pe.after("pt", l, h, jj))
                        for i in range(jj + 1):
                            ins = eng.matmul(bank(to)[:, P * jj:P * jj + P], av[i][:, hp],
                                             pt[:, (4 * h + jj) % 3, P * i:P * i + P], start=i == 0, stop=i == jj)
                        ins.then_inc(*pe.signals(("pv", l, h, jj), *([("full", to)] if jj == NQ - 1 else [])))

                for m in range(ND):
                    branch(0, m)
                for j in range(NQ):
                    scores(0, j)
                for h in range(A_HEADS):
                    branch(1, h)
                    outputs(h)
                for m in range(ND):
                    gemm(TILE["gc", l] + m, BLOCK["gc", l] + 8 * m, 8, hh, hl, hkey)
                for m in range(ND):
                    gemm(TILE["bc", l] + m, BLOCK["bc", l] + 4 * m, 4, ah, al, lambda k: ("y", l, 2, k))
                for m in range(ND):
                    gemm(TILE["wo", l] + m, BLOCK["wo", l] + 8 * m, 8, hh, hl, lambda k: ("mer", l, k))
                norm(2 * l + 1)
                for half in range(2):
                    for p in range(NFF // 2):
                        t, b = TILE["up", l, half, p], BLOCK["up", l, half, p]
                        if half == p == 0:
                            gemm_abreast(t, b, 2, ND, hh, hl, lambda k: ("h", 2 * l + 1, k))
                            continue
                        gemm(t, b, 8, hh, hl, lambda k: ("h", 2 * l + 1, k))
                        gemm(t + 1, b + 8, 8, hh, hl, lambda k: ("h", 2 * l + 1, k))
                    if l == DEPTH - 1 and half:
                        mem_norm(0)
                    for m in range(ND):
                        gemm(TILE["down", l, half] + m, BLOCK["down", l, half] + 12 * m, 12, ah, al,
                             lambda k: ("ff", l, half, k))
            for l in range(DEPTH):
                n1 = N_SECOND + 2 * l
                hkey = lambda k: ("h", n1, k)
                b = BLOCK["memk", l]
                for m in range(MEM_HEADS):
                    t = TILE["memk", l] + m
                    opened(t)
                    for k in range(ND):
                        take(b)
                        eng.wait_ge(*pe.after("mem", l, k))
                        wh, wl = wblk(b)
                        ins = three(bank(t)[:, 0:MEM], wh, wl, memh[:, k, :], meml[:, k, :], k == 0, k == ND - 1)
                        ends = [("full", t)] if k == ND - 1 else []
                        if b % SLOT == SLOT - 1:
                            ends.append(("slot", b // SLOT))
                        if ends:
                            ins.then_inc(*pe.signals(*ends))
                        b += 1
                norm(n1 if l else N_FINAL)
                b = BLOCK["memv", l]
                t = TILE["memv", l]
                for i in range(NMEM):
                    opened(t + i)
                for k in range(ND):
                    take(b)
                    wh, wl = wblk(b, 4)
                    for i in range(NMEM):
                        c = slice(i * P, i * P + P)
                        ins = three(bank(t + i)[:, :], memh[:, k, c], meml[:, k, c], wh, wl, k == 0, k == ND - 1)
                        ends = [("full", t + i)] if k == ND - 1 else []
                        if i == NMEM - 1 and (b + 3) % SLOT == SLOT - 1:
                            ends.append(("slot", b // SLOT))
                        if ends:
                            ins.then_inc(*pe.signals(*ends))
                    b += 4
                for i in range(2):
                    t = TILE["memkst", l] + i
                    eng.wait_ge(*pe.after("ksq", l, i))
                    tile_mm(t, [(bank(t)[:, :], ones, ksq[:, i, :])])
                if l == 0:
                    norm(n1)
                if l == 0:
                    gemm_abreast(TILE["cq", l], BLOCK["cq", l], NQR, ND, hh, hl, hkey)
                    for name, n in (("ckv", NKV), ("kpe", 1)):
                        for m in range(n):
                            gemm(TILE[name, l] + m, BLOCK[name, l] + ND * m, ND, hh, hl, hkey)
                    for name, c0, n in (("cqst", 0, NQR), ("ckvst", NQR, NKV)):
                        t = TILE[name, l]
                        opened(t)
                        for c in range(c0, c0 + n):
                            eng.wait_ge(*pe.after("csq", l, c))
                            ins = eng.matmul(bank(t)[:, :], ones, cqs[:, c, :], start=c == c0, stop=c == c0 + n - 1)
                        ins.then_inc(*pe.signals(("full", t)))
                    t = TILE["kst", l]
                    eng.wait_ge(*pe.after("jsq", "kpe", l))
                    tile_mm(t, [(bank(t)[:, :], ones64, sqbuf[0])])
                else:
                    gemm_abreast(TILE["kg", l], BLOCK["kg", l], GKV, ND, hh, hl, hkey)
                for m in range(MEM_HEADS):
                    gemm(qmem_tile(l, m), BLOCK["qmem", l] + ND * m, ND, hh, hl, hkey)
                    if l == 1 and m == 0:
                        for i in range(GKV):
                            t = TILE["kst", l] + i
                            eng.wait_ge(*pe.after("jsq", "kg", l, i))
                            tile_mm(t, [(bank(t)[:, :], ones, sqbuf[i])])

                def values(g):
                    b, t = BLOCK["v2", l, g], TILE["v2", l, g]
                    if l == 0:
                        gemm_tokens(t, b, NKV, hh[:, NQR:, :], hl[:, NQR:, :], lambda k: ("lat", l, NQR + k))
                        return
                    for i in range(NQ):
                        opened(t + i)
                    for k in range(ND):
                        take(b)
                        wh, wl = wblk(b, 2)
                        for i in range(NQ):
                            c = slice(i * P, i * P + P)
                            ins = three(bank(t + i)[:, 0:GKV * P], hh[:, k, c], hl[:, k, c], wh, wl, k == 0, k == ND - 1)
                            ends = [("full", t + i)] if k == ND - 1 else []
                            if i == NQ - 1 and (b + 1) % SLOT == SLOT - 1:
                                ends.append(("slot", b // SLOT))
                            if ends:
                                ins.then_inc(*pe.signals(*ends))
                        b += 2

                def scores2(u, j):
                    t = score_tile2(l, u, j)
                    q = slice(P * j, P * j + P)
                    eng.wait_ge(*pe.after("q2", l, u))
                    if u < MEM_HEADS:
                        eng.wait_ge(*pe.after("kmem", l))
                        tile_mm(t, [(bank(t)[:, 0:MEM], qmem[:, u, q], kmem[:, u, :])])
                        return
                    h = u - MEM_HEADS
                    if l == 1:
                        eng.wait_ge(*pe.after("kg", l, h // (H2 // GKV)))
                        tile_mm(t, [(bank(t)[:, :], gq[h % 2][:, q], kg[:, h // (H2 // GKV), :])])
                        return
                    eng.wait_ge(*pe.after("k2", l, u))
                    eng.wait_ge(*pe.after("pe2", l, u - h % 2))
                    eng.wait_ge(*pe.after("kpe", l))
                    r = slice(64 * (h % 2), 64 * (h % 2) + 64)
                    tile_mm(t, [(bank(t)[:, :], ring_q[h % 2][:, q], ring_k[h % 2][:, :]),
                                (bank(t)[:, :], ring_p[h // 2 % 2][r, q], kpe[r, :])])

                def turn2(u, j):
                    t = turn_tile2(l, u, j)
                    opened(t)
                    eng.wait_ge(*pe.after("p2", l, u, j))
                    for i in range(NMEM if u < MEM_HEADS else NQ):
                        ins = eng.transpose(bank(t)[:, P * i:P * i + P], sm2[:, j, P * i:P * i + P], ident)
                    ins.then_inc(*pe.signals(("full", t), ("turned2", l, u, j)))

                def prep_a(u):
                    if not prep_tiles(l, u):
                        return
                    t, b = TILE["pa", l, u], BLOCK["pa", l, u]
                    for kind, n in prep_tiles(l, u):
                        if l == 1:
                            gemm(t, b, n, hh, hl, hkey)
                        elif kind == "k":
                            gemm(t, b, n, hh[:, NQR:, :], hl[:, NQR:, :], lambda k: ("lat", l, NQR + k))
                        else:
                            gemm(t, b, n, hh, hl, lambda k: ("lat", l, k))
                        t += 1
                        b += n

                def prep_b(u):
                    for i, (key, buf, one, n, gain, turns) in enumerate(jobs(l, u)):
                        t = TILE["pb", l, u] + i
                        eng.wait_ge(*pe.after("jsq", *key))
                        tile_mm(t, [(bank(t)[:, :], one, sqbuf[place(u, i)])])

                for u in range(2):
                    prep_b(u)
                values(0)
                for j in range(NQ):
                    scores2(0, j)
                if l == 0:
                    values(1)
                for u in range(HEADS2):
                    if u + 2 < HEADS2:
                        prep_a(u + 2)
                    to = out_tile2(l, u)
                    h = u - MEM_HEADS
                    nk = NMEM if u < MEM_HEADS else NQ
                    for j in range(NQ + 1):
                        if j < NQ:
                            turn2(u, j)
                            if u + 1 < HEADS2:
                                scores2(u + 1, j)
                        if j == 0:
                            continue
                        if j == 1:
                            opened(to)
                            for i in range(nk):
                                eng.wait_ge(*pe.after(*(("vmem", l, i) if u < MEM_HEADS else ("v2", l, i))))
                        jj = j - 1
                        eng.wait_ge(*pe.after("pt2", l, u, jj))
                        for i in range(nk):
                            if u < MEM_HEADS:
                                v = vmem[:, i, u * P:u * P + P]
                            elif l == 0:
                                v = v2[:, i, h * P:h * P + P]
                            else:
                                g = h // (H2 // GKV)
                                v = vg[:, i, g * P:g * P + P]
                            ins = eng.matmul(bank(to)[:, P * jj:P * jj + P], v, pt2[(4 * u + jj) % 3][:, P * i:P * i + P],
                                             start=i == 0, stop=i == nk - 1)
                        ins.then_inc(*pe.signals(("pv2", l, u, jj), *([("full", to)] if jj == NQ - 1 else [])))
                        if j == 1 and u + 2 < HEADS2:
                            prep_b(u + 2)
                for m in range(ND):
                    gemm(TILE["wo2", l] + m, BLOCK["wo2", l] + MIX * m, MIX, ah, al,
                         lambda k: ("mix", l, (k + MEM_HEADS) % HEADS2))
                norm(n1 + 1)
                for half in range(2):
                    for p in range(NFF2 // 2):
                        t, b = TILE["up2", l, half, p], BLOCK["up2", l, half, p]
                        if half == p == 0:
                            gemm_abreast(t, b, 2, ND, hh, hl, lambda k: ("h", n1 + 1, k))
                            continue
                        gemm(t, b, 8, hh, hl, lambda k: ("h", n1 + 1, k))
                        gemm(t + 1, b + 8, 8, hh, hl, lambda k: ("h", n1 + 1, k))
                    if l == 0 and half:
                        mem_norm(1)
                    for m in range(ND):
                        gemm(TILE["down2", l, half] + m, BLOCK["down2", l, half] + 11 * m, 11, ah, al,
                             lambda k: ("ff2", l, half, k))

        @block.scalar
        def _(eng):
            act = Engine("act", sems, marks, known)
            nxt = [0]

            def ahead(b):
                while nxt[0] <= min(b // SLOT + 1, N_SLOTS - 1):
                    s = nxt[0]
                    eng.wait_ge(*act.after("landed", s))
                    if s >= HALF:
                        eng.wait_ge(*act.after("slot", s - HALF))
                    eng.activation(whi[:, s % HALF, :], raw[:, s % RAW, :], ACT.Copy).then_inc(*act.signals(("hi", s)))
                    eng.wait_ge(*act.previous)
                    nxt[0] += 1

            def read(t, out, func, *names, **kw):
                eng.wait_ge(*act.after("full", t))
                eng.activation(out, bank(t)[:, :], func, **kw).then_inc(*act.signals(("read", t), *names))
                eng.wait_ge(*act.previous)

            def log_and_exp():
                eng.preload_act_table_set("natural_log_exp_and_others")

            def inverse_root(t, out, n, *names, refined=False):
                w = out.shape[-1]
                eng.wait_ge(*act.after("full", t))
                eng.activation(out, bank(t)[:, 0:w], ACT.Ln, bias=bcol[:, 0:1],
                               scale=1.0 / n).then_inc(*act.signals(*([] if refined else [("read", t)])))
                eng.wait_ge(*act.previous)
                eng.activation(out, out, ACT.Exp, scale=-0.5).then_inc(*act.signals(*names))
                eng.wait_ge(*act.previous)

            def square(n, c):
                eng.wait_ge(*act.after("x", n, c))
                if n == 0:
                    out = nsq0[:, c, :]
                elif c == 0:
                    out = nsum[:, :]
                else:
                    if c >= 3:
                        eng.wait_ge(*act.after("ssum", n, c - 2))
                    out = nsq[:, c % 2, :]
                eng.activation(out, x[:, c, :], ACT.Square).then_inc(*act.signals(("sq", n, c)))
                eng.wait_ge(*act.previous)

            def norm(n, between=None):
                if n not in (N_FINAL, N_SECOND, N_SECOND + 2):
                    log_and_exp()
                for c in range(0 if n in (0, N_SECOND) else ND - 1, ND):
                    square(n, c)
                if between:
                    between()
                t = TILE["norm", n]
                inverse_root(t, nri[:, :], D, ("rms", n))
                if n == 0:
                    ahead(0)
                if n != N_FINAL:
                    for c in range(ND):
                        eng.wait_ge(*act.after("hf", n, c))
                        eng.activation(hh[:, c, :], nhf[:, c % 2, :], ACT.Copy).then_inc(*act.signals(("hh", n, c)))
                        eng.wait_ge(*act.previous)

            def rope(t, swap, key):
                eng.wait_ge(*act.after("full", t))
                for g in range(4):
                    o = g ^ 1
                    ins = eng.activation(swap[32 * g:32 * g + 32, :], bank(t)[32 * o:32 * o + 32, :], ACT.Copy)
                ins.then_inc(*act.signals(("swap",) + key))
                eng.wait_ge(*act.previous)

            eng.wait_ge(*act.after("bcol"))
            eng.wait_ge(*act.after("con_in"))
            eng.wait_ge(*act.after("par_in"))
            def mem_load(l):
                eng.dma_start(memf[:, :, :], A["mem"]).then_inc(sems["mem_in"], 16)
                if l == 1:
                    eng.wait_ge(*act.after("jend", "pe2", 0, HEADS2 - 2))
                eng.dma_start(tabc[:, :], A["tab"][l, 0]).then_inc(sems["tab_in"], 16)
                eng.dma_start(tabs[:, :], A["tab"][l, 1]).then_inc(sems["tab_in"], 16)

            def mem_squares(l):
                eng.wait_ge(*act.after("mem_in", l))
                for c in range(ND):
                    eng.activation(msq[:, c, :], memf[:, c, :], ACT.Square).then_inc(*act.signals(("msq", l, c)))
                    eng.wait_ge(*act.previous)

            def mem_high(l):
                for c in range(ND):
                    eng.wait_ge(*act.after("memn", l, c))
                    eng.activation(memh[:, c, :], memf[:, c, :], ACT.Copy).then_inc(*act.signals(("memh", l, c)))
                    eng.wait_ge(*act.previous)

            for l in range(DEPTH):
                norm(2 * l)
                if l == 0:
                    eng.wait_ge(*act.after("ang", 0))
                    eng.activation(tabs[:, :], rtab[:, 2, :], ACT.Sin).then_inc(*act.signals(("sin",)))
                    eng.wait_ge(*act.previous)
                    eng.wait_ge(*act.after("ang", 1))
                    eng.activation(tabc[:, :], rtab[:, 4, :], ACT.Sin).then_inc(*act.signals(("tabc",)))
                    eng.wait_ge(*act.previous)
                    eng.wait_ge(*act.after("lam_abs"))
                    eng.activation(spt[:, 1, :], spt[:, 0, :], ACT.Exp, scale=-1.0).then_inc(*act.signals(("lam_exp",)))
                    eng.wait_ge(*act.previous)
                ahead(BLOCK["qi", l] + 31 - SLOT)
                ahead(BLOCK["qi", l] + 31)
                for m in range(4):
                    if m >= 2:
                        eng.wait_ge(*act.after("qi", l, m - 2))
                    rope(TILE["qi", l] + m, rsw[:, m % 2, :], ("qi", l, m))
                ahead(BLOCK["ki", l] + 7)
                eng.wait_ge(*act.after("qi", l, 2))
                rope(TILE["ki", l], rsw[:, 0, :], ("ki", l))
                ahead(BLOCK["if", l] + 7)
                t = TILE["if", l]
                eng.wait_ge(*act.after("full", t))
                eng.activation(rows[0][:, :], bank(t)[0:4, :], ACT.Identity, bias=par[0:4, l * PLAYER + PCOL["i_bias"]:l * PLAYER + PCOL["i_bias"] + 1]).then_inc(*act.signals())
                eng.wait_ge(*act.previous)
                eng.activation(rows[1][:, :], bank(t)[32:36, :], ACT.Copy).then_inc(*act.signals(("if", l)))
                eng.wait_ge(*act.previous)
                eng.activation(wrow[:, :], bank(t)[64:72, :], ACT.Copy,
                               scale=float(A_HEADS) ** -0.5).then_inc(*act.signals(("read", t), ("wrow", l)))
                eng.wait_ge(*act.previous)
                t += 1
                eng.wait_ge(*act.after("full", t))
                eng.activation(wcol[:, :, :], bank(t)[:, 0:32].rearrange("p (a b) -> p a b", b=8), ACT.Copy).then_inc(*act.signals(("read", t), ("wcol", l)))
                eng.wait_ge(*act.previous)
                eng.wait_ge(*act.after("fabs", l))
                eng.activation(rows[3][:, :], rows[2][:, :], ACT.Exp, scale=-1.0).then_inc(*act.signals(("fexp", l)))
                eng.wait_ge(*act.previous)
                t = TILE["idx", l]
                for j in range(3, 0, -1):
                    for h in range(A_HEADS):
                        i = t - TILE["idx", l]
                        eng.wait_ge(*act.after("full", t))
                        if i >= 2:
                            eng.wait_ge(*act.after("acc", l, i - 2))
                        eng.activation(relu[:, i % 2, 0:P * (j + 1)], bank(t)[:, 0:P * (j + 1)],
                                                ACT.Relu, scale=float(HD) ** -0.5).then_inc(*act.signals(("read", t), ("relu", l, i)))
                        eng.wait_ge(*act.previous)
                        t += 1
                def mqk_silu(m):
                    eng.wait_ge(*act.after("conv", l, m))
                    dst = mq if m < 4 else mk
                    eng.activation(dst[:, m % 4, :], cacc[:, m % 2, :], ACT.Silu).then_inc(*act.signals(("mqk", l, m)))
                    eng.wait_ge(*act.previous)
                for m in range(8):
                    ahead(BLOCK["mqk", l] + 8 * m + 7)
                    t = TILE["mqk", l] + m
                    if m >= 2:
                        eng.wait_ge(*act.after("conv", l, m - 2))
                    read(t, cin[:, m % 2, 3:3 + S], ACT.Copy, ("cin", l, m))
                    if m:
                        mqk_silu(m - 1)
                mqk_silu(7)
                ahead(BLOCK["mv", l] + 31 - SLOT)
                for i in range(NQ):
                    if i == 0:
                        ahead(BLOCK["mv", l] + 31)
                    read(TILE["mv", l] + i, mv[:, i, :], ACT.Copy, ("mv", l, i))
                t = TILE["acol", l]
                eng.wait_ge(*act.after("full", t))
                eng.activation(acol[:, :, :], bank(t)[:, 0:16].rearrange("p (a b) -> p a b", b=4), ACT.Copy).then_inc(*act.signals(("read", t), ("acol", l)))
                eng.wait_ge(*act.previous)
                def m_open(h):
                    t = TILE["m1", l, h]
                    read(t, mnm[:, :], ACT.Copy, ("mnm", l, h))
                    read(t + 1, mex[:, :], ACT.Exp, ("mex", l, h))

                def m_weights(h, js):
                    eng.wait_ge(*act.after("mdm", l, h))
                    for j in js:
                        if j >= 2:
                            eng.wait_ge(*act.after("mp", l, h, j - 2))
                        bias = acol[:, j, h:h + 1]
                        ins = eng.activation(mwx[:, j % 2, P * j:P * j + P], mdm[:, j, :], ACT.Exp, bias=bias)
                        if j < NQ - 1:
                            ins = eng.activation(mwx[:, j % 2, P * j + P:], mnm[:, P * j + P:], ACT.Exp, bias=bias)
                        ins.then_inc(*act.signals(("mwx", l, h, j)))
                        eng.wait_ge(*act.previous)

                m_open(0)
                m_weights(0, range(NQ))
                for h in range(M_HEADS):
                    ahead(BLOCK["rx", l, h] + 7)
                    if h >= 2:
                        eng.wait_ge(*act.after("xc", l, h - 2))
                    read(TILE["rx", l, h], cin[:, h % 2, 3:3 + S], ACT.Copy, ("rcin", l, h))
                    ahead(BLOCK["mo", l, h] + 7)
                    read(TILE["mo", l, h], mo[:, :], ACT.Sigmoid, ("mo", l, h))
                    log_and_exp()
                    ahead(BLOCK["ak", l, h] + 7)
                    if h:
                        eng.wait_ge(*act.after("ak", l, h - 1))
                    rope(TILE["ak", l, h], aswap, ("ak", l, h))
                    if h == M_HEADS - 1:
                        ahead(BLOCK["rg", l, 0] + 7)
                    eng.wait_ge(*act.after("mhc", l, h))
                    eng.activation(mwx[:, 0, :], mq[:, h, :], ACT.Square).then_inc(*act.signals(("mhsq", l, h)))
                    eng.wait_ge(*act.previous)
                    if h + 1 < M_HEADS:
                        m_open(h + 1)
                    t = TILE["m4", l, h]
                    inverse_root(t, mdn[:, :], P, ("mstd", l, h))
                    if h + 1 < M_HEADS:
                        m_weights(h + 1, (0, 1))
                    eng.wait_ge(*act.after("yf", l, 0, h))
                    eng.activation(ah[:, h, :], yf[:, h, :], ACT.Copy).then_inc(*act.signals(("yh", l, 0, h)))
                    eng.wait_ge(*act.previous)
                    if h + 1 < M_HEADS:
                        m_weights(h + 1, (2, 3))
                for c in range(NBR):
                    ahead(BLOCK["rg", l, c] + 7)
                    read(TILE["rg", l, c], rg[:, c, :], ACT.Gelu_apprx_tanh, ("rg", l, c))
                    t = TILE["rgl", l, c]
                    if c:
                        eng.wait_ge(*act.after("rgdone", l, c - 1))
                    read(t, rt[:, 0, :], ACT.Sigmoid, ("rr", l, c), bias=pcol("rglru_b_a", l, c))
                    read(t + 1, rt[:, 1, :], ACT.Sigmoid, ("ri", l, c), bias=pcol("rglru_b_x", l, c))
                    eng.wait_ge(*act.after("spn"))
                    eng.activation(rt[:, 2, :], rt[:, 0, :], ACT.Tanh,
                                   scale=sp8[:, 4 * l + c:4 * l + c + 1]).then_inc(*act.signals(("rth", l, c)))
                    eng.wait_ge(*act.previous)
                    eng.activation(rt[:, 3, :], rt[:, 0, :], ACT.Exp,
                                   scale=spt[:, 5, 4 * l + c:4 * l + c + 1]).then_inc(*act.signals(("ra", l, c)))
                    eng.wait_ge(*act.previous)
                    eng.wait_ge(*act.after("rq", l, c))
                    eng.activation(rt[:, 5, :], rt[:, 4, :], ACT.Sqrt, scale=2.0).then_inc(*act.signals(("rs", l, c)))
                    eng.wait_ge(*act.previous)
                    ahead(BLOCK["aq", l, c] + (7 if c < NBR - 1 else SLOT - 1))
                    if c >= 2:
                        eng.wait_ge(*act.after("aq", l, c - 2))
                    rope(TILE["aq", l, c], rsw2[:, c % 2, :], ("aq", l, c))
                ahead(BLOCK["av", l] + 31 - SLOT)
                for i in range(NQ):
                    if i == 0:
                        ahead(BLOCK["av", l] + 31)
                    read(TILE["av", l] + i, av[i][:, :], ACT.Copy, ("av", l, i))

                n_sig = [0]

                def branch(b, m):
                    t, blk = TILE["br", l, b, m], BLOCK["br", l, b, m]
                    ahead(blk + 7)
                    if n_sig[0]:
                        eng.wait_ge(*act.after("merged", l, (8 * b + m - 1) // 8, (m - 1) % 8))
                    read(t, sig[:, :], ACT.Sigmoid, ("sig", l, b, m))
                    n_sig[0] += 1
                    ahead(blk + 11)

                def split_y(b):
                    for k in range(4):
                        if b == 2:
                            eng.wait_ge(*act.after("yfo", l, 2 * k))
                            eng.wait_ge(*act.after("yfo", l, 2 * k + 1))
                        else:
                            eng.wait_ge(*act.after("yf", l, b, k))
                        if k == 0:
                            eng.wait_ge(*act.after("full", TILE["br", l, b - 1, ND - 1] + 1))
                        eng.activation(ah[:, k, :], yf[:, k, :], ACT.Copy).then_inc(*act.signals(("yh", l, b, k)))
                        eng.wait_ge(*act.previous)

                def exp(h, j):
                    eng.wait_ge(*act.after("sm", l, h, j))
                    eng.activation(sm[:, j, 0:P * (j + 1)], sm[:, j, 0:P * (j + 1)], ACT.Exp,
                                   bias=nmx[:, j:j + 1], scale=-1.0,
                                   accum_out=rsum[:, j:j + 1]).then_inc(*act.signals(("e", l, h, j)))
                    eng.wait_ge(*act.previous)

                for m in range(ND):
                    branch(0, m)
                split_y(1)
                for j in range(NQ):
                    exp(0, j)
                for h in range(A_HEADS):
                    branch(1, h)
                    for j in range(NQ):
                        t = turn_tile(l, h, j)
                        u = 4 * h + j
                        if u >= 3:
                            eng.wait_ge(*act.after("pv", l, (u - 3) // 4, (u - 3) % 4))
                        eng.wait_ge(*act.after("full", t))
                        eng.activation(pt[:, u % 3, 0:P * (j + 1)], bank(t)[:, 0:P * (j + 1)], ACT.Copy).then_inc(*act.signals(("read", t), ("pt", l, h, j)))
                        eng.wait_ge(*act.previous)
                        if j and h + 1 < A_HEADS:
                            exp(h + 1, j - 1)
                    if h + 1 < A_HEADS:
                        exp(h + 1, NQ - 1)
                    t = out_tile(l, h)
                    r = slice(64 * (h % 2), 64 * (h % 2) + 64)
                    eng.wait_ge(*act.after("full", t))
                    eng.activation(yf[r, h // 2, :], bank(t)[r, :], ACT.Copy).then_inc(*act.signals(("read", t), ("yfo", l, h)))
                    eng.wait_ge(*act.previous)
                for m in range(ND):
                    ahead(BLOCK["gc", l] + 8 * m + 7)
                    read(TILE["gc", l] + m, sigc[:, m, :], ACT.Sigmoid, ("sigc", l, m))
                split_y(2)
                for m in range(ND):
                    ahead(BLOCK["bc", l] + 4 * m + 3)
                    eng.wait_ge(*act.after("merf", l, m))
                    if m == 0:
                        eng.wait_ge(*act.after("full", TILE["gc", l] + ND - 1))
                    eng.activation(hh[:, m, :], mer[:, m, :], ACT.Copy).then_inc(*act.signals(("merh", l, m)))
                    eng.wait_ge(*act.previous)
                for m in range(ND):
                    ahead(BLOCK["wo", l] + 8 * m + 7)
                    if m:
                        square(2 * l + 1, m - 1)
                norm(2 * l + 1)
                for half in range(2):
                    for p in range(NFF // 2):
                        if l == DEPTH - 1 and half and p == 0:
                            mem_load(0)
                        if l == DEPTH - 1 and half and p == NFF // 2 - 3:
                            mem_squares(0)
                        t, b = TILE["up", l, half, p], BLOCK["up", l, half, p]
                        i = half * NFF // 2 + p
                        ahead(b + (15 if i == 0 else 7))
                        if i >= 2:
                            eng.wait_ge(*act.after("fconv", l, i - 2))
                        read(t, cin[:, i % 2, 3:3 + S], ACT.Copy, ("fcin", l, i))
                        ahead(b + 15)
                        eng.wait_ge(*act.after("fconv", l, i))
                        if i >= 2:
                            eng.wait_ge(*act.after("fhf", l, i - 2))
                        eng.activation(fga[:, i % 2, :], cacc[:, i % 2, :], ACT.Gelu_apprx_tanh).then_inc(*act.signals(("fga", l, i)))
                        eng.wait_ge(*act.previous)
                        if p:
                            eng.wait_ge(*act.after("fhf", l, i - 1))
                            eng.activation(ah[:, p - 1, :], fhf[:, (i - 1) % 2, :], ACT.Copy).then_inc(*act.signals(("ffh", l, half, p - 1)))
                            eng.wait_ge(*act.previous)
                        elif half:
                            eng.wait_ge(*act.after("full", TILE["down", l, 0] + ND - 1))
                    p = NFF // 2
                    i = half * NFF // 2 + p
                    eng.wait_ge(*act.after("fhf", l, i - 1))
                    eng.activation(ah[:, p - 1, :], fhf[:, (i - 1) % 2, :], ACT.Copy).then_inc(*act.signals(("ffh", l, half, p - 1)))
                    eng.wait_ge(*act.previous)
                    for m in range(ND):
                        ahead(BLOCK["down", l, half] + 12 * m + 11)
                        if l == DEPTH - 1 and half and m == 0:
                            log_and_exp()
                            inverse_root(TILE["memnorm", 0], mri[:, :], D, ("mrms", 0))
                        if l == DEPTH - 1 and half and m == 4:
                            mem_high(0)
                        if half and m:
                            square(2 * l + 2, m - 1)

            sq_prev = {}

            def job_sq(i, key, raw_):
                if i in sq_prev:
                    eng.wait_ge(*act.after("jn", *sq_prev[i]))
                sq_prev[i] = key
                eng.activation(sqbuf[i], raw_, ACT.Square).then_inc(*act.signals(("jsq",) + key))
                eng.wait_ge(*act.previous)

            def job_std(i, t, key, n):
                if job_prev[i % 2]:
                    eng.wait_ge(*act.after(*job_prev[i % 2]))
                inverse_root(t, jst[:, i % 2, :], n, ("jstd",) + key, refined=key[0] in ("kpe", "kg"))
                job_prev[i % 2] = ("jend",) + key

            def job_swap(key, buf):
                eng.wait_ge(*act.after("jn", *key))
                for g in range(4):
                    o = g ^ 1
                    ins = eng.activation(swap2[32 * g:32 * g + 32, :], buf[32 * o:32 * o + 32, :], ACT.Copy)
                ins.then_inc(*act.signals(("jswap",) + key))
                eng.wait_ge(*act.previous)

            job_prev = [None, None]
            for l in range(DEPTH):
                n1 = N_SECOND + 2 * l
                def mem_keys():
                    for m in range(MEM_HEADS):
                        ahead(BLOCK["memk", l] + 8 * m + 7)
                        t = TILE["memk", l] + m
                        eng.wait_ge(*act.after("full", t))
                        eng.activation(kraw[:, m // 2, MEM * (m % 2):MEM * (m % 2) + MEM], bank(t)[:, 0:MEM],
                                       ACT.Copy).then_inc(*act.signals(("read", t), ("kraw", l, m)))
                        eng.wait_ge(*act.previous)
                        if m % 2:
                            eng.activation(ksq[:, m // 2, :], kraw[:, m // 2, :], ACT.Square).then_inc(*act.signals(("ksq", l, m // 2)))
                            eng.wait_ge(*act.previous)
                    ahead(BLOCK["memv", l] + SLOT - 1)

                def mem_values():
                    ahead(BLOCK["memv", l] + 31)
                    eng.wait_ge(*act.after("full", TILE["memv", l] + NMEM - 1))
                    for i in range(NMEM):
                        read(TILE["memv", l] + i, vmem[:, i, :], ACT.Copy, ("vmem", l, i))
                    for i in range(2):
                        inverse_root(TILE["memkst", l] + i, kst[:, i, :], P, ("kst", l, i), refined=True)

                if l == 0:
                    norm(N_FINAL, mem_keys)
                    norm(n1, mem_values)
                else:
                    norm(n1, mem_keys)
                    mem_values()
                if l == 0:
                    ahead(BLOCK["cq", l] + ND * NQR - 1 - SLOT)
                    for c in range(NQR + NKV):
                        ahead(BLOCK["cq", l] + ND * max(c + 1, NQR) - 1)
                        read(TILE["cq", l] + c, cqr[:, c, :], ACT.Copy, ("craw", l, c))
                        eng.activation(cqs[:, c, :], cqr[:, c, :], ACT.Square).then_inc(*act.signals(("csq", l, c)))
                        eng.wait_ge(*act.previous)
                    ahead(BLOCK["kpe", l] + ND - 1)
                    read(TILE["kpe", l], kpe[:, :], ACT.Copy, ("kperaw", l))
                    job_sq(0, ("kpe", l), kpe[:, :])
                    for i, (name, n) in enumerate((("cqst", QR), ("ckvst", KVR))):
                        inverse_root(TILE[name, l], cqi[:, i, :], n, ("cstd", l, i), refined=True)
                    job_std(0, TILE["kst", l], ("kpe", l), ROPE)
                else:
                    for m in range(GKV):
                        ahead(BLOCK["kg", l] + ND * GKV - 1)
                        read(TILE["kg", l] + m, kg[:, m, :], ACT.Copy)
                        job_sq(m, ("kg", l, m), kg[:, m, :])
                eng.wait_ge(*act.after("tab_in", l))
                for m in range(MEM_HEADS):
                    ahead(BLOCK["qmem", l] + ND * m + ND - 1)
                    read(qmem_tile(l, m), qmem[:, m, :], ACT.Copy, ("qmemraw", l, m))
                    if l == 1 and m == 0:
                        for i in range(GKV):
                            job_std(i, TILE["kst", l] + i, ("kg", l, i), P)
                    if m < 2:
                        job_sq(m, (("q2", l, m)), qmem[:, m, :])
                    if l == 0 and m == 0:
                        job_swap(("kpe", l), kpe[:, :])
                    if l == 1 and m < GKV:
                        job_swap(("kg", l, m), kg[:, m, :])

                def latent_high(c):
                    eng.wait_ge(*act.after("clat", l, c))
                    eng.activation(hh[:, c, :], cqr[:, c, :], ACT.Copy).then_inc(*act.signals(("lath", l, c)))
                    eng.wait_ge(*act.previous)

                if l == 0:
                    for c in range(NQR, NQR + NKV):
                        latent_high(c)

                def prep_a(u):
                    js = jobs(l, u)
                    if u < MEM_HEADS:
                        job_sq(place(u, 0), js[0][0], js[0][1])
                        return
                    b = BLOCK["pa", l, u]
                    h = u - MEM_HEADS
                    for i, (kind, n) in enumerate(prep_tiles(l, u)):
                        b += n
                        ahead(b - 1)
                        if h >= 2:
                            eng.wait_ge(*act.after("full", score_tile2(l, u - 2, NQ - 1)))
                        read(TILE["pa", l, u] + i, js[i][1], ACT.Copy)
                        job_sq(i, js[i][0], js[i][1])

                def prep_std(u, part):
                    for i, (key, buf, one, n, gain, turns) in enumerate(jobs(l, u)):
                        if i // 2 == part:
                            job_std(place(u, i), TILE["pb", l, u] + i, key, n)

                def prep_swap(u):
                    for key, buf, one, n, gain, turns in jobs(l, u):
                        if turns:
                            job_swap(key, buf)

                def exp2(u, j):
                    n = MEM if u < MEM_HEADS else S
                    t = score_tile2(l, u, j)
                    eng.wait_ge(*act.after("nmx2", l, u, j))
                    eng.activation(sm2[:, j, 0:n], bank(t)[:, 0:n], ACT.Exp, bias=nmx[:, j:j + 1],
                                   accum_out=rsum[:, j:j + 1]).then_inc(*act.signals(("read", t), ("e2", l, u, j)))
                    eng.wait_ge(*act.previous)

                def read_values(g):
                    ahead(BLOCK["v2", l, g] + (7 if l == 0 else 15))
                    for j in range(NQ):
                        t = TILE["v2", l, g] + j
                        if l == 0:
                            read(t, v2[:, j, g * BR:g * BR + BR], ACT.Copy, *([("v2", l, j)] if g else []))
                        else:
                            eng.wait_ge(*act.after("full", t))
                            eng.activation(vg[:, j, :], bank(t)[:, 0:GKV * P],
                                           ACT.Copy).then_inc(*act.signals(("read", t), ("v2", l, j)))
                            eng.wait_ge(*act.previous)

                for u in range(2):
                    prep_std(u, 0)
                if l == 0:
                    for c in range(NQR):
                        latent_high(c)
                read_values(0)
                for j in range(NQ):
                    exp2(0, j)
                if l == 0:
                    read_values(1)
                for u in range(HEADS2):
                    n = MEM if u < MEM_HEADS else S
                    if u + 2 < HEADS2:
                        prep_a(u + 2)
                    for j in range(NQ):
                        t = turn_tile2(l, u, j)
                        i = 4 * u + j
                        if i >= 3:
                            eng.wait_ge(*act.after("pv2", l, (i - 3) // 4, (i - 3) % 4))
                        eng.wait_ge(*act.after("full", t))
                        eng.activation(pt2[i % 3][:, 0:n], bank(t)[:, 0:n], ACT.Copy).then_inc(*act.signals(("read", t), ("pt2", l, u, j)))
                        eng.wait_ge(*act.previous)
                        if j and u + 1 < HEADS2:
                            exp2(u + 1, j - 1)
                        if 0 < j < 3 and u + 2 < HEADS2:
                            prep_std(u + 2, j - 1)
                    t = out_tile2(l, u)
                    c = (u - MEM_HEADS) % HEADS2
                    eng.wait_ge(*act.after("full", t))
                    eng.activation(ah[:, c, :], bank(t)[:, :], ACT.Copy).then_inc(*act.signals(("mixh", l, u)))
                    eng.wait_ge(*act.previous)
                    if u + 1 < HEADS2:
                        exp2(u + 1, NQ - 1)
                    if u + 2 < HEADS2:
                        prep_swap(u + 2)
                for m in range(ND):
                    ahead(BLOCK["wo2", l] + MIX * m + MIX - 1)
                    if m:
                        square(n1 + 1, m - 1)
                norm(n1 + 1)
                for half in range(2):
                    for p in range(NFF2 // 2):
                        if l == 0 and half and p == 0:
                            mem_load(1)
                        if l == 0 and half and p == NFF2 // 2 - 3:
                            mem_squares(1)
                        t, b = TILE["up2", l, half, p], BLOCK["up2", l, half, p]
                        i = half * NFF2 // 2 + p
                        ahead(b + (15 if i == 0 else 7))
                        if i >= 2:
                            eng.wait_ge(*act.after("fhf2", l, i - 2))
                        read(t, fga2[:, i % 2, :], ACT.Silu, ("fga2", l, i))
                        ahead(b + 15)
                        if p:
                            eng.wait_ge(*act.after("fhf2", l, i - 1))
                            eng.activation(ah[:, p - 1, :], fhf2[:, (i - 1) % 2, :], ACT.Copy).then_inc(*act.signals(("ffh2", l, half, p - 1)))
                            eng.wait_ge(*act.previous)
                        elif half:
                            eng.wait_ge(*act.after("full", TILE["down2", l, 0] + ND - 1))
                    p = NFF2 // 2
                    i = half * NFF2 // 2 + p
                    eng.wait_ge(*act.after("fhf2", l, i - 1))
                    eng.activation(ah[:, p - 1, :], fhf2[:, (i - 1) % 2, :], ACT.Copy).then_inc(*act.signals(("ffh2", l, half, p - 1)))
                    eng.wait_ge(*act.previous)
                    for m in range(ND):
                        ahead(BLOCK["down2", l, half] + 11 * m + 10)
                        if l == 0 and half and m == 0:
                            log_and_exp()
                            inverse_root(TILE["memnorm", 1], mri[:, :], D, ("mrms", 1))
                        if l == 0 and half and m == 4:
                            mem_high(1)
                        if l == 0 and half and m:
                            square(n1 + 2, m - 1)

        @block.vector
        def _(eng):
            dve = Engine("dve", sems, marks, known)
            nxt = [0]

            def ahead(b):
                while nxt[0] <= min(b // SLOT + 1, N_SLOTS - 1):
                    s = nxt[0]
                    eng.wait_ge(*dve.after("hi", s))
                    eng.tensor_tensor(wlo[:, s % HALF, :], raw[:, s % RAW, :],
                                               whi[:, s % HALF, :].bitcast(F32), ALU.subtract).then_inc(*dve.signals(("lo", s)))
                    eng.wait_ge(*dve.previous)
                    nxt[0] += 1

            def lo(out, full, hi, *names):
                eng.tensor_tensor(out, full, hi.bitcast(F32), ALU.subtract).then_inc(*dve.signals(*names))
                eng.wait_ge(*dve.previous)

            def add_squares(n, c):
                if c >= 1:
                    eng.wait_ge(*dve.after("sq", n, c))
                    eng.tensor_tensor(nsum[:, :], nsum[:, :], nsq[:, c % 2, :], ALU.add).then_inc(*dve.signals(("ssum", n, c)))
                    eng.wait_ge(*dve.previous)

            def norm(n):
                eng.wait_ge(*dve.after("rms", n))
                last = n == N_FINAL
                for c in range(ND + 1):
                    if n == 0 and c == 2:
                        ahead(0)
                    if c < ND:
                        if last:
                            eng.scalar_tensor_tensor(out=x[:, c, :], in0=x[:, c, :], scalar=norm_gain(n, c),
                                                              in1=nri[:, :], op0=ALU.mult, op1=ALU.mult).then_inc(*dve.signals(("x", N_SECOND, c)))
                            eng.wait_ge(*dve.previous)
                            add_squares(N_SECOND, c - 1)
                            continue
                        eng.scalar_tensor_tensor(out=nhf[:, c % 2, :], in0=x[:, c, :], scalar=norm_gain(n, c),
                                                          in1=nri[:, :], op0=ALU.mult, op1=ALU.mult).then_inc(*dve.signals(("hf", n, c)))
                        eng.wait_ge(*dve.previous)
                    if c and not last:
                        eng.wait_ge(*dve.after("hh", n, c - 1))
                        lo(hl[:, c - 1, :], nhf[:, (c - 1) % 2, :], hh[:, c - 1, :], ("h", n, c - 1))

            def rope(t, swap, tmp, out, key, *names):
                eng.wait_ge(*dve.after("swap", *key))
                eng.wait_ge(*dve.after("tabc"))
                eng.tensor_tensor(tmp, bank(t)[:, :], tabc[:, :], ALU.mult).then_inc(*dve.signals(("read", t)))
                eng.wait_ge(*dve.previous)
                eng.tensor_tensor(swap, swap, tabs[:, :], ALU.mult).then_inc(*dve.signals())
                eng.wait_ge(*dve.previous)
                eng.tensor_tensor(out, tmp, swap, ALU.add).then_inc(*dve.signals(key, *names))
                eng.wait_ge(*dve.previous)

            def log1p(out, y, t0, t1):
                eng.tensor_scalar(t0, y, 2.0, None, ALU.add).then_inc(*dve.signals())
                eng.wait_ge(*dve.previous)
                eng.reciprocal(t1, t0).then_inc(*dve.signals())
                eng.wait_ge(*dve.previous)
                eng.tensor_tensor(t0, y, t1, ALU.mult).then_inc(*dve.signals())
                eng.wait_ge(*dve.previous)
                eng.tensor_tensor(t1, t0, t0, ALU.mult).then_inc(*dve.signals())
                eng.wait_ge(*dve.previous)
                eng.tensor_scalar(out, t1, 1.0 / 15, None, ALU.mult).then_inc(*dve.signals())
                eng.wait_ge(*dve.previous)
                for n in (13, 11, 9, 7, 5, 3):
                    eng.scalar_tensor_tensor(out=out, in0=out, scalar=1.0 / n, in1=t1, op0=ALU.add, op1=ALU.mult).then_inc(*dve.signals())
                    eng.wait_ge(*dve.previous)
                eng.tensor_scalar(out, out, 1.0, 2.0, ALU.add, ALU.mult).then_inc(*dve.signals())
                eng.wait_ge(*dve.previous)
                eng.tensor_tensor(out, out, t0, ALU.mult).then_inc(*dve.signals())
                eng.wait_ge(*dve.previous)

            def conv(taps, wcol, bcol_, src, dst, n, *names):
                first = 4 - taps
                eng.tensor_scalar(dst, src[:, first:first + S], wcol(0), bcol_, ALU.mult, ALU.add).then_inc(*dve.signals())
                eng.wait_ge(*dve.previous)
                for j in range(1, taps):
                    ins = eng.scalar_tensor_tensor(out=dst, in0=src[:, first + j:first + j + S], scalar=wcol(j),
                                                   in1=dst, op0=ALU.mult, op1=ALU.add)
                    if j < taps - 1:
                        ins.then_inc(*dve.signals())
                        eng.wait_ge(*dve.previous)
                    else:
                        ins.then_inc(*dve.signals(*names))
                        eng.wait_ge(*dve.previous)

            eng.memset(bcol[:, 0:1], EPS).then_inc(*dve.signals(("bcol",)))
            eng.wait_ge(*dve.previous)
            eng.memset(cin[:, :, 0:3], 0.0).then_inc(*dve.signals())
            eng.wait_ge(*dve.previous)
            for c in range(ND):
                marks[("x", 0, c)] = (f"x_in{2 * c // ND}", 16)
            eng.wait_ge(*dve.after("par_in"))
            def mem_split(l):
                eng.wait_ge(*dve.after("mrms", l))
                for c in range(ND):
                    eng.scalar_tensor_tensor(out=memf[:, c, :], in0=memf[:, c, :], scalar=par[:, PCOL2["mem_norm"] + c:PCOL2["mem_norm"] + c + 1],
                                                  in1=mri[:, :], op0=ALU.mult, op1=ALU.mult).then_inc(*dve.signals(("memn", l, c)))
                    eng.wait_ge(*dve.previous)
                    if c:
                        eng.wait_ge(*dve.after("memh", l, c - 1))
                        lo(meml[:, c - 1, :], memf[:, c - 1, :], memh[:, c - 1, :], ("mem", l, c - 1))
                eng.wait_ge(*dve.after("memh", l, ND - 1))
                lo(meml[:, ND - 1, :], memf[:, ND - 1, :], memh[:, ND - 1, :], ("mem", l, ND - 1))

            for l in range(DEPTH):
                if l == 0:
                    eng.wait_ge(*dve.after("con_in"))
                    eng.wait_ge(*dve.after("pos_in"))
                    ang = rtab[:, 0, :]
                    eng.tensor_copy(rtab[:, 1, :], pos_i[:, :]).then_inc(*dve.signals())
                    eng.wait_ge(*dve.previous)
                    eng.tensor_scalar(ang, rtab[:, 1, :], con[:, C_INV:C_INV + 1], None, ALU.mult).then_inc(*dve.signals())
                    eng.wait_ge(*dve.previous)
                    two_pi = 2.0 * np.pi
                    c1 = 6.28125
                    c2 = float(np.float32(np.round((two_pi - c1) * 2 ** 21) / 2 ** 21))
                    c3 = float(two_pi - c1 - c2)
                    magic = float(3 << 22)
                    for i, shift in enumerate((0.0, 0.25)):
                        kk, r = rtab[:, 3, :], rtab[:, 2 + 2 * i, :]
                        eng.tensor_scalar(kk, ang, 1.0 / two_pi, shift, ALU.mult, ALU.add).then_inc(*dve.signals())
                        eng.wait_ge(*dve.previous)
                        eng.tensor_scalar(kk, kk, magic, None, ALU.add).then_inc(*dve.signals())
                        eng.wait_ge(*dve.previous)
                        eng.tensor_scalar(kk, kk, -magic, None, ALU.add).then_inc(*dve.signals())
                        eng.wait_ge(*dve.previous)
                        eng.scalar_tensor_tensor(out=r, in0=kk, scalar=-c1, in1=ang, op0=ALU.mult, op1=ALU.add).then_inc(*dve.signals())
                        eng.wait_ge(*dve.previous)
                        eng.scalar_tensor_tensor(out=r, in0=kk, scalar=-c2, in1=r, op0=ALU.mult, op1=ALU.add).then_inc(*dve.signals())
                        eng.wait_ge(*dve.previous)
                        eng.scalar_tensor_tensor(out=r, in0=kk, scalar=-c3, in1=r, op0=ALU.mult, op1=ALU.add).then_inc(*dve.signals())
                        eng.wait_ge(*dve.previous)
                        if i:
                            eng.tensor_scalar(r, r, float(np.pi / 2), None, ALU.add).then_inc(*dve.signals())
                            eng.wait_ge(*dve.previous)
                        pi = float(np.nextafter(np.float32(np.pi), np.float32(0)))
                        eng.tensor_scalar(r, r, pi, -pi, ALU.min, ALU.max).then_inc(*dve.signals(("ang", i)))
                        eng.wait_ge(*dve.previous)
                if l:
                    add_squares(2 * l, ND - 1)
                norm(2 * l)
                if l == 0:
                    eng.wait_ge(*dve.after("sin"))
                    eng.tensor_scalar(tabs[:, :], tabs[:, :], con[:, C_SGN:C_SGN + 1], None, ALU.mult).then_inc(*dve.signals())
                    eng.wait_ge(*dve.previous)
                    for name, i, v in (("memq", 0, HD_SCALE), ("memq", 1, HD_SCALE), ("mla_q", 0, MLA_SCALE),
                                       ("mla_qpe", 0, MLA_SCALE), ("gqa_q", 0, HD_SCALE)):
                        c = par[:, PCOL2[name] + i:PCOL2[name] + i + 1]
                        eng.tensor_scalar(c, c, v, None, ALU.mult).then_inc(*dve.signals())
                        eng.wait_ge(*dve.previous)
                    for d in range(DEPTH):
                        lam = pcol("rglru_lambda", d, 0, 4)
                        eng.scalar_tensor_tensor(out=spt[:, 0, 4 * d:4 * d + 4], in0=lam, scalar=-1.0, in1=lam,
                                                      op0=ALU.mult, op1=ALU.max).then_inc(*dve.signals(*([("lam_abs",)] if d == DEPTH - 1 else [])))
                        eng.wait_ge(*dve.previous)
                        eng.tensor_scalar(spt[:, 4, 4 * d:4 * d + 4], pcol("rglru_lambda", d, 0, 4), 0.0, -1.0, ALU.min, ALU.mult).then_inc(*dve.signals())
                        eng.wait_ge(*dve.previous)
                    eng.wait_ge(*dve.after("lam_exp"))
                    log1p(spt[:, 5, :], spt[:, 1, :], spt[:, 2, :], spt[:, 3, :])
                    eng.tensor_tensor(spt[:, 5, :], spt[:, 5, :], spt[:, 4, :], ALU.add).then_inc(*dve.signals())
                    eng.wait_ge(*dve.previous)
                    eng.tensor_scalar(sp8[:, :], spt[:, 5, :], 8.0, None, ALU.mult).then_inc(*dve.signals())
                    eng.wait_ge(*dve.previous)
                    eng.tensor_scalar(spt[:, 5, :], spt[:, 5, :], -8.0, None, ALU.mult).then_inc(*dve.signals(("spn",)))
                    eng.wait_ge(*dve.previous)
                ahead(BLOCK["qi", l] + 31 - SLOT)
                ahead(BLOCK["qi", l] + 31)
                for m in range(4):
                    rope(TILE["qi", l] + m, rsw[:, m % 2, :], rt1[:, m % 2, :], qi[:, m, :], ("qi", l, m))
                ahead(BLOCK["ki", l] + 7)
                rope(TILE["ki", l], rsw[:, 0, :], rt1[:, 0, :], ki[:, :], ("ki", l))
                ahead(BLOCK["if", l] + 7)
                eng.wait_ge(*dve.after("if", l))
                R = lambda i: rows[i][:, :]
                eng.tensor_scalar(R(1), R(1), par[0:4, l * PLAYER + PCOL["f_bias"]:l * PLAYER + PCOL["f_bias"] + 1], None, ALU.add).then_inc(*dve.signals())
                eng.wait_ge(*dve.previous)
                eng.scalar_tensor_tensor(out=R(2), in0=R(1), scalar=-1.0, in1=R(1), op0=ALU.mult, op1=ALU.max).then_inc(*dve.signals(("fabs", l)))
                eng.wait_ge(*dve.previous)
                eng.tensor_scalar(R(1), R(1), 0.0, None, ALU.min).then_inc(*dve.signals())
                eng.wait_ge(*dve.previous)
                eng.wait_ge(*dve.after("fexp", l))
                log1p(R(2), R(3), R(4), R(5))
                eng.tensor_tensor(R(1), R(1), R(2), ALU.subtract).then_inc(*dve.signals())
                eng.wait_ge(*dve.previous)
                eng.memset(R(4), 1.0).then_inc(*dve.signals())
                eng.wait_ge(*dve.previous)
                eng.tensor_tensor_scan(R(2), R(4), R(1), 0.0, ALU.mult, ALU.add).then_inc(*dve.signals())
                eng.wait_ge(*dve.previous)
                eng.tensor_tensor(R(0), R(0), R(2), ALU.subtract).then_inc(*dve.signals(("arow", l)))
                eng.wait_ge(*dve.previous)
                eng.memset(R(4), 0.0).then_inc(*dve.signals())
                eng.wait_ge(*dve.previous)
                eng.tensor_tensor_scan(R(3), R(4), R(0), 0.0, ALU.add, ALU.max).then_inc(*dve.signals())
                eng.wait_ge(*dve.previous)
                eng.tensor_scalar(negm[:, :], R(3), -1.0, None, ALU.mult).then_inc(*dve.signals(("negm", l)))
                eng.wait_ge(*dve.previous)
                eng.scalar_tensor_tensor(out=negg[:, :], in0=R(2), scalar=-1.0, in1=R(3),
                                              op0=ALU.mult, op1=ALU.subtract).then_inc(*dve.signals(("negg", l)))
                eng.wait_ge(*dve.previous)
                eng.wait_ge(*dve.after("wcol", l))
                i = 0
                for j in range(3, 0, -1):
                    w = work[:, j - 1, 0:P * (j + 1)]
                    for h in range(A_HEADS):
                        eng.wait_ge(*dve.after("relu", l, i))
                        src = relu[:, i % 2, 0:P * (j + 1)]
                        ws = wcol[:, j, h:h + 1]
                        if h == 0:
                            eng.tensor_scalar(w, src, ws, None, ALU.mult).then_inc(*dve.signals(("acc", l, i)))
                            eng.wait_ge(*dve.previous)
                        else:
                            eng.scalar_tensor_tensor(out=w, in0=src, scalar=ws, in1=w, op0=ALU.mult, op1=ALU.add).then_inc(*dve.signals(("acc", l, i)))
                            eng.wait_ge(*dve.previous)
                        i += 1
                    d = work[:, j - 1, P * j:P * j + P]
                    eng.scalar_tensor_tensor(out=d, in0=mask_qk, scalar=float(UNSEEN / NEG), in1=d,
                                                  op0=ALU.mult, op1=ALU.add).then_inc(*dve.signals())
                    eng.wait_ge(*dve.previous)

                rounds = [(j, r) for j in (3, 2, 1) for r in range(TOPK // 8)]

                def select(n):
                    for _ in range(n):
                        if not rounds:
                            return
                        j, r = rounds.pop(0)
                        w, t8 = work[:, j - 1, 0:P * (j + 1)], top[:, j - 1, :]
                        eng.max(t8, w).then_inc(*dve.signals())
                        eng.wait_ge(*dve.previous)
                        eng.match_replace(w, t8, w, TAKEN).then_inc(*dve.signals())
                        eng.wait_ge(*dve.previous)
                        if r == TOPK // 8 - 1:
                            eng.tensor_scalar(w, w, 0.5 * (UNSEEN + TAKEN), NEG, ALU.is_gt, ALU.mult).then_inc(*dve.signals())
                            eng.wait_ge(*dve.previous)

                for m in range(8):
                    ahead(BLOCK["mqk", l] + 8 * m + 7)
                    eng.wait_ge(*dve.after("cin", l, m))
                    if m >= 2:
                        eng.wait_ge(*dve.after("mqk", l, m - 2))
                    conv(4, lambda j: pcol("mlstm_conv_w", l, 8 * j + m), pcol("mlstm_conv_b", l, m),
                         cin[:, m % 2, :], cacc[:, m % 2, :], m, ("conv", l, m))
                    select(1)
                ahead(BLOCK["mv", l] + 31 - SLOT)
                select(8)
                ahead(BLOCK["mv", l] + 31)
                select(4)
                def m_masked(h):
                    eng.wait_ge(*dve.after("mnm", l, h))
                    eng.tensor_tensor(mdm[:, :, :], mnm[:, :].rearrange("p (a b) -> p a b", b=P),
                                           mask_st.unsqueeze(1).to_broadcast([P, NQ, P]), ALU.add).then_inc(*dve.signals(("mdm", l, h)))
                    eng.wait_ge(*dve.previous)

                m_masked(0)
                for h in range(M_HEADS):
                    t = TILE["m1", l, h] + 2
                    for j in range(NQ):
                        eng.wait_ge(*dve.after("mwx", l, h, j))
                        eng.wait_ge(*dve.after("full", t + j))
                        eng.scalar_tensor_tensor(out=mp[:, j, P * j:], in0=bank(t + j)[:, P * j:], scalar=M_SCALE,
                                                          in1=mwx[:, j % 2, P * j:], op0=ALU.mult, op1=ALU.mult).then_inc(*dve.signals(("read", t + j), ("mp", l, h, j)))
                        eng.wait_ge(*dve.previous)
                    ahead(BLOCK["rx", l, h] + 7)
                    ahead(BLOCK["mo", l, h] + 7)
                    t = TILE["m2", l, h]
                    eng.wait_ge(*dve.after("full", t + 1))
                    eng.wait_ge(*dve.after("mex", l, h))
                    eng.scalar_tensor_tensor(out=mdn[:, :], in0=bank(t + 1)[:, :], scalar=-1.0, in1=mex[:, :],
                                                  op0=ALU.mult, op1=ALU.max).then_inc(*dve.signals())
                    eng.wait_ge(*dve.previous)
                    eng.tensor_tensor(mdn[:, :], bank(t + 1)[:, :], mdn[:, :], ALU.max).then_inc(*dve.signals(("read", t + 1)))
                    eng.wait_ge(*dve.previous)
                    eng.reciprocal(mdn[:, :], mdn[:, :]).then_inc(*dve.signals())
                    eng.wait_ge(*dve.previous)
                    eng.wait_ge(*dve.after("full", t))
                    eng.tensor_tensor(mq[:, h, :], bank(t)[:, :], mdn[:, :], ALU.mult).then_inc(*dve.signals(("read", t), ("mh", l, h)))
                    eng.wait_ge(*dve.previous)
                    ahead(BLOCK["ak", l, h] + 7)
                    eng.wait_ge(*dve.after("rcin", l, h))
                    conv(4, lambda j: pcol("rglru_conv_w", l, 4 * j + h), pcol("rglru_conv_b", l, h),
                         cin[:, h % 2, :], xc[:, h, :], h, ("xc", l, h))
                    t = TILE["m3", l, h]
                    eng.wait_ge(*dve.after("full", t))
                    eng.scalar_tensor_tensor(out=mq[:, h, :], in0=bank(t)[:, :], scalar=-1.0 / P, in1=mq[:, h, :],
                                                  op0=ALU.mult, op1=ALU.add).then_inc(*dve.signals(("read", t), ("mhc", l, h)))
                    eng.wait_ge(*dve.previous)
                    rope(TILE["ak", l, h], aswap[:, :], atmp[:, :], ak[:, h, :], ("ak", l, h))
                    if h + 1 < M_HEADS:
                        m_masked(h + 1)
                    else:
                        ahead(BLOCK["rg", l, 0] + 7)
                    eng.wait_ge(*dve.after("mstd", l, h))
                    eng.scalar_tensor_tensor(out=mq[:, h, :], in0=mq[:, h, :], scalar=pcol("mlstm_norm", l, h),
                                                  in1=mdn[:, :], op0=ALU.mult, op1=ALU.mult).then_inc(*dve.signals())
                    eng.wait_ge(*dve.previous)
                    eng.wait_ge(*dve.after("mo", l, h))
                    eng.tensor_tensor(yf[:, h, :], mq[:, h, :], mo[:, :], ALU.mult).then_inc(*dve.signals(("yf", l, 0, h)))
                    eng.wait_ge(*dve.previous)
                    eng.wait_ge(*dve.after("yh", l, 0, h))
                    lo(al[:, h, :], yf[:, h, :], ah[:, h, :], ("y", l, 0, h), ("msplit", l, h))
                for c in range(NBR):
                    ahead(BLOCK["rg", l, c] + 7)
                    eng.wait_ge(*dve.after("rth", l, c))
                    eng.tensor_scalar(rt[:, 4, :], rt[:, 2, :], 1.0, None, ALU.add).then_inc(*dve.signals())
                    eng.wait_ge(*dve.previous)
                    eng.reciprocal(rt[:, 5, :], rt[:, 4, :]).then_inc(*dve.signals())
                    eng.wait_ge(*dve.previous)
                    eng.tensor_tensor(rt[:, 4, :], rt[:, 2, :], rt[:, 5, :], ALU.mult).then_inc(*dve.signals(("rq", l, c)))
                    eng.wait_ge(*dve.previous)
                    eng.wait_ge(*dve.after("ri", l, c))
                    eng.tensor_tensor(rt[:, 1, :], rt[:, 1, :], xc[:, c, :], ALU.mult).then_inc(*dve.signals())
                    eng.wait_ge(*dve.previous)
                    eng.wait_ge(*dve.after("rs", l, c))
                    eng.tensor_tensor(rt[:, 1, :], rt[:, 1, :], rt[:, 5, :], ALU.mult).then_inc(*dve.signals())
                    eng.wait_ge(*dve.previous)
                    eng.wait_ge(*dve.after("ra", l, c))
                    eng.tensor_tensor_scan(rt[:, 0, :], rt[:, 3, :], rt[:, 1, :], 0.0, ALU.mult, ALU.add).then_inc(*dve.signals())
                    eng.wait_ge(*dve.previous)
                    eng.wait_ge(*dve.after("rg", l, c))
                    eng.tensor_tensor(yf[:, c, :], rt[:, 0, :], rg[:, c, :], ALU.mult).then_inc(*dve.signals(("yf", l, 1, c), ("rgdone", l, c)))
                    eng.wait_ge(*dve.previous)
                    ahead(BLOCK["aq", l, c] + (7 if c < NBR - 1 else SLOT - 1))
                    rope(TILE["aq", l, c], rsw2[:, c % 2, :], cacc[:, c % 2, :], aq[:, c, :], ("aq", l, c))
                ahead(BLOCK["av", l] + 31 - SLOT)
                ahead(BLOCK["av", l] + 31)

                def branch(b, m):
                    t, blk = TILE["br", l, b, m], BLOCK["br", l, b, m]
                    ahead(blk + 7)
                    ahead(blk + 11)
                    eng.wait_ge(*dve.after("sig", l, b, m))
                    eng.wait_ge(*dve.after("full", t + 1))
                    if b == 0:
                        eng.tensor_tensor(mer[:, m, :], bank(t + 1)[:, :], sig[:, :], ALU.mult).then_inc(*dve.signals(("read", t + 1), ("merged", l, b, m)))
                        eng.wait_ge(*dve.previous)
                    else:
                        eng.tensor_tensor(cacc[:, 0, :], bank(t + 1)[:, :], sig[:, :], ALU.mult).then_inc(*dve.signals(("read", t + 1), ("merged", l, b, m)))
                        eng.wait_ge(*dve.previous)
                        eng.tensor_tensor(mer[:, m, :], mer[:, m, :], cacc[:, 0, :], ALU.add).then_inc(*dve.signals())
                        eng.wait_ge(*dve.previous)

                def split_y(b):
                    for k in range(4):
                        eng.wait_ge(*dve.after("yh", l, b, k))
                        lo(al[:, k, :], yf[:, k, :], ah[:, k, :], ("y", l, b, k))

                def masked(h, j):
                    t = score_tile(l, h, j)
                    eng.wait_ge(*dve.after("full", t))
                    if h:
                        eng.wait_ge(*dve.after("turned", l, h - 1, j))
                    m = mask_qk if j == 0 else work[:, j - 1, 0:P * (j + 1)]
                    eng.tensor_tensor_reduce(sm[:, j, 0:P * (j + 1)], bank(t)[:, 0:P * (j + 1)], m, -A_SCALE,
                                                      3.0e38, ALU.add, ALU.min, nmx[:, j:j + 1]).then_inc(*dve.signals(("read", t), ("sm", l, h, j)))
                    eng.wait_ge(*dve.previous)

                def normed(h, j):
                    eng.wait_ge(*dve.after("e", l, h, j))
                    eng.reciprocal(rinv[:, j:j + 1], rsum[:, j:j + 1]).then_inc(*dve.signals())
                    eng.wait_ge(*dve.previous)
                    eng.tensor_scalar(sm[:, j, 0:P * (j + 1)], sm[:, j, 0:P * (j + 1)], rinv[:, j:j + 1],
                                               None, ALU.mult).then_inc(*dve.signals(("p", l, h, j)))
                    eng.wait_ge(*dve.previous)

                for m in range(ND):
                    branch(0, m)
                    select(4)
                select(48)
                split_y(1)
                for j in range(NQ):
                    masked(0, j)
                for j in range(NQ):
                    normed(0, j)
                for h in range(A_HEADS):
                    branch(1, h)
                    if h + 1 < A_HEADS:
                        for j in range(NQ):
                            masked(h + 1, j)
                            if j:
                                normed(h + 1, j - 1)
                        normed(h + 1, NQ - 1)
                for m in range(ND):
                    ahead(BLOCK["gc", l] + 8 * m + 7)
                split_y(2)
                for m in range(ND):
                    ahead(BLOCK["bc", l] + 4 * m + 3)
                    t = TILE["bc", l] + m
                    eng.wait_ge(*dve.after("sigc", l, m))
                    eng.wait_ge(*dve.after("full", t))
                    eng.tensor_tensor(sigc[:, m, :], bank(t)[:, :], sigc[:, m, :], ALU.mult).then_inc(*dve.signals(("read", t)))
                    eng.wait_ge(*dve.previous)
                    eng.tensor_tensor(mer[:, m, :], mer[:, m, :], sigc[:, m, :], ALU.add).then_inc(*dve.signals(("merf", l, m)))
                    eng.wait_ge(*dve.previous)
                    if m:
                        eng.wait_ge(*dve.after("merh", l, m - 1))
                        lo(hl[:, m - 1, :], mer[:, m - 1, :], hh[:, m - 1, :], ("mer", l, m - 1))
                eng.wait_ge(*dve.after("merh", l, ND - 1))
                lo(hl[:, ND - 1, :], mer[:, ND - 1, :], hh[:, ND - 1, :], ("mer", l, ND - 1))
                for m in range(ND):
                    ahead(BLOCK["wo", l] + 8 * m + 7)
                    t = TILE["wo", l] + m
                    eng.wait_ge(*dve.after("full", t))
                    eng.tensor_tensor(x[:, m, :], x[:, m, :], bank(t)[:, :], ALU.add).then_inc(*dve.signals(("read", t), ("x", 2 * l + 1, m)))
                    eng.wait_ge(*dve.previous)
                    add_squares(2 * l + 1, m - 1)
                add_squares(2 * l + 1, ND - 1)
                norm(2 * l + 1)
                for half in range(2):
                    for p in range(NFF // 2):
                        t, b = TILE["up", l, half, p], BLOCK["up", l, half, p]
                        i = half * NFF // 2 + p
                        ahead(b + (15 if i == 0 else 7))
                        eng.wait_ge(*dve.after("fcin", l, i))
                        if i >= 2:
                            eng.wait_ge(*dve.after("fga", l, i - 2))
                        conv(3, lambda j: pcol("ffn_conv_w", l, NFF * j + i), pcol("ffn_conv_b", l, i),
                             cin[:, i % 2, :], cacc[:, i % 2, :], i, ("fconv", l, i))
                        ahead(b + 15)
                        if p:
                            eng.wait_ge(*dve.after("ffh", l, half, p - 1))
                            lo(al[:, p - 1, :], fhf[:, (i - 1) % 2, :], ah[:, p - 1, :], ("ff", l, half, p - 1))
                        eng.wait_ge(*dve.after("fga", l, i))
                        eng.wait_ge(*dve.after("full", t + 1))
                        eng.tensor_tensor(fhf[:, i % 2, :], fga[:, i % 2, :], bank(t + 1)[:, :], ALU.mult).then_inc(*dve.signals(("read", t + 1), ("fhf", l, i)))
                        eng.wait_ge(*dve.previous)
                    p = NFF // 2
                    i = half * NFF // 2 + p
                    eng.wait_ge(*dve.after("ffh", l, half, p - 1))
                    lo(al[:, p - 1, :], fhf[:, (i - 1) % 2, :], ah[:, p - 1, :], ("ff", l, half, p - 1))
                    for m in range(ND):
                        ahead(BLOCK["down", l, half] + 12 * m + 11)
                        if l == DEPTH - 1 and half and m == 4:
                            mem_split(0)
                        t = TILE["down", l, half] + m
                        eng.wait_ge(*dve.after("full", t))
                        eng.tensor_tensor(x[:, m, :], x[:, m, :], bank(t)[:, :], ALU.add).then_inc(*dve.signals(("read", t), ("x" if half else "xhalf", 2 * l + 2, m)))
                        eng.wait_ge(*dve.previous)
                        if half:
                            add_squares(2 * l + 2, m - 1)

            def refine(t, r, tmp, n):
                eng.scalar_tensor_tensor(out=tmp, in0=bank(t)[:, :], scalar=EPS * n, in1=r, op0=ALU.add,
                                         op1=ALU.mult).then_inc(*dve.signals(("read", t)))
                eng.wait_ge(*dve.previous)
                eng.scalar_tensor_tensor(out=tmp, in0=tmp, scalar=-0.5 / n, in1=r, op0=ALU.mult,
                                         op1=ALU.mult).then_inc(*dve.signals())
                eng.wait_ge(*dve.previous)
                eng.scalar_tensor_tensor(out=r, in0=tmp, scalar=1.5, in1=r, op0=ALU.add,
                                         op1=ALU.mult).then_inc(*dve.signals())
                eng.wait_ge(*dve.previous)

            def n_ref(key):
                return key[0] in ("kpe", "kg")

            def job(i, t, key, buf, n, gain, turns):
                r = jst[:, i % 2, :]
                eng.wait_ge(*dve.after("jstd", *key))
                if n_ref(key):
                    refine(t, r, sqbuf[i], n)
                eng.scalar_tensor_tensor(out=buf, in0=buf, scalar=gain, in1=r, op0=ALU.mult,
                                         op1=ALU.mult).then_inc(*dve.signals(("jn",) + key, *([] if turns else [("jend",) + key, key])))
                eng.wait_ge(*dve.previous)

            def job_turn(i, key, buf):
                r = jst[:, i % 2, :]
                eng.wait_ge(*dve.after("jswap", *key))
                eng.tensor_tensor(r, swap2, tabs[:, :], ALU.mult).then_inc(*dve.signals())
                eng.wait_ge(*dve.previous)
                eng.tensor_tensor(buf, buf, tabc[:, :], ALU.mult).then_inc(*dve.signals())
                eng.wait_ge(*dve.previous)
                eng.tensor_tensor(buf, buf, r, ALU.add).then_inc(*dve.signals(("jend",) + key, key))
                eng.wait_ge(*dve.previous)

            for l in range(DEPTH):
                n1 = N_SECOND + 2 * l
                g = lambda name, i=0: par[:, PCOL2[name] + i:PCOL2[name] + i + 1]
                add_squares(N_FINAL if l == 0 else n1, ND - 1)
                for m in range(MEM_HEADS):
                    ahead(BLOCK["memk", l] + 8 * m + 7)
                ahead(BLOCK["memv", l] + SLOT - 1)
                if l == 0:
                    norm(N_FINAL)
                    add_squares(N_SECOND, ND - 1)
                    ahead(BLOCK["memv", l] + 31)
                norm(n1)
                ahead(BLOCK["memv", l] + 31)
                for i in range(2):
                    eng.wait_ge(*dve.after("kst", l, i))
                    refine(TILE["memkst", l] + i, kst[:, i, :], ksq[:, i, :], P)
                    eng.scalar_tensor_tensor(out=kmem[:, 2 * i:2 * i + 2, :].rearrange("p a b -> p (a b)"),
                                                  in0=kraw[:, i, :], scalar=g("memk", l), in1=kst[:, i, :],
                                                  op0=ALU.mult, op1=ALU.mult).then_inc(*dve.signals(*([("kmem", l)] if i else [])))
                    eng.wait_ge(*dve.previous)
                if l == 0:
                    ahead(BLOCK["cq", l] + ND * NQR - 1 - SLOT)
                    for c in range(NQR, NQR + NKV + 1):
                        ahead(BLOCK["cq", l] + ND * c - 1)
                    ahead(BLOCK["kpe", l] + ND - 1)
                    for i in range(2):
                        eng.wait_ge(*dve.after("cstd", l, i))
                        refine(TILE[("cqst", "ckvst")[i], l], cqi[:, i, :], cqs[:, i, :], (QR, KVR)[i])
                    for c in range(NQR + NKV):
                        eng.scalar_tensor_tensor(out=cqr[:, c, :], in0=cqr[:, c, :],
                                                 scalar=g("q_a", c) if c < NQR else g("kv_a", c - NQR),
                                                 in1=cqi[:, int(c >= NQR), :], op0=ALU.mult,
                                                 op1=ALU.mult).then_inc(*dve.signals(("clat", l, c)))
                        eng.wait_ge(*dve.previous)
                    ahead(BLOCK["qmem", l] + ND - 1)
                    job(0, TILE["kst", l], ("kpe", l), kpe[:, :], ROPE, g("mla_kpe"), True)
                    ahead(BLOCK["qmem", l] + 2 * ND - 1)
                    job_turn(0, ("kpe", l), kpe[:, :])
                else:
                    ahead(BLOCK["kg", l] + ND * GKV - 1)
                    ahead(BLOCK["qmem", l] + ND - 1)
                    for m in range(GKV):
                        job(m, TILE["kst", l] + m, ("kg", l, m), kg[:, m, :], P, g("gqa_k"), True)
                        job_turn(m, ("kg", l, m), kg[:, m, :])
                        ahead(BLOCK["qmem", l] + (m + 2) * ND - 1)
                for m in range(2, MEM_HEADS):
                    ahead(BLOCK["qmem", l] + (m + 1) * ND - 1)

                def latent_low(c):
                    eng.wait_ge(*dve.after("lath", l, c))
                    lo(hl[:, c, :], cqr[:, c, :], hh[:, c, :], ("lat", l, c))

                if l == 0:
                    for c in range(NQR, NQR + NKV):
                        latent_low(c)

                def prep_a(u):
                    if u >= MEM_HEADS:
                        b = BLOCK["pa", l, u]
                        for kind, n in prep_tiles(l, u):
                            b += n
                            ahead(b - 1)

                def prep_norm(u, part):
                    for i, (key, buf, one, n, gain, turns) in enumerate(jobs(l, u)):
                        if i // 2 == part:
                            job(place(u, i), TILE["pb", l, u] + i, key, buf, n, gain, turns)

                def prep_turn(u):
                    for i, (key, buf, one, n, gain, turns) in enumerate(jobs(l, u)):
                        if turns:
                            job_turn(place(u, i), key, buf)

                for u in range(2):
                    prep_norm(u, 0)
                if l == 0:
                    for c in range(NQR):
                        latent_low(c)
                    ahead(BLOCK["v2", l, 0] + 7)
                    ahead(BLOCK["v2", l, 1] + 7)
                else:
                    ahead(BLOCK["v2", l, 0] + 15)

                def peak(u, j):
                    n = MEM if u < MEM_HEADS else S
                    t = score_tile2(l, u, j)
                    eng.wait_ge(*dve.after("full", t))
                    if u:
                        eng.wait_ge(*dve.after("turned2", l, u - 1, j))
                    eng.tensor_reduce(nmx[:, j:j + 1], bank(t)[:, 0:n], AX, ALU.max, negate=True).then_inc(*dve.signals(("nmx2", l, u, j)))
                    eng.wait_ge(*dve.previous)

                def normed2(u, j):
                    n = MEM if u < MEM_HEADS else S
                    eng.wait_ge(*dve.after("e2", l, u, j))
                    eng.reciprocal(rinv[:, j:j + 1], rsum[:, j:j + 1]).then_inc(*dve.signals())
                    eng.wait_ge(*dve.previous)
                    eng.tensor_scalar(sm2[:, j, 0:n], sm2[:, j, 0:n], rinv[:, j:j + 1], None,
                                      ALU.mult).then_inc(*dve.signals(("p2", l, u, j)))
                    eng.wait_ge(*dve.previous)

                for j in range(NQ):
                    peak(0, j)
                for j in range(NQ):
                    normed2(0, j)
                for u in range(HEADS2):
                    if u + 2 < HEADS2:
                        prep_a(u + 2)
                    for j in range(NQ):
                        if u + 1 < HEADS2:
                            peak(u + 1, j)
                            if j:
                                normed2(u + 1, j - 1)
                        if 0 < j < 3 and u + 2 < HEADS2:
                            prep_norm(u + 2, j - 1)
                    t = out_tile2(l, u)
                    c = (u - MEM_HEADS) % HEADS2
                    eng.wait_ge(*dve.after("mixh", l, u))
                    eng.tensor_tensor(al[:, c, :], bank(t)[:, :], ah[:, c, :].bitcast(F32), ALU.subtract).then_inc(*dve.signals(("read", t), ("mix", l, u)))
                    eng.wait_ge(*dve.previous)
                    if u + 1 < HEADS2:
                        normed2(u + 1, NQ - 1)
                    if u + 2 < HEADS2:
                        prep_turn(u + 2)
                for m in range(ND):
                    ahead(BLOCK["wo2", l] + MIX * m + MIX - 1)
                    t = TILE["wo2", l] + m
                    eng.wait_ge(*dve.after("full", t))
                    eng.tensor_tensor(x[:, m, :], x[:, m, :], bank(t)[:, :], ALU.add).then_inc(*dve.signals(("read", t), ("x", n1 + 1, m)))
                    eng.wait_ge(*dve.previous)
                    add_squares(n1 + 1, m - 1)
                add_squares(n1 + 1, ND - 1)
                norm(n1 + 1)
                for half in range(2):
                    for p in range(NFF2 // 2):
                        t, b = TILE["up2", l, half, p], BLOCK["up2", l, half, p]
                        i = half * NFF2 // 2 + p
                        ahead(b + 7)
                        ahead(b + 15)
                        if p:
                            eng.wait_ge(*dve.after("ffh2", l, half, p - 1))
                            lo(al[:, p - 1, :], fhf2[:, (i - 1) % 2, :], ah[:, p - 1, :], ("ff2", l, half, p - 1))
                        eng.wait_ge(*dve.after("fga2", l, i))
                        eng.wait_ge(*dve.after("full", t + 1))
                        eng.tensor_tensor(fhf2[:, i % 2, :], fga2[:, i % 2, :], bank(t + 1)[:, :], ALU.mult).then_inc(*dve.signals(("read", t + 1), ("fhf2", l, i)))
                        eng.wait_ge(*dve.previous)
                    p = NFF2 // 2
                    i = half * NFF2 // 2 + p
                    eng.wait_ge(*dve.after("ffh2", l, half, p - 1))
                    lo(al[:, p - 1, :], fhf2[:, (i - 1) % 2, :], ah[:, p - 1, :], ("ff2", l, half, p - 1))
                    for m in range(ND):
                        ahead(BLOCK["down2", l, half] + 11 * m + 10)
                        if l == 0 and half and m == 4:
                            mem_split(1)
                        t = TILE["down2", l, half] + m
                        eng.wait_ge(*dve.after("full", t))
                        names = [("read", t)]
                        if half:
                            names.append(("out", m) if l else ("x", N_SECOND + 2, m))
                        eng.tensor_tensor(x[:, m, :], x[:, m, :], bank(t)[:, :], ALU.add).then_inc(*dve.signals(*names))
                        eng.wait_ge(*dve.previous)
                        if half and l == 0:
                            add_squares(n1 + 2, m - 1)

    return marks


def kernel(**inputs):
    import concourse.bacc as bacc
    from concourse.bass_utils import run_bass_kernel_spmd

    w = {name: np.asarray(a) for name, a in inputs.items()}
    arrays = {
        "x": np.ascontiguousarray(w["x"][0].T.reshape(ND, P, S).transpose(1, 0, 2)),
        "mem": np.ascontiguousarray(w["mem_2"][0].T.reshape(ND, P, MEM).transpose(1, 0, 2)),
        "pos": np.ascontiguousarray(w["positions"].astype(np.int32)),
        "w": pack_weights(w), "par": pack_params(w), "rgw": pack_rglru(w), "con": constants(), "tab": axial_tables(),
    }
    known = None
    for _ in range(2):
        nc = bacc.Bacc("TRN2", target_bir_lowering=False, num_devices=1, dynamic_dma_scratch_size=1024)
        args = {n: nc.dram_tensor(f"in_{n}", a.shape, mybir.dt.from_np(a.dtype), kind="ExternalInput").ap()
                for n, a in arrays.items()}
        args["out"] = nc.dram_tensor("out", (P, ND, S), F32, kind="ExternalOutput").ap()
        known = build(nc, args, known)
    r = run_bass_kernel_spmd(nc, [{f"in_{n}": a for n, a in arrays.items()}], core_ids=[0])
    out = r.results[0]["out"]
    return np.ascontiguousarray(out.transpose(1, 0, 2).reshape(D, S).T)[None]
```
